# Optimizing a Trainium2 kernel written in Bass

```python
import math
import jax
import jax.numpy as jnp
from jax import lax
import numpy as np

D_MODEL = 1024
BATCH = 1
SEQ = 256
DEPTH = 2

F32 = jnp.float32
GRID_W = 64
CTX_LEN = 256
N_MOD = 6
NORM_EPS = 1e-6
ROPE_BASE = 10000.0
CONV_W = 4

LRU_WIDTH = 512
LRU_BLOCKS = 8
LRU_BLOCK = LRU_WIDTH // LRU_BLOCKS
LRU_C = 8.0

HEAD_DIM = 64
WIN_HEADS = 8
WIN_KV_HEADS = 2
WINDOW = 128
WBLK = 128

DIFF_HEADS = 4
DIFF_DH = 64
QBLK = 128

SSD_HEADS = 8
SSD_HEAD_DIM = 64
SSD_INNER = SSD_HEADS * SSD_HEAD_DIM
SSD_GROUPS = 2
SSD_STATE = 128
SSD_CHUNK = 128
SSD_CONV_DIM = SSD_INNER + 2 * SSD_GROUPS * SSD_STATE

N_EXPERTS = 64
N_EXPERT_GROUPS = 8
TOPK_GROUPS = 4
TOP_K = 8
D_EXPERT = 256
D_SHARED = 256
ROUTED_SCALE = 2.5
EXPERT_BLK = 256

N_EVEN = (DEPTH + 1) // 2
N_ODD = DEPTH // 2

AB_Q = WIN_HEADS * HEAD_DIM
AB_KV = WIN_KV_HEADS * HEAD_DIM
AB_CTX_START = LRU_WIDTH + AB_Q
AB_IN = AB_CTX_START + LRU_WIDTH + 2 * AB_KV
AB_SPLITS = (LRU_WIDTH, AB_CTX_START, AB_CTX_START + LRU_WIDTH, AB_CTX_START + LRU_WIDTH + AB_KV)
AB_CTX_SPLITS = (LRU_WIDTH, LRU_WIDTH + AB_KV)
AB_OUT = LRU_WIDTH + AB_Q

CD_QK = DIFF_HEADS * 2 * DIFF_DH
CD_V = DIFF_HEADS * 2 * DIFF_DH
CD_CTX_START = CD_QK + SSD_INNER
CD_IN = CD_CTX_START + CD_QK + CD_V + SSD_CONV_DIM + 2 * SSD_HEADS
CD_SPLITS = (CD_QK, CD_CTX_START, CD_CTX_START + CD_QK, CD_CTX_START + CD_QK + CD_V,
             CD_CTX_START + CD_QK + CD_V + SSD_CONV_DIM)
CD_CTX_SPLITS = (CD_QK, CD_QK + CD_V, CD_QK + CD_V + SSD_CONV_DIM)
CD_OUT = CD_V + SSD_INNER

kernel_name = 'hybrid_diffusion_rglru_swa_diffattn_ssd_moe'

def rms_norm(x, g):
    x32 = x.astype(F32)
    y = x32 * lax.rsqrt(jnp.mean(x32 * x32, axis=-1, keepdims=True) + NORM_EPS)
    return (y * g.astype(F32)).astype(x.dtype)

def modulate(h, shift, scale):
    return h * (1.0 + scale) + shift

def axial_rope_tables(n_tok, dim, dtype):
    rows = n_tok // GRID_W
    row = jnp.repeat(jnp.arange(rows), GRID_W).astype(F32)
    col = jnp.tile(jnp.arange(GRID_W), rows).astype(F32)
    n = dim // 4
    inv = ROPE_BASE ** (-jnp.arange(n, dtype=F32) / n)
    ang = jnp.concatenate([row[:, None] * inv, col[:, None] * inv], axis=-1)
    return jnp.cos(ang).astype(dtype), jnp.sin(ang).astype(dtype)

def apply_rope(x, cos, sin):
    half = x.shape[-1] // 2
    x1, x2 = x[..., :half], x[..., half:]
    c, s = cos[:, None, :], sin[:, None, :]
    return jnp.concatenate([x1 * c - x2 * s, x1 * s + x2 * c], axis=-1)

def dwconv_centred(u, w, b):
    ch = u.shape[-1]
    y = lax.conv_general_dilated(u, w[:, None, :].astype(u.dtype), window_strides=(1,),
                                 padding=[((CONV_W - 1) // 2, CONV_W // 2)],
                                 dimension_numbers=('NWC', 'WIO', 'NWC'), feature_group_count=ch)
    return y + b

def linear_scan(a, b, h0, reverse):
    def combine(left, right):
        a1, b1 = left
        a2, b2 = right
        return a1 * a2, a2 * b1 + b2
    a_cum, h = lax.associative_scan(combine, (a, b), axis=1, reverse=reverse)
    h = h + a_cum * h0[:, None, :]
    h_final = h[:, 0] if reverse else h[:, -1]
    return h, h_final

def rglru_coeffs(u, w_r, b_r, w_i, b_i, lam):
    bsz, n_tok, _ = u.shape
    ub = u.reshape(bsz, n_tok, LRU_BLOCKS, LRU_BLOCK)
    r = jax.nn.sigmoid(jnp.einsum('blnc,ncd->blnd', ub, w_r).reshape(bsz, n_tok, LRU_WIDTH).astype(F32)
                       + b_r.astype(F32))
    i = jax.nn.sigmoid(jnp.einsum('blnc,ncd->blnd', ub, w_i).reshape(bsz, n_tok, LRU_WIDTH).astype(F32)
                       + b_i.astype(F32))
    log_a = -LRU_C * r * jax.nn.softplus(-lam.astype(F32))
    a = jnp.exp(log_a)
    bx = jnp.sqrt(-jnp.expm1(2.0 * log_a)) * i * u.astype(F32)
    return a, bx

def window_attention(q, k, v, k_ctx, v_ctx, sink):
    bsz, s_len, kv, grp, hd = q.shape
    c_len = k_ctx.shape[1]
    nb = s_len // WBLK
    qb = q.reshape(bsz, nb, WBLK, kv, grp, hd)

    def band(t):
        tp = jnp.pad(t, ((0, 0), (WBLK, WBLK), (0, 0), (0, 0))).reshape(bsz, nb + 2, WBLK, kv, hd)
        return jnp.concatenate([tp[:, :-2], tp[:, 1:-1], tp[:, 2:]], axis=2)

    kb, vb = band(k), band(v)
    scale = hd ** -0.5
    s_band = jnp.einsum('bnqhgd,bnkhd->bnhgqk', qb, kb).astype(F32) * scale
    qpos = jnp.arange(nb)[:, None, None] * WBLK + jnp.arange(WBLK)[None, :, None]
    kpos = jnp.arange(nb)[:, None, None] * WBLK - WBLK + jnp.arange(3 * WBLK)[None, None, :]
    valid = (jnp.abs(qpos - kpos) <= WINDOW) & (kpos >= 0) & (kpos < s_len)
    s_band = jnp.where(valid[None, :, None, None], s_band, -jnp.inf)
    s_ctx = jnp.einsum('bnqhgd,bkhd->bnhgqk', qb, k_ctx).astype(F32) * scale
    s_sink = jnp.broadcast_to(sink.astype(F32)[None, None, :, :, None, None], s_ctx.shape[:-1] + (1,))
    p = jax.nn.softmax(jnp.concatenate([s_sink, s_ctx, s_band], axis=-1), axis=-1).astype(v.dtype)
    o = (jnp.einsum('bnhgqk,bkhd->bnqhgd', p[..., 1:1 + c_len], v_ctx)
         + jnp.einsum('bnhgqk,bnkhd->bnqhgd', p[..., 1 + c_len:], vb))
    return o.reshape(bsz, s_len, kv * grp * hd)

def context_sink_attention(q, k, v, sink):
    bsz, c_len, kv, grp, hd = q.shape
    s = jnp.einsum('bqhgd,bkhd->bhgqk', q, k).astype(F32) * hd ** -0.5
    s_sink = jnp.broadcast_to(sink.astype(F32)[None, :, :, None, None], s.shape[:-1] + (1,))
    p = jax.nn.softmax(jnp.concatenate([s_sink, s], axis=-1), axis=-1)[..., 1:].astype(v.dtype)
    return jnp.einsum('bhgqk,bkhd->bqhgd', p, v).reshape(bsz, c_len, kv * grp * hd)

def diff_attention(q, k, v, lam, lam_init, subln_g):
    s = jnp.einsum('bqhmd,bkhmd->bhmqk', q, k).astype(F32) * DIFF_DH ** -0.5
    p = jax.nn.softmax(s, axis=-1)
    w = (p[:, :, 0] - lam * p[:, :, 1]).astype(v.dtype)
    o = jnp.einsum('bhqk,bkhe->bqhe', w, v)
    return rms_norm(o, subln_g) * (1.0 - lam_init)

def ssd_inputs(xbc, conv_w, conv_b):
    bsz, n_tok, _ = xbc.shape
    u = jax.nn.silu(dwconv_centred(xbc, conv_w, conv_b)).astype(F32)
    xs, bm, cm = jnp.split(u, (SSD_INNER, SSD_INNER + SSD_GROUPS * SSD_STATE), axis=-1)
    return (xs.reshape(bsz, n_tok, SSD_HEADS, SSD_HEAD_DIM),
            bm.reshape(bsz, n_tok, SSD_GROUPS, SSD_STATE),
            cm.reshape(bsz, n_tok, SSD_GROUPS, SSD_STATE))

def ssd_chunked(x, dt, a, bm, cm, h0, with_output):
    bsz, n_tok, n_h, n_p = x.shape
    n_g, n_n = bm.shape[2], bm.shape[3]
    n_r = n_h // n_g
    nc = n_tok // SSD_CHUNK
    q = SSD_CHUNK
    xc = x.reshape(bsz, nc, q, n_g, n_r, n_p)
    dtc = dt.reshape(bsz, nc, q, n_g, n_r)
    bc = bm.reshape(bsz, nc, q, n_g, n_n)
    acum = jnp.cumsum(dtc * a.reshape(n_g, n_r), axis=2)
    to_end = jnp.exp(acum[:, :, -1:] - acum) * dtc
    states = jnp.einsum('bclgn,bclgrp->bcgrpn', bc, xc * to_end[..., None])
    chunk_decay = jnp.exp(acum[:, :, -1])

    def step(h, inp):
        s_c, dcy = inp
        return dcy[..., None, None] * h + s_c, h

    h_fin, h_in = lax.scan(step, h0.reshape(bsz, n_g, n_r, n_p, n_n),
                           (jnp.moveaxis(states, 1, 0), jnp.moveaxis(chunk_decay, 1, 0)))
    h_fin = h_fin.reshape(bsz, n_h, n_p, n_n)
    if not with_output:
        return None, h_fin
    h_in = jnp.moveaxis(h_in, 0, 1)
    cc = cm.reshape(bsz, nc, q, n_g, n_n)
    seg = acum[:, :, :, None] - acum[:, :, None, :]
    lower = jnp.tril(jnp.ones((q, q), bool))[:, :, None, None]
    decay = jnp.exp(jnp.where(lower, seg, -jnp.inf))
    cb = jnp.einsum('bclgn,bcsgn->bclsg', cc, bc)
    w = cb[..., None] * decay * dtc[:, :, None]
    y = jnp.einsum('bclsgr,bcsgrp->bclgrp', w, xc)
    y = y + jnp.einsum('bclgn,bcgrpn->bclgrp', cc, h_in) * jnp.exp(acum)[..., None]
    return y.reshape(bsz, n_tok, n_h, n_p), h_fin

def ssd_dir(x, dt, a, bm, cm, h0, reverse, with_output):
    if reverse:
        x, dt, bm, cm = (jnp.flip(t, axis=1) for t in (x, dt, bm, cm))
    y, h_fin = ssd_chunked(x, dt, a, bm, cm, h0, with_output)
    if reverse and with_output:
        y = jnp.flip(y, axis=1)
    return y, h_fin

def gated_group_norm(y, z, g):
    bsz, n_tok = y.shape[:2]
    gs = SSD_INNER // SSD_GROUPS
    yz = y.reshape(bsz, n_tok, SSD_GROUPS, gs) * jax.nn.silu(z.astype(F32)).reshape(bsz, n_tok, SSD_GROUPS, gs)
    return rms_norm(yz, g.reshape(SSD_GROUPS, gs)).reshape(bsz, n_tok, SSD_INNER).astype(z.dtype)

def mixer_rglru_window(hl, hc, w_in, w_out, conv_w, conv_b, w_r, b_r, w_i, b_i, lam, sink, ctx_out):
    bsz, s_len, _ = hl.shape
    c_len = hc.shape[1]
    grp = WIN_HEADS // WIN_KV_HEADS
    gate_l, q_l, xa_l, k_l, v_l = jnp.split(hl @ w_in, AB_SPLITS, axis=-1)
    if ctx_out:
        gate_c, q_c, xa_c, k_c, v_c = jnp.split(hc @ w_in, AB_SPLITS, axis=-1)
    else:
        xa_c, k_c, v_c = jnp.split(hc @ w_in[:, AB_CTX_START:], AB_CTX_SPLITS, axis=-1)
    u_l = dwconv_centred(xa_l, conv_w, conv_b)
    u_c = dwconv_centred(xa_c, conv_w, conv_b)
    rec_l = jnp.zeros(u_l.shape, F32)
    rec_c = jnp.zeros(u_c.shape, F32)
    for d, rev in enumerate((False, True)):
        a_c, bx_c = rglru_coeffs(u_c, w_r[d], b_r[d], w_i[d], b_i[d], lam[d])
        h_c, h_c_final = linear_scan(a_c, bx_c, jnp.zeros((bsz, LRU_WIDTH), F32), rev)
        a_l, bx_l = rglru_coeffs(u_l, w_r[d], b_r[d], w_i[d], b_i[d], lam[d])
        h_l, _ = linear_scan(a_l, bx_l, h_c_final, rev)
        rec_l = rec_l + h_l
        if ctx_out:
            rec_c = rec_c + h_c
    cos, sin = axial_rope_tables(s_len, HEAD_DIM, hl.dtype)
    q_l = apply_rope(q_l.reshape(bsz, s_len, WIN_HEADS, HEAD_DIM), cos, sin).reshape(
        bsz, s_len, WIN_KV_HEADS, grp, HEAD_DIM)
    k_l = apply_rope(k_l.reshape(bsz, s_len, WIN_KV_HEADS, HEAD_DIM), cos, sin)
    v_l = v_l.reshape(bsz, s_len, WIN_KV_HEADS, HEAD_DIM)
    k_c = k_c.reshape(bsz, c_len, WIN_KV_HEADS, HEAD_DIM)
    v_c = v_c.reshape(bsz, c_len, WIN_KV_HEADS, HEAD_DIM)
    sink = sink.reshape(WIN_KV_HEADS, grp)
    att_l = window_attention(q_l, k_l, v_l, k_c, v_c, sink)
    lru_l = rec_l.astype(hl.dtype) * jax.nn.gelu(gate_l)
    out_l = jnp.concatenate([lru_l, att_l], axis=-1) @ w_out
    if not ctx_out:
        return out_l, None
    att_c = context_sink_attention(q_c.reshape(bsz, c_len, WIN_KV_HEADS, grp, HEAD_DIM), k_c, v_c, sink)
    lru_c = rec_c.astype(hc.dtype) * jax.nn.gelu(gate_c)
    out_c = jnp.concatenate([lru_c, att_c], axis=-1) @ w_out
    return out_l, out_c

def mixer_diff_ssd(hl, hc, w_in, w_out, lam_vecs, subln_g, conv_w, conv_b, dt_bias, a_log, d_skip,
                   norm_g, lam_init, ctx_out):
    bsz, s_len, _ = hl.shape
    c_len = hc.shape[1]
    q_l, z_l, k_l, v_l, xbc_l, dt_l = jnp.split(hl @ w_in, CD_SPLITS, axis=-1)
    if ctx_out:
        q_c, z_c, k_c, v_c, xbc_c, dt_c = jnp.split(hc @ w_in, CD_SPLITS, axis=-1)
    else:
        k_c, v_c, xbc_c, dt_c = jnp.split(hc @ w_in[:, CD_CTX_START:], CD_CTX_SPLITS, axis=-1)
    lv = lam_vecs.astype(F32)
    lam = jnp.exp(jnp.sum(lv[0] * lv[1])) - jnp.exp(jnp.sum(lv[2] * lv[3])) + lam_init
    cos, sin = axial_rope_tables(s_len, DIFF_DH, hl.dtype)

    def rope_qk(t):
        t = t.reshape(bsz, s_len, 2 * DIFF_HEADS, DIFF_DH)
        return apply_rope(t, cos, sin).reshape(bsz, s_len, DIFF_HEADS, 2, DIFF_DH)

    q_l, k_l = rope_qk(q_l), rope_qk(k_l)
    k_c = k_c.reshape(bsz, c_len, DIFF_HEADS, 2, DIFF_DH)
    v_c = v_c.reshape(bsz, c_len, DIFF_HEADS, 2 * DIFF_DH)
    k_all = jnp.concatenate([k_c, k_l], axis=1)
    v_all = jnp.concatenate([v_c, v_l.reshape(bsz, s_len, DIFF_HEADS, 2 * DIFF_DH)], axis=1)
    nb = s_len // QBLK
    q_blocks = jnp.moveaxis(q_l.reshape(bsz, nb, QBLK, DIFF_HEADS, 2, DIFF_DH), 1, 0)
    o_blocks = lax.map(lambda qb: diff_attention(qb, k_all, v_all, lam, lam_init, subln_g), q_blocks)
    diff_l = jnp.moveaxis(o_blocks, 0, 1).reshape(bsz, s_len, CD_V)
    x_l, bm_l, cm_l = ssd_inputs(xbc_l, conv_w, conv_b)
    x_c, bm_c, cm_c = ssd_inputs(xbc_c, conv_w, conv_b)
    dsk = d_skip.astype(F32)[:, None]
    y_l = dsk * x_l
    y_c = dsk * x_c if ctx_out else None
    h_zero = jnp.zeros((bsz, SSD_HEADS, SSD_HEAD_DIM, SSD_STATE), F32)
    for d, rev in enumerate((False, True)):
        a_d = -jnp.exp(a_log[d].astype(F32))
        cols = slice(d * SSD_HEADS, (d + 1) * SSD_HEADS)
        dt_c_d = jax.nn.softplus(dt_c[..., cols].astype(F32) + dt_bias[d].astype(F32))
        dt_l_d = jax.nn.softplus(dt_l[..., cols].astype(F32) + dt_bias[d].astype(F32))
        yc_d, h_c_final = ssd_dir(x_c, dt_c_d, a_d, bm_c, cm_c, h_zero, rev, ctx_out)
        yl_d, _ = ssd_dir(x_l, dt_l_d, a_d, bm_l, cm_l, h_c_final, rev, True)
        y_l = y_l + yl_d
        if ctx_out:
            y_c = y_c + yc_d
    ssd_l = gated_group_norm(y_l, z_l, norm_g)
    out_l = jnp.concatenate([diff_l, ssd_l], axis=-1) @ w_out
    if not ctx_out:
        return out_l, None
    diff_c = diff_attention(q_c.reshape(bsz, c_len, DIFF_HEADS, 2, DIFF_DH), k_c, v_c, lam, lam_init,
                            subln_g).reshape(bsz, c_len, CD_V)
    ssd_c = gated_group_norm(y_c, z_c, norm_g)
    out_c = jnp.concatenate([diff_c, ssd_c], axis=-1) @ w_out
    return out_l, out_c

def moe_ffn(h, w_router, b_router, w_gate, w_up, w_down, ws_gate, ws_up, ws_down):
    n_tok = h.shape[0]
    per = N_EXPERTS // N_EXPERT_GROUPS
    scores = jax.nn.sigmoid((h @ w_router).astype(F32))
    sel = scores + b_router.astype(F32)
    grp_score = jnp.sum(lax.top_k(sel.reshape(n_tok, N_EXPERT_GROUPS, per), 2)[0], axis=-1)
    _, top_grp = lax.top_k(grp_score, TOPK_GROUPS)
    grp_mask = jnp.any(top_grp[..., None] == jnp.arange(N_EXPERT_GROUPS), axis=1)
    sel = jnp.where(jnp.repeat(grp_mask, per, axis=1), sel, -jnp.inf)
    _, idx = lax.top_k(sel, TOP_K)
    gate = jnp.take_along_axis(scores, idx, axis=1)
    gate = gate / jnp.sum(gate, axis=-1, keepdims=True) * ROUTED_SCALE
    n_slots = n_tok * TOP_K
    e_flat = idx.reshape(-1)
    order = jnp.argsort(e_flat)
    e_sorted = e_flat[order]
    tok_sorted = (order // TOP_K).astype(jnp.int32)
    w_sorted = gate.reshape(-1)[order]
    counts = jnp.bincount(e_flat, length=N_EXPERTS)
    padded = (counts + EXPERT_BLK - 1) // EXPERT_BLK * EXPERT_BLK
    start = jnp.cumsum(counts) - counts
    pend = jnp.cumsum(padded)
    pstart = pend - padded
    dest = pstart[e_sorted] + jnp.arange(n_slots) - start[e_sorted]
    n_blocks = -(-n_slots // EXPERT_BLK) + N_EXPERTS
    cap = n_blocks * EXPERT_BLK
    buf_tok = jnp.zeros((cap,), jnp.int32).at[dest].set(tok_sorted)
    buf_w = jnp.zeros((cap,), F32).at[dest].set(w_sorted)
    blk_e = jnp.minimum(jnp.searchsorted(pend, jnp.arange(n_blocks) * EXPERT_BLK, side='right'), N_EXPERTS - 1)

    def body(acc, blk):
        e, tok, w = blk
        xb = h[tok]
        y = (jax.nn.silu(xb @ w_gate[e]) * (xb @ w_up[e])) @ w_down[e]
        return acc.at[tok].add(y * w[:, None].astype(y.dtype)), None

    routed, _ = lax.scan(body, jnp.zeros_like(h),
                         (blk_e, buf_tok.reshape(n_blocks, EXPERT_BLK), buf_w.reshape(n_blocks, EXPERT_BLK)))
    shared = (jax.nn.silu(h @ ws_gate) * (h @ ws_up)) @ ws_down
    return shared + routed

def setup_inputs(seed: int = 0) -> dict:
    key = jax.random.key(seed)
    keys = iter(jax.random.split(key, 64))

    def nrm(shape, scale):
        return jax.random.normal(next(keys), shape, F32) * scale

    def unif(shape, lo, hi):
        return jax.random.uniform(next(keys), shape, F32, lo, hi)

    dm = D_MODEL
    a0 = unif((N_EVEN, 2, LRU_WIDTH), 0.9, 0.999) ** (1.0 / LRU_C)
    dt0 = jnp.exp(unif((N_ODD, 2, SSD_HEADS), math.log(1e-3), math.log(1e-1)))
    return {
        'x': nrm((BATCH, SEQ, dm), 1.0),
        'c': nrm((BATCH, dm), 1.0),
        'ctx': nrm((BATCH, CTX_LEN, dm), 1.0),
        'c_ctx': nrm((dm,), 1.0),
        'w_mod': nrm((DEPTH, dm, N_MOD * dm), 0.5 * dm ** -0.5),
        'b_mod': nrm((DEPTH, N_MOD * dm), 0.02),
        'g_mix': 1.0 + nrm((DEPTH, dm), 0.02),
        'g_ffn': 1.0 + nrm((DEPTH, dm), 0.02),
        'g_final': 1.0 + nrm((dm,), 0.02),
        'ab_w_in': nrm((N_EVEN, dm, AB_IN), dm ** -0.5),
        'ab_w_out': nrm((N_EVEN, AB_OUT, dm), AB_OUT ** -0.5),
        'ab_conv_w': nrm((N_EVEN, CONV_W, LRU_WIDTH), CONV_W ** -0.5),
        'ab_conv_b': nrm((N_EVEN, LRU_WIDTH), 0.02),
        'ab_w_r': nrm((N_EVEN, 2, LRU_BLOCKS, LRU_BLOCK, LRU_BLOCK), LRU_BLOCK ** -0.5),
        'ab_b_r': nrm((N_EVEN, 2, LRU_WIDTH), 0.02),
        'ab_w_i': nrm((N_EVEN, 2, LRU_BLOCKS, LRU_BLOCK, LRU_BLOCK), LRU_BLOCK ** -0.5),
        'ab_b_i': nrm((N_EVEN, 2, LRU_WIDTH), 0.02),
        'ab_lam': jnp.log(a0) - jnp.log1p(-a0),
        'ab_sink': nrm((N_EVEN, WIN_HEADS), 0.5),
        'cd_w_in': nrm((N_ODD, dm, CD_IN), dm ** -0.5),
        'cd_w_out': nrm((N_ODD, CD_OUT, dm), CD_OUT ** -0.5),
        'cd_lam': nrm((N_ODD, 4, DIFF_DH), 0.1),
        'cd_subln_g': 1.0 + nrm((N_ODD, 2 * DIFF_DH), 0.02),
        'cd_conv_w': nrm((N_ODD, CONV_W, SSD_CONV_DIM), CONV_W ** -0.5),
        'cd_conv_b': nrm((N_ODD, SSD_CONV_DIM), 0.02),
        'cd_dt_bias': dt0 + jnp.log(-jnp.expm1(-dt0)),
        'cd_a_log': jnp.log(unif((N_ODD, 2, SSD_HEADS), 1.0, 16.0)),
        'cd_d_skip': 1.0 + nrm((N_ODD, SSD_HEADS), 0.1),
        'cd_norm_g': 1.0 + nrm((N_ODD, SSD_INNER), 0.02),
        'w_router': nrm((DEPTH, dm, N_EXPERTS), dm ** -0.5),
        'b_router': nrm((DEPTH, N_EXPERTS), 0.01),
        'w_e_gate': nrm((DEPTH, N_EXPERTS, dm, D_EXPERT), dm ** -0.5),
        'w_e_up': nrm((DEPTH, N_EXPERTS, dm, D_EXPERT), dm ** -0.5),
        'w_e_down': nrm((DEPTH, N_EXPERTS, D_EXPERT, dm), D_EXPERT ** -0.5),
        'ws_gate': nrm((DEPTH, dm, D_SHARED), dm ** -0.5),
        'ws_up': nrm((DEPTH, dm, D_SHARED), dm ** -0.5),
        'ws_down': nrm((DEPTH, D_SHARED, dm), D_SHARED ** -0.5),
    }

def reference(x, c, ctx, c_ctx, w_mod, b_mod, g_mix, g_ffn, g_final,
              ab_w_in, ab_w_out, ab_conv_w, ab_conv_b, ab_w_r, ab_b_r, ab_w_i, ab_b_i, ab_lam, ab_sink,
              cd_w_in, cd_w_out, cd_lam, cd_subln_g, cd_conv_w, cd_conv_b, cd_dt_bias, cd_a_log, cd_d_skip,
              cd_norm_g, w_router, b_router, w_e_gate, w_e_up, w_e_down, ws_gate, ws_up, ws_down):
    bsz, s_len, dm = x.shape
    c_len = ctx.shape[1]
    cs = jax.nn.silu(c)
    ccs = jax.nn.silu(c_ctx)
    for l in range(DEPTH):
        last = l == DEPTH - 1
        i = l // 2
        ml = (cs @ w_mod[l] + b_mod[l])[:, None, :]
        mc = ccs @ w_mod[l] + b_mod[l]
        sh1, sc1, g1, sh2, sc2, g2 = jnp.split(ml, N_MOD, axis=-1)
        csh1, csc1, cg1, csh2, csc2, cg2 = jnp.split(mc, N_MOD, axis=-1)
        hl = modulate(rms_norm(x, g_mix[l]), sh1, sc1)
        hc = modulate(rms_norm(ctx, g_mix[l]), csh1, csc1)
        if l % 2 == 0:
            ol, oc = mixer_rglru_window(hl, hc, ab_w_in[i], ab_w_out[i], ab_conv_w[i], ab_conv_b[i], ab_w_r[i],
                                        ab_b_r[i], ab_w_i[i], ab_b_i[i], ab_lam[i], ab_sink[i], not last)
        else:
            lam_init = 0.8 - 0.6 * math.exp(-0.3 * l)
            ol, oc = mixer_diff_ssd(hl, hc, cd_w_in[i], cd_w_out[i], cd_lam[i], cd_subln_g[i], cd_conv_w[i],
                                    cd_conv_b[i], cd_dt_bias[i], cd_a_log[i], cd_d_skip[i], cd_norm_g[i],
                                    lam_init, not last)
        x = x + g1 * ol
        hl = modulate(rms_norm(x, g_ffn[l]), sh2, sc2).reshape(bsz * s_len, dm)
        moe_w = (w_router[l], b_router[l], w_e_gate[l], w_e_up[l], w_e_down[l], ws_gate[l], ws_up[l], ws_down[l])
        if last:
            x = x + g2 * moe_ffn(hl, *moe_w).reshape(bsz, s_len, dm)
        else:
            ctx = ctx + cg1 * oc
            hc = modulate(rms_norm(ctx, g_ffn[l]), csh2, csc2).reshape(bsz * c_len, dm)
            f = moe_ffn(jnp.concatenate([hl, hc], axis=0), *moe_w)
            x = x + g2 * f[:bsz * s_len].reshape(bsz, s_len, dm)
            ctx = ctx + cg2 * f[bsz * s_len:].reshape(bsz, c_len, dm)
    return rms_norm(x, g_final)


_drawn_inputs = setup_inputs


def setup_inputs(seed=0):
    import zlib

    import numpy as np

    out = dict(_drawn_inputs(seed))
    spreads = {}
    factors = {'g_final': 2.931,
     'ab_b_r': 4.987,
     'ab_b_i': 4.898,
     'ab_sink': 8.0,
     'cd_lam': 5.686,
     'cd_subln_g': 8.0,
     'cd_conv_b': 3.841,
     'cd_d_skip': 3.101,
     'cd_norm_g': 5.489}
    for name, (base, spread) in spreads.items():
        noise = np.random.default_rng([zlib.crc32(name.encode()), seed]).standard_normal(out[name].shape)
        drawn = base * np.exp(spread * noise) if base else spread * noise
        out[name] = jnp.asarray(drawn.astype(out[name].dtype))
    for name, factor in factors.items():
        out[name] = (out[name] * factor).astype(out[name].dtype)
    return out
```

```python
from contextlib import ExitStack
import math

import numpy as np

import concourse.bass as bass
from concourse import mybir

F32 = mybir.dt.float32
I32 = mybir.dt.int32
U32 = mybir.dt.uint32
ALU = mybir.AluOpType
ACT = mybir.ActivationFunctionType
AX = mybir.AxisListType.X

P = 128
D = 1024
KD = D // P
SEQ = 256
CTX = 256
T = SEQ + CTX
NT = T // P
NL = SEQ // P
DEPTH = 2
EPS = 1e-6
NE = 64
NG = 8
TOPG = 4
TOPK = 8
DE = 256
SCALED = 2.5
OVB = 32
MORE_STEPS = 13
NCOL = NE + OVB
BIG = float(1 << 20)
NEG = -1e30
SCALE = 0.125
LAM_INIT = 0.8 - 0.6 * math.exp(-0.3)
GRID_W = 64
H = SEQ
PADW = SEQ + 3
LRU_C = 8.0


def chunks(d):
    return (2, 3, 0, 1) if d == 0 else (3, 2, 1, 0)


STAGES = []
for _l in range(DEPTH):
    STAGES += [f"{n}{_l}" for n in (
        ("mod", "norm1", "proj", "lru", "attn", "out") if _l == 0 else
        ("mod", "norm1", "proj", "conv", "attn", "ssd", "out"))]
    STAGES += [f"{n}{_l}" for n in ("norm2", "route", "experts", "more", "combine")]

CONSTS = ["ident", "swap", "cos", "sin", "tri_le", "tri_ge", "tri_lt", "ones", "mask_lo", "mask_hi",
          "iota", "rowid", "pcol"]
CWID = dict(cos=SEQ, sin=SEQ, rowid=NT * TOPK, pcol=1)


def const_columns():
    at, n = {}, 0
    for c in CONSTS:
        w = CWID.get(c, P)
        at[c] = (n, n + w)
        n += w
    return at, n


def const_table():
    at, n = const_columns()
    t = np.zeros((P, n), np.float32)

    def put(name, a):
        t[:, at[name][0]:at[name][1]] = a

    r = np.arange(P)
    put("ident", np.eye(P))
    put("swap", np.eye(P)[(r // 64) * 64 + (r % 64 + 32) % 64])
    half = 16
    inv = (np.float32(10000.0) ** (-np.arange(half, dtype=np.float32) / np.float32(half))).astype(np.float32)
    tok = np.arange(SEQ)
    row, col = (tok // GRID_W).astype(np.float32), (tok % GRID_W).astype(np.float32)
    ang = np.concatenate([row[:, None] * inv, col[:, None] * inv], axis=-1).astype(np.float32)
    put("cos", np.cos(ang).T[r % 32])
    put("sin", np.sin(ang).T[r % 32] * np.where(r % 64 < 32, -1.0, 1.0)[:, None])
    a, b = r[:, None], r[None, :]
    put("tri_le", a <= b)
    put("tri_ge", a >= b)
    put("tri_lt", a < b)
    put("ones", 1.0)
    put("mask_lo", np.where(b < a, NEG, 0.0))
    put("mask_hi", np.where(b > a, NEG, 0.0))
    put("iota", np.broadcast_to(b, (P, P)))
    k = np.arange(NT * TOPK)[None, :]
    put("rowid", ((k // TOPK) * P + a) * TOPK + k % TOPK + 1)
    put("pcol", a)
    return t


def select_rows():
    s = np.zeros((2, 2, P), np.float32)
    s[0, 0] = 1.0
    s[1, 1] = 1.0
    return s.reshape(2, 2 * P)


V_CONVW, V_CONVB, V_BR, V_BI, V_LAM, V_DCONVW, V_DCONVB = 0, 16, 20, 28, 36, 44, 76
V_ROWS = 84
N_SMALL = 4 + 2 * DEPTH + 7 + 7


def build(nc, a, out):
    at, ncon = const_columns()
    ctx = ExitStack()
    with ctx:
        def sb(name, shape, dt=F32):
            return ctx.enter_context(nc.sbuf_tensor(name, shape, dt))

        sems = {}

        def S(name):
            if name not in sems:
                sems[name] = ctx.enter_context(nc.semaphore(name))
            return sems[name]

        X = sb("X", [P, NT, D])
        hT = sb("hT", [P, KD, T])
        G = sb("G", [P, 2, 2, D])
        stream = sb("stream", [P, 2, KD, 512])
        wg = sb("wg", [P, 2, KD, DE])
        wu = sb("wu", [P, 2, KD, DE])
        wd = sb("wd", [P, 2, 2, D])
        con = sb("con", [P, ncon])
        C = {n: con[:, at[n][0]:at[n][1]] for n in CONSTS}
        sel = sb("sel", [2, 2 * P])
        VT = sb("VT", [P, V_ROWS])
        craw = sb("craw", [P, 2, KD])
        csT = sb("csT", [P, KD, 2])
        gvec = sb("gvec", [P, 2, DEPTH, KD])
        modT = sb("modT", [P, 4, KD, 2])
        mscale = sb("mscale", [P, 2, KD, 2])
        half_exp = sb("half_exp", [P, 8])
        router_w = sb("router_w", [P, KD, NE])
        router_b = sb("router_b", [P, NE])
        gates = sb("gates", [P, NT, TOPK])
        small = sb("small", [P, 320])
        rows_i = sb("rows_i", [P, NCOL], I32)
        toks_i = sb("toks_i", [P, NCOL], I32)
        gat_i = sb("gat_i", [P, 2], I32)
        sca_i = sb("sca_i", [P, 2], I32)
        more_i = sb("more_i", [P, 1], I32)
        moree_i = sb("moree_i", [1, P], I32)
        RW = 14336
        R = sb("R", [P, RW])
        B = [ctx.enter_context(nc.psum_tensor(f"B{i}", [P, 512], F32)) for i in range(8)]

        h_rows = nc.dram_tensor("h_rows", (T, D), F32, kind="Internal").ap()
        y_rows = nc.dram_tensor("y_rows", (T * TOPK, D), F32, kind="Internal").ap()

        def rv(off, *dims):
            n = math.prod(dims)
            assert off + n <= RW
            v = R[:, off:off + n]
            if len(dims) == 2:
                return v.rearrange("p (a b) -> p a b", b=dims[1])
            if len(dims) == 3:
                return v.rearrange("p (a b c) -> p a b c", b=dims[1], c=dims[2])
            return v

        def bc(ap, axis, n):
            v = ap.unsqueeze(axis)
            shape = list(v.shape)
            shape[axis] = n
            return v.to_broadcast(shape)

        modrow = R[0:2, 4096:4096 + 6 * D]
        xn = rv(0, NT, D)
        vraw = R[0:V_ROWS, 0:P]
        catA = rv(0, 8, T)
        bdiag = rv(4096, 16, P)
        kd = rv(6144, 2, T)
        ktmp = rv(7168, T)
        vA = rv(7680, NT, P)
        xap = rv(8192, 4, 2 * PADW)
        uA = hT[:, 0:4, :]
        rec = hT[:, 4:8, :]
        a4, m4, z4 = rv(8192, 4, T), rv(10240, 4, T), rv(12288, 4, T)
        pA, pTA, attA = rv(8192, 2, T), rv(9216, 2, T), rv(10240, 512)
        catC = rv(0, 8, SEQ)
        qC = rv(2048, 4, SEQ)
        zC = rv(3072, NL, 512)
        kC = rv(4096, 4, T)
        vC = rv(6144, NT, 512)
        xbc = rv(8192, 8, 2 * PADW)
        ropeC = rv(12336, SEQ)
        dtraw = rv(12592, NT, 16)
        dtw = rv(12656, KD, 16)
        pC = rv(8192, 4, T)
        wTC = rv(10240, 2, T)
        oC = rv(11264, 512)
        sqC = rv(11776, 512)
        xtok = rv(8192, NT, 512)
        btok = rv(10240, NT, 256)
        cbT = rv(11264, 4, P)
        seg = rv(11776, 512)
        tri_dta = rv(4096, 512)
        xdt = rv(4608, 512)
        xte = rv(5120, 512)
        Hst = rv(5632, 512)
        yacc = rv(6144, NL, 512)
        ytmp = rv(7168, 512)
        oh = rv(4096, NT, TOPK * NE)
        lo_oh = rv(6144, TOPK, P)
        hi_oh = rv(7168, TOPK, NCOL)
        ohtmp = rv(7936, 512)
        actS = rv(8448, 2, T)
        sS = rv(9472, 2, T)
        scores = rv(10496, NT, NE)
        Msel = rv(10752, NT, NE)
        rank = rv(11008, NT, NE)
        cnt = rv(11264, NE)
        tabf = rv(11328, NCOL)
        tab2 = rv(11424, NCOL)
        selv = rv(11520, NE)
        t64a = rv(11584, NE)
        t64b = rv(11648, NE)
        srt = rv(11712, NG, 8)
        ends = rv(11776, NE)
        v1 = rv(11840, NE)
        gsc = rv(11904, 8)
        gtop = rv(11912, 8)
        gidx = rv(11920, 8)
        goh = rv(11928, TOPG, NG)
        gmask = rv(11960, 8)
        top8 = rv(11968, 8)
        idx8 = rv(11976, 8)
        r8 = rv(11984, 8)
        q8 = rv(11992, 8)
        b8 = rv(12000, 8)
        c8 = rv(12008, 8)
        i8 = rv(12016, 8).bitcast(U32)
        s1 = rv(12024, 8)
        xg = rv(0, 2, D)
        xgT = rv(2048, 2, D)
        ysb = rv(4096, 2, D)
        sg = rv(6144, 2, DE)
        act_ = rv(6656, 2, DE)
        actT = rv(7168, 2, 2 * P)
        ych = rv(0, 2, 4 * D)
        acc = rv(8192, D)

        ss = small[:, 0:4]
        rstd = small[:, 4:8]
        nmx = small[:, 8:40]
        rsum = small[:, 40:72]
        sinkb = small[:, 72:80]
        sink8 = small[:, 80:88]
        lsc = small[:, 88:96]
        lnsc = small[:, 96:104]
        hbr = small[:, 104:112]
        hbi = small[:, 112:120]
        dskip = small[:, 120:128]
        alog = small[:, 128:144]
        dtb = small[:, 144:160]
        lamc = small[:, 160:168]
        tmpc = small[:, 168:232]
        nac_ = small[:, 232:296]
        ovf = small[:, 296:300]
        dt_ = sb("dt_", [P, NT, 16])
        dta = sb("dta", [P, NT, 16])
        acum = sb("acum", [P, NT, 16])
        eac = sb("eac", [P, NT, 16])
        tend = sb("tend", [P, NT, 16])
        etot = sb("etot", [P, NT, 16])
        subg = sb("subg", [P, P])
        normg = sb("normg", [P, 512])
        lamv = sb("lamv", [P, 256])

        stage_no = {s: i for i, s in enumerate(STAGES)}

        def end_stage(eng, name):
            eng.drain().then_inc(S("stage_ended"), 1)
            eng.wait_ge(S("stage_ended"), 4 * (stage_no[name] + 1))

        def after_stage(eng, name):
            eng.wait_ge(S("stage_ended"), 4 * (stage_no[name] + 1))

        def linker(eng, own):
            count = {}

            def link(ins, name=own, wait=True):
                ins.then_inc(S(name), 1)
                count[name] = count.get(name, 0) + 1
                if wait:
                    eng.wait_ge(S(name), count[name])
                return count[name]
            return link

        def wait(eng, name, value, earlier=0):
            if not (isinstance(value, int) and value <= 0):
                eng.wait_ge(S(name), value + earlier)

        def nth(l, i, n):
            pair = i + (n // 2 + (NE // 2) * l)
            return pair * 2 + n % 2, pair, n % 2

        def over_pairs(eng, body):
            body(0)
            body(1)
            with eng.Fori(2, NE // 2 - 1) as i:
                body(i)
            body(NE // 2 - 1)

        norm_tiles = [NT, NT, NT, NL, NL]

        first_layer = dict(
            ld_bmod=16, ld_router=32, ld_shared=32, ld_sdown=16, hrow_act=NT, hrow_dve=NT, h_stored=16 * NT,
            ych_used=2 * NT, g_bcast=8, row_turned=2 * NT, logits=1, scores=1, shared_gu=4, shared_silu=2,
            mod_rows=14, mod_turned=1, modT=1, Msel=NT, ranks=1, more_col=1, more_row=1, act_shared=2,
            shared_out=2 * NT, shared_y=2 * NT, onehot=NT, table=NT, out=2 * NT)
        ms_order = [0, 1, 2, "d0", "d1", "s0", "s1", 3, 4]

        def before(name, key):
            if name in first_layer:
                return first_layer[name] * key
            if name in ("ms", "rstd"):
                return ms_order.index(key)
            per_tile = {"ss": 1.0, "xn_act": 0.5, "xn_dve": 0.5, "hT_act": 2.0, "hT_dve": 2.0}
            if name == "xT":
                return KD * key
            return int(per_tile[name] * sum(norm_tiles[:key]))

        proj1 = ([("q", 0, m) for m in range(4)] + [("z", 1, t) for t in range(NL)]
                 + [("k", 2, m) for m in range(4)] + [("v", 3, t) for t in range(NT)]
                 + [("xbc", 4, m) for m in range(4)] + [("xbc", 5, 4 + m) for m in range(4)]
                 + [("dt", None, 0)])

        def gate_banks(l):
            return [(gi, s, h, (3 + gi * 4 + s * 2 + h) % 8)
                    for gi in range(2) for s in range(2 if l == 0 else 1) for h in range(2)]

        def row_half(t, half):
            return xn[:, t, :].rearrange("q (p k) -> q k p", k=KD)[:, 4 * half:4 * half + 4, :]

        def proj1_move(n):
            kind, _, m = proj1[n]
            bank = B[n % 8]
            if kind == "q":
                return qC[:, m, :], bank[:, 0:SEQ]
            if kind == "xbc":
                return (xbc[:, m, :].rearrange("p (s w) -> p s w", s=2)[:, :, 1:1 + H],
                        bank[:, :].rearrange("p (s w) -> p s w", s=2))
            if kind == "dt":
                return dtraw, bank[:, 0:NT * 16].rearrange("p (t h) -> p t h", t=NT)
            return {"z": zC, "k": kC, "v": vC}[kind][:, m, :], bank[:, :]

        n_in = [4, 6]
        base = [0, 12 + n_in[0] + 2 + 2]
        total_blocks = base[1] + 12 + n_in[1] + 2 + 2
        assert base[1] % 2 == 0

        block = ctx.enter_context(nc.Block())

        @block.sync
        def _(sp):

            def small_load(dst, src):
                sp.dma_start(dst, src).then_inc(S("ld_small"), 16)

            small_load(con[:], a["con"])
            small_load(sel[:], a["sel"])
            small_load(craw[:, 0, :], a["c"][0, :].rearrange("(p k) -> p k", k=KD))
            small_load(craw[:, 1, :], a["c_ctx"].rearrange("(p k) -> p k", k=KD))
            for l in range(DEPTH):
                for i, n in enumerate(("g_mix", "g_ffn")):
                    small_load(gvec[:, i, l, :], a[n][l].rearrange("(p k) -> p k", k=KD))
            for src, r0 in ((a["ab_conv_w"][0], V_CONVW), (a["ab_conv_b"], V_CONVB), (a["ab_b_r"][0], V_BR),
                            (a["ab_b_i"][0], V_BI), (a["ab_lam"][0], V_LAM), (a["cd_conv_w"][0], V_DCONVW),
                            (a["cd_conv_b"], V_DCONVB)):
                rows = src.rearrange("r (c p) -> (r c) p", p=P)
                small_load(R[r0:r0 + rows.shape[0], 0:P], rows)
            for dst, src in ((sinkb, a["ab_sink"][0:1, :]), (dskip, a["cd_d_skip"][0:1, :]),
                             (alog, a["cd_a_log"].rearrange("a d h -> a (d h)")),
                             (dtb, a["cd_dt_bias"].rearrange("a d h -> a (d h)")),
                             (lamv[:], a["cd_lam"].rearrange("a d h -> a (d h)")),
                             (subg[:], a["cd_subln_g"][0:1, :]), (normg[:], a["cd_norm_g"][0:1, :])):
                small_load(dst, src.to_broadcast([P, src.shape[1]]))

            def load_block(s, slot, src, ncols=512):
                sp.wait_ge(S("stream_free"), s + 1)
                sp.dma_start(stream[:, slot, :, 0:ncols], src).then_inc(S(f"stream_ld{slot}"), 16)

            def load_expert(l, i, n):
                e, pair, slot = nth(l, i, n)
                wait(sp, "gu_done", e - 1)
                el = i * 2 + n
                one = (lambda w: w[l, el]) if isinstance(i, int) else (lambda w: w[l, bass.ds(el, 1)].squeeze(0))
                sp.dma_start(wg[:, slot], one(a["w_e_gate"]).rearrange("(p k) f -> p k f", k=KD)).then_inc(S(f"gu_ld{slot}"), 16)
                sp.dma_start(wu[:, slot], one(a["w_e_up"]).rearrange("(p k) f -> p k f", k=KD)).then_inc(S(f"gu_ld{slot}"), 16)
                wait(sp, "y_done", e * 2 - 2)
                sp.dma_start(wd[:, slot], one(a["w_e_down"]).rearrange("(p j) n -> p j n", j=2)).then_inc(S(f"down_ld{slot}"), 16)

            for l in range(DEPTH):
                nt = NT if l == 0 else NL
                if l:
                    after_stage(sp, f"combine{l - 1}")
                sp.dma_start(modrow, a["b_mod"][l:l + 1, :].to_broadcast([2, 6 * D])).then_inc(S("ld_bmod"), 16)
                sp.dma_start(router_w[:], a["w_router"][l].rearrange("(p k) e -> p k e", k=KD)).then_inc(S("ld_router"), 16)
                sp.dma_start(router_b[:], a["b_router"][l:l + 1, :].to_broadcast([P, NE])).then_inc(S("ld_router"), 16)
                w_mod = a["w_mod"][l].rearrange("(p k) n -> p k n", k=KD)
                with sp.Fori(0, 6) as i:
                    for j in range(2):
                        load_block(i * 2 + (base[l] + j), j, w_mod[:, :, bass.ds(i * 1024 + j * 512, 512)])
                if l == 0:
                    sp.dma_start(X[:, 0:NL, :], a["x"][0].rearrange("(t p) d -> p t d", p=P)).then_inc(S("ld_x"), 16)
                    sp.dma_start(X[:, NL:NT, :], a["ctx"][0].rearrange("(t p) d -> p t d", p=P)).then_inc(S("ld_x"), 16)
                s = base[l] + 12
                w_in = (a["ab_w_in"] if l == 0 else a["cd_w_in"])[0].rearrange("(p k) n -> p k n", k=KD)
                for n in range(n_in[l]):
                    width = 256 if (l == 0 and n == 3) else 512
                    load_block(s, s % 2, w_in[:, :, n * 512:n * 512 + width], width)
                    s += 1
                    if n == 1:
                        load_expert(l, 0, 0)
                        load_expert(l, 0, 1)
                        after_stage(sp, f"norm1{l}")
                        if l == 0:
                            sp.wait_ge(S("bdiag_zeroed"), 1)
                            for d in range(2):
                                for m, nm in enumerate(("ab_w_r", "ab_w_i")):
                                    src = a[nm][0, d].rearrange("(c b) i j -> b i c j", b=2)
                                    for b in range(2):
                                        q = d * 8 + m * 4
                                        sp.dma_start(bdiag[64 * b:64 * b + 64, q:q + 4, 64 * b:64 * b + 64],
                                                     src[b]).then_inc(S("ld_bdiag"), 16)
                        else:
                            sp.dma_start(dtw, w_in[:, :, 3072:3088]).then_inc(S("ld_dtw"), 16)
                w_out = (a["ab_w_out"] if l == 0 else a["cd_w_out"])[0].rearrange("(k p) n -> p k n", p=P)
                for n in range(2):
                    load_block(s, s % 2, w_out[:, :, n * 512:n * 512 + 512])
                    s += 1
                sp.wait_ge(S("stream_free"), s + 1)
                for n, nm in enumerate(("ws_gate", "ws_up")):
                    sp.dma_start(stream[:, s % 2, :, n * DE:(n + 1) * DE],
                                 a[nm][l].rearrange("(p k) n -> p k n", k=KD)).then_inc(S("ld_shared"), 16)
                s += 1
                sp.wait_ge(S("stream_free"), s + 1)
                sp.dma_start(stream[:, s % 2, 0:4, :],
                             a["ws_down"][l].rearrange("(j p) (h n) -> p j h n", p=P, h=2)).then_inc(S("ld_sdown"), 16)
                for t in range(nt):
                    sp.wait_ge(S("hrow_act"), t + 1 + before("hrow_act", l))
                    sp.wait_ge(S("hrow_dve"), t + 1 + before("hrow_dve", l))
                    sp.dma_start(h_rows[t * P:(t + 1) * P, :], xn[:, t, :]).then_inc(S("h_stored"), 16)
                with sp.Fori(1, NE // 2) as i:
                    for n in range(2):
                        load_expert(l, i, n)
                after_stage(sp, f"experts{l}")
                more = sp.value_load(more_i[0:1, 0:1], min_val=0, max_val=OVB)
                with sp.If(more):
                    with sp.Fori(0, OVB) as i:
                        e = sp.value_load(moree_i[0:1, bass.ds(i, 1)], min_val=0, max_val=NE - 1)
                        sp.wait_ge(S(f"more_step{l}"), i * MORE_STEPS + 2)
                        sp.dma_start(wg[:, 0], a["w_e_gate"][l, bass.ds(e, 1)].squeeze(0).rearrange("(p k) f -> p k f", k=KD)).then_inc(S(f"more_w{l}"), 16)
                        sp.dma_start(wu[:, 0], a["w_e_up"][l, bass.ds(e, 1)].squeeze(0).rearrange("(p k) f -> p k f", k=KD)).then_inc(S(f"more_w{l}"), 16)
                        sp.dma_start(wd[:, 0], a["w_e_down"][l, bass.ds(e, 1)].squeeze(0).rearrange("(p j) n -> p j n", j=2)).then_inc(S(f"more_w{l}"), 16)
                after_stage(sp, f"more{l}")
                yv = y_rows.rearrange("(t p q k) d -> t q p (k d)", p=P, q=2, k=4)
                for t in range(nt):
                    for q in range(2):
                        wait(sp, "ych_used", 2 * t + q - 1, before("ych_used", l))
                        sp.dma_start(ych[:, q, :], yv[t, q]).then_inc(S(f"ych_ld{q}"), 16)
            after_stage(sp, f"combine{DEPTH - 1}")
            sp.dma_start(G[:, 0, 0, :], a["g_final"].unsqueeze(0).to_broadcast([P, D])).then_inc(S("ld_gfin"), 16)
            for t in range(NL):
                sp.wait_ge(S("out_ready"), t + 1)
                sp.dma_start(out[0, t * P:(t + 1) * P, :], xn[:, t, :]).then_inc(S("out_stored"), 16)
            sp.wait_ge(S("out_stored"), 16 * NL)

        @block.gpsimd
        def _(pool):
            link = linker(pool, "pool_chain")

            def waited():
                pool.sem_inc(S("pool_waited"), 1)

            def rsqrt(q, n=4):
                pool.wait_ge(S("ms"), 1 + before("ms", q))
                pool.tensor_tensor(rstd[:, 0:n], ss[:, 0:n], half_exp[:, 0:n], ALU.pow).then_inc(S("rstd"), 1)

            link(pool.memset(half_exp[:], -0.5))
            for l in range(DEPTH):
                nt = NT if l == 0 else NL
                end_stage(pool, f"mod{l}")
                rsqrt(2 * l, NT)
                end_stage(pool, f"norm1{l}")
                if l == 0:
                    link(pool.memset(xap, 0.0), "pads_zeroed")
                    link(pool.memset(bdiag, 0.0), "bdiag_zeroed")
                    for s in ("proj0", "lru0", "attn0", "out0"):
                        end_stage(pool, s)
                else:
                    link(pool.memset(xbc, 0.0), "pads_zeroed")
                    end_stage(pool, "proj1")
                    end_stage(pool, "conv1")
                    for qt in range(NL):
                        rsqrt(f"d{qt}")
                    end_stage(pool, "attn1")
                    for c in range(NL):
                        rsqrt(f"s{c}", 2)
                    end_stage(pool, "ssd1")
                    end_stage(pool, "out1")
                rsqrt(2 * l + 1, nt)
                end_stage(pool, f"norm2{l}")
                pool.wait_ge(S("h_stored"), 16 * nt + before("h_stored", l))
                link(pool.memset(xg, 0.0))
                end_stage(pool, f"route{l}")

                def gather(i, n):
                    e, pair, slot = nth(l, i, n)
                    wait(pool, "x_turned", e * 2 - 2)
                    waited()
                    pool.tensor_copy(gat_i[:, slot:slot + 1], toks_i[:, bass.ds(i * 2 + n, 1)]).then_inc(S("gat_idx"), 1)
                    pool.wait_ge(S("gat_idx"), e + 1)
                    waited()
                    pool.indirect_dma_start(out=xg[:, slot, :], out_offset=None, in_=h_rows,
                                            in_offset=bass.IndirectOffsetOnAxis(gat_i[:, slot:slot + 1], 0),
                                            bounds_check=nt * P - 1, oob_is_err=False).then_inc(S(f"xg_ld{slot}"), 16)

                def scatter(i, n):
                    e, pair, slot = nth(l, i, n)
                    wait(pool, f"y_stored{slot}", pair * 16)
                    waited()
                    pool.tensor_copy(sca_i[:, slot:slot + 1], rows_i[:, bass.ds(i * 2 + n, 1)]).then_inc(S("sca_idx"), 1)
                    pool.wait_ge(S("sca_idx"), e + 1)
                    pool.wait_ge(S("y_act"), e + 1)
                    pool.wait_ge(S("y_dve"), e + 1)
                    waited()
                    pool.indirect_dma_start(out=y_rows, out_offset=bass.IndirectOffsetOnAxis(sca_i[:, slot:slot + 1], 0),
                                            in_=ysb[:, slot, :], in_offset=None,
                                            bounds_check=nt * P * TOPK - 1, oob_is_err=False).then_inc(S(f"y_stored{slot}"), 16)

                def pair_of(i):
                    for n in range(2):
                        if not (isinstance(i, int) and i == NE // 2 - 1):
                            gather(i, n + 2)
                        scatter(i, n)

                gather(0, 0)
                gather(0, 1)
                over_pairs(pool, pair_of)
                for n in range(2):
                    pool.wait_ge(S(f"y_stored{n}"), 16 * (NE // 2) * (l + 1))
                end_stage(pool, f"experts{l}")
                more = pool.value_load(more_i[0:1, 0:1], min_val=0, max_val=OVB)
                with pool.If(more):
                    with pool.Fori(0, OVB) as i:
                        step = S(f"more_step{l}")
                        pool.tensor_copy(gat_i[:, 0:1], toks_i[:, bass.ds(i + NE, 1)]).then_inc(step, 1)
                        pool.tensor_copy(sca_i[:, 0:1], rows_i[:, bass.ds(i + NE, 1)]).then_inc(step, 1)
                        pool.wait_ge(step, i * MORE_STEPS + 2)
                        waited()
                        pool.indirect_dma_start(out=xg[:, 0, :], out_offset=None, in_=h_rows,
                                                in_offset=bass.IndirectOffsetOnAxis(gat_i[:, 0:1], 0),
                                                bounds_check=nt * P - 1, oob_is_err=False).then_inc(S(f"more_dma{l}"), 16)
                        pool.wait_ge(step, i * MORE_STEPS + 13)
                        waited()
                        pool.indirect_dma_start(out=y_rows, out_offset=bass.IndirectOffsetOnAxis(sca_i[:, 0:1], 0),
                                                in_=ysb[:, 0, :], in_offset=None,
                                                bounds_check=nt * P * TOPK - 1, oob_is_err=False).then_inc(S(f"more_dma{l}"), 16)
                        pool.wait_ge(S(f"more_dma{l}"), i * 32 + 32)
                end_stage(pool, f"more{l}")
                end_stage(pool, f"combine{l}")
            rsqrt(4, NL)
            pool.drain()

        @block.scalar
        def _(act):
            link = linker(act, "act_chain")

            def squares(q):
                for t in range(norm_tiles[q]):
                    link(act.activation(xn[:, t, :], X[:, t, :], ACT.Square, accum_out=ss[:, t:t + 1]), "ss")

            def norm(q, which):
                nt = norm_tiles[q]
                squares(q)
                act.wait_ge(S("rstd"), 1 + before("rstd", q))
                for t in range(0, nt, 2):
                    link(act.activation(xn[:, t, :], X[:, t, :], ACT.Copy, scale=rstd[:, t:t + 1]), "xn_act")
                for k in range(0, KD, 2):
                    act.wait_ge(S("xT"), k + 1 + before("xT", q))
                    for s in range(nt // 2):
                        link(act.activation(hT[:, k, s * H:s * H + H], B[k][:, s * H:s * H + H], ACT.Identity,
                                            scale=mscale[:, which, k, s:s + 1], bias=modT[:, 2 * which, k, s:s + 1]), "hT_act")

            act.wait_ge(S("ld_small"), 16 * N_SMALL)
            link(act.activation(csT[:].rearrange("p k s -> p s k"), craw[:], ACT.Silu), "c_silu")
            act.wait_ge(S("ld_x"), 32)
            for l in range(DEPTH):
                nt = NT if l == 0 else NL
                for n, (gi, s, h, bank) in enumerate(gate_banks(l)):
                    act.wait_ge(S("g_bcast"), n + 1 + before("g_bcast", l))
                    link(act.activation(G[:, gi, s, h * 512:h * 512 + 512], B[bank][:, :], ACT.Copy))
                end_stage(act, f"mod{l}")
                norm(2 * l, 0)
                end_stage(act, f"norm1{l}")
                if l == 0:
                    act.wait_ge(S("pads_zeroed"), 1)
                    for n in range(0, 14, 2):
                        act.wait_ge(S("proj0"), n + 1)
                        src = B[n % 8][:, :]
                        if n < 8:
                            dst = catA[:, n, :]
                        elif n < 12:
                            dst = xap[:, n - 8, :].rearrange("p (s w) -> p s w", s=2)[:, :, 1:1 + H]
                            src = src.rearrange("p (s w) -> p s w", s=2)
                        else:
                            dst = ktmp
                        link(act.activation(dst, src, ACT.Copy), "proj0_act")
                    end_stage(act, "proj0")
                    for m in range(4):
                        link(act.activation(catA[:, m, :], catA[:, m, :], ACT.Gelu_apprx_tanh), "gelu")
                    act.wait_ge(S("rope0"), 5)
                    for g in range(2):
                        for b in range(2):
                            link(act.activation(kd[64 * b:64 * b + 64, g, :], ktmp[64 * g:64 * g + 64, :], ACT.Copy))
                    act.wait_ge(S("lam_abs"), 1)
                    link(act.activation(tmpc[:, 8:16], tmpc[:, 0:8], ACT.Exp, scale=-1.0))
                    link(act.activation(tmpc[:, 16:24], tmpc[:, 8:16], ACT.Ln, bias=1.0), "lam_ln")
                    act.wait_ge(S("lsc_ready"), 1)
                    for d in range(2):
                        wait(act, "scan_done", 4 * d)
                        for c in range(4):
                            n = d * 4 + c
                            act.wait_ge(S("lru_mm"), 2 * n + 1)
                            link(act.activation(a4[:, c, :], B[(2 * n) % 8][:, :], ACT.Tanh, scale=0.5, bias=hbr[:, n:n + 1]), "lru_r")
                            link(act.activation(m4[:, c, :], a4[:, c, :], ACT.Tanh, scale=lnsc[:, n:n + 1], bias=lnsc[:, n:n + 1]), "lru_th")
                            link(act.activation(a4[:, c, :], a4[:, c, :], ACT.Exp, scale=lsc[:, n:n + 1], bias=lsc[:, n:n + 1]), "lru_a")
                            act.wait_ge(S("lru_mm"), 2 * n + 2)
                            link(act.activation(z4[:, c, :], B[(2 * n + 1) % 8][:, :], ACT.Tanh, scale=0.5, bias=hbi[:, n:n + 1]), "lru_i")
                        for c in range(4):
                            n = d * 4 + c
                            act.wait_ge(S("lru_m"), n + 1)
                            link(act.activation(m4[:, c, :], m4[:, c, :], ACT.Sqrt, scale=0.5), "lru_sq")
                    end_stage(act, "lru0")
                    for n in range(8 * NT + 2):
                        if n < 8 * NT:
                            nk = T if n < 8 * NL else CTX
                            act.wait_ge(S("nmax0"), n + 1)
                            wait(act, "p_turned", n - 1)
                            link(act.activation(pA[:, n % 2, 0:nk], B[n % 2][:, 0:nk], ACT.Exp, scale=SCALE, bias=nmx[:, n:n + 1],
                                                accum_out=rsum[:, n:n + 1]), "p_ready")
                        if n and n % 8 == 0:
                            act.wait_ge(S("sink_in"), n // 8)
                            link(act.activation(tmpc[:, 8:16], tmpc[:, 0:8], ACT.Exp), "sink_exp")
                        if n > 1 and n % 8 == 1:
                            qt = n // 8 - 1
                            act.wait_ge(S("att_turned"), qt + 1)
                            link(act.activation(catA[:, 4:8, qt * P:qt * P + P],
                                                B[6 + qt % 2][:, :].rearrange("p (c q) -> p c q", c=4), ACT.Copy), "att_cat")
                    end_stage(act, "attn0")
                    end_stage(act, "out0")
                else:
                    act.wait_ge(S("pads_zeroed"), 2)
                    for n in range(0, len(proj1), 2):
                        act.wait_ge(S("proj1"), n + 1)
                        dst, src = proj1_move(n)
                        link(act.activation(dst, src, ACT.Copy), "proj1_act")
                    end_stage(act, "proj1")
                    for c in range(8):
                        act.wait_ge(S("conv1"), c + 1)
                        link(act.activation(hT[:, c, :], hT[:, c, :], ACT.Silu))
                    link(act.activation(zC, zC, ACT.Silu))
                    act.wait_ge(S("dt_in"), 1)
                    link(act.activation(dta[:], dta[:], ACT.Exp, scale=-1.0))
                    link(act.activation(alog, alog, ACT.Exp))
                    link(act.activation(lamc[:, 0:2], lamc[:, 0:2], ACT.Exp))
                    link(act.activation(dta[:], dta[:], ACT.Ln, bias=1.0), "dt_ln")
                    end_stage(act, "conv1")
                    for u in range(4 * NL + 1):
                        if u < 4 * NL:
                            wait(act, "w_turned", u - 1)
                            for m in range(2):
                                n = 2 * u + m
                                act.wait_ge(S("nmax1"), n + 1)
                                link(act.activation(pC[:, 2 * (u % 2) + m, :], B[n % 2][:, :], ACT.Exp, scale=SCALE, bias=nmx[:, n:n + 1],
                                                    accum_out=rsum[:, n:n + 1]), "p1_ready")
                        if u:
                            act.wait_ge(S("w_turned"), u)
                            link(act.activation(wTC[:, (u - 1) % 2, :], B[2 + (u - 1) % 2][:, :], ACT.Copy), "wT_ready")
                    end_stage(act, "attn1")
                    act.wait_ge(S("acum_ready"), 1)
                    link(act.activation(eac[:], acum[:], ACT.Exp))
                    link(act.activation(tend[:], tend[:], ACT.Exp))
                    link(act.activation(etot[:], etot[:], ACT.Exp), "acum_exp")
                    for n in range(2 * NL * 2):
                        act.wait_ge(S("seg_ready"), n + 1)
                        link(act.activation(seg, seg, ACT.Exp), "seg_exp")
                    end_stage(act, "ssd1")
                    end_stage(act, "out1")
                norm(2 * l + 1, 1)
                for t in range(nt):
                    act.wait_ge(S("row_turned"), 2 * t + 1 + before("row_turned", l))
                    link(act.activation(row_half(t, 0), B[2 * t][:, :].rearrange("q (k p) -> q k p", k=4), ACT.Copy), "hrow_act")
                end_stage(act, f"norm2{l}")
                act.wait_ge(S("logits"), 1 + before("logits", l))
                link(act.activation(scores[:, 0:nt, :], B[0][:, 0:nt * NE].rearrange("p (t e) -> p t e", e=NE), ACT.Sigmoid), "scores")
                for m in range(2):
                    act.wait_ge(S("shared_gu"), 2 * m + 1 + before("shared_gu", l))
                    link(act.activation(sS[:, m, 0:nt * P], B[4 + 2 * m][:, 0:nt * P], ACT.Silu), "shared_silu")
                end_stage(act, f"route{l}")

                def x_evac(i, n):
                    e, pair, slot = nth(l, i, n)
                    act.wait_ge(S("x_turned"), e * 2 + 1)
                    act.activation(xgT[:, slot, 0:512], B[0][:, :], ACT.Copy).then_inc(S("xgT_act"), 1)

                def y_evac(i, n):
                    e, pair, slot = nth(l, i, n)
                    act.wait_ge(S("y_done"), e * 2 + 1)
                    wait(act, f"y_stored{slot}", pair * 16)
                    act.activation(ysb[:, slot, 0:512], B[6][:, :], ACT.Copy).then_inc(S("y_act"), 1)

                def pair_of(i):
                    for n in range(2):
                        e, pair, slot = nth(l, i, n)
                        act.wait_ge(S("gu_done"), e + 1)
                        act.activation(sg[:, slot, :], B[2 + slot][:, 0:DE], ACT.Silu).then_inc(S("sg_ready"), 1)
                        if not (isinstance(i, int) and i == NE // 2 - 1 and n == 1):
                            x_evac(i, n + 1)
                        if not (isinstance(i, int) and i == 0 and n == 0):
                            y_evac(i, n - 1)

                x_evac(0, 0)
                over_pairs(act, pair_of)
                y_evac(NE // 2 - 1, 1)
                end_stage(act, f"experts{l}")
                more = act.value_load(more_i[0:1, 0:1], min_val=0, max_val=OVB)
                with act.If(more):
                    with act.Fori(0, OVB) as i:
                        act.wait_ge(S(f"more_step{l}"), i * MORE_STEPS + 6)
                        act.activation(sg[:, 0, :], B[2][:, 0:DE], ACT.Silu).then_inc(S(f"more_step{l}"), 1)
                end_stage(act, f"more{l}")
                end_stage(act, f"combine{l}")
            squares(4)
            act.drain()

        @block.tensor
        def _(pe):
            def product(out, pairs, start=True):
                for n, (lhsT, rhs) in enumerate(pairs):
                    ins = pe.matmul(out, lhsT, rhs, start=(start and n == 0), stop=(n == len(pairs) - 1))
                return ins

            def turn(out, in_, n=P):
                return pe.transpose(out, in_, C["ident"][0:n, 0:n])

            def block_ready(l, o):
                pe.wait_ge(S(f"stream_ld{o % 2}"), 16 * (9 * l + o // 2 + 1))
                return stream[:, o % 2]

            def norm(q):
                nt = norm_tiles[q]
                pe.wait_ge(S("xn_act"), nt // 2 + before("xn_act", q))
                pe.wait_ge(S("xn_dve"), nt // 2 + before("xn_dve", q))
                for k in range(KD):
                    for t in range(nt):
                        ins = turn(B[k][:, t * P:t * P + P], xn[:, t, k::KD])
                    ins.then_inc(S("xT"), 1)

            pe.wait_ge(S("ld_small"), 16 * N_SMALL)
            pe.sem_inc(S("stream_free"), 2)
            turn(B[7][:, 0:V_ROWS], vraw, V_ROWS).then_inc(S("v_turned"), 1)
            pe.wait_ge(S("c_silu"), 1)
            for l in range(DEPTH):
                nt = NT if l == 0 else NL
                cat = catA if l == 0 else catC
                with pe.Fori(0, 6) as i:
                    for j in range(2):
                        pe.wait_ge(S(f"stream_ld{j}"), i * 16 + 16 * (9 * l + 1))
                        pe.wait_ge(S("mod_rows"), i * 2 + j + 1 + before("mod_rows", l))
                        product(B[j][0:2, :], [(csT[:, k, :], stream[:, j, k, :]) for k in range(KD)]).then_inc(S("stream_free"), 1)
                pe.wait_ge(S("mod_rows"), 14 + before("mod_rows", l))
                for v, split in enumerate((0, 1, 3, 4)):
                    for k in range(KD):
                        ins = turn(B[2][:, (v * KD + k) * 2:(v * KD + k) * 2 + 2],
                                   modrow[:, split * D + k:(split + 1) * D:KD], 2)
                ins.then_inc(S("mod_turned"), 1)
                for gi, s, h, bank in gate_banks(l):
                    if bank == 2:
                        pe.wait_ge(S("modT"), 1 + before("modT", l))
                    c0 = (2 + 3 * gi) * D + h * 512
                    pe.matmul(B[bank][:, :], sel[:, s * P:s * P + P], modrow[:, c0:c0 + 512],
                              start=True, stop=True).then_inc(S("g_bcast"), 1)
                end_stage(pe, f"mod{l}")
                norm(2 * l)
                end_stage(pe, f"norm1{l}")
                if l == 0:
                    for n in range(14):
                        blk, m = n // 4, n % 4
                        if m == 0:
                            W = block_ready(0, 12 + blk)
                        if n >= 8:
                            pe.wait_ge(S("proj0_act" if n % 2 == 0 else "proj0_dve"), (n - 8) // 2 + 1)
                        if n < 13:
                            ins = product(B[n % 8][:, :], [(W[:, k, m * P:m * P + P], hT[:, k, :]) for k in range(KD)])
                        else:
                            for t in range(NT):
                                ins = product(B[n % 8][:, t * P:t * P + P],
                                              [(hT[:, k, t * P:t * P + P], W[:, k, P:2 * P]) for k in range(KD)])
                        ins.then_inc(S("proj0"), 1)
                        if m == 3 or n == 13:
                            pe.drain().then_inc(S("stream_free"), 1)
                    end_stage(pe, "proj0")
                    for m in range(5):
                        src = catA[:, 4 + m, 0:H] if m < 4 else ktmp[:, 0:H]
                        pe.matmul(B[m][:, 0:H], C["swap"], src, start=True, stop=True).then_inc(S("swapped0"), 1)
                    pe.wait_ge(S("ld_bdiag"), 16 * 8)
                    pe.wait_ge(S("rope0"), 5)
                    for d in range(2):
                        for c in range(4):
                            n = d * 4 + c
                            if d == 0:
                                pe.wait_ge(S("conv0"), c + 1)
                            wait(pe, "lru_r", n - 3)
                            pe.matmul(B[(2 * n) % 8][:, :], bdiag[:, d * 8 + c, :], uA[:, c, :], start=True, stop=True).then_inc(S("lru_mm"), 1)
                            wait(pe, "lru_i", n - 3)
                            pe.matmul(B[(2 * n + 1) % 8][:, :], bdiag[:, d * 8 + 4 + c, :], uA[:, c, :], start=True, stop=True).then_inc(S("lru_mm"), 1)
                    end_stage(pe, "lru0")

                    def att_turn(qt):
                        pe.wait_ge(S("att_ready"), qt + 1)
                        wait(pe, "att_cat", qt - 1)
                        for c in range(4):
                            ins = turn(B[6 + qt % 2][:, c * P:c * P + P], attA[:, c * P:c * P + P])
                        ins.then_inc(S("att_turned"), 1)

                    for n in range(8 * NT + 1):
                        if n < 8 * NT:
                            qt, h = n // 8, n % 8
                            b, g = 64 * (h % 2), h // 4
                            k0, nk = (0, T) if qt < NL else (SEQ, CTX)
                            wait(pe, "p_ready", n - 1)
                            masked = {0: P, 1: 0}.get(qt)
                            for c0, c1 in {0: ((0, P), (P, 2 * P), (2 * P, T)), 1: ((0, P), (P, T))}.get(qt, ((0, nk),)):
                                q_ap, k_ap = catA[b:b + 64, 4 + h // 2, qt * P:qt * P + P], kd[b:b + 64, g, k0 + c0:k0 + c1]
                                if c0 == masked:
                                    pe.matmul(B[n % 2][:, c0:c1], C["ident"], C["mask_hi" if qt == 0 else "mask_lo"],
                                              start=True, stop=False)
                                ins = pe.matmul(B[n % 2][:, c0:c1], q_ap, k_ap, start=(c0 != masked), stop=True)
                            ins.then_inc(S("scores0"), 1)
                        if n:
                            m = n - 1
                            qt, h = m // 8, m % 8
                            nk, t0 = (NT, 0) if qt < NL else (NL, NL)
                            pe.wait_ge(S("p_ready"), m + 1)
                            wait(pe, "pT_ready", m - 1)
                            for t in range(nk):
                                ins = turn(B[2 + m % 2][:, t * P:t * P + P], pA[:, m % 2, t * P:t * P + P])
                            ins.then_inc(S("p_turned"), 1)
                            pe.wait_ge(S("pT_ready"), m + 1)
                            if h == 0:
                                wait(pe, "att_ready", qt - 1)
                            g = h // 4
                            ins = product(B[4 + qt % 2][:, h * 64:h * 64 + 64],
                                          [(pTA[:, m % 2, t * P:t * P + P], vA[:, t0 + t, g * 64:g * 64 + 64]) for t in range(nk)])
                            if h == 7:
                                ins.then_inc(S("pv_done"), 1)
                            if h == 0 and qt:
                                att_turn(qt - 1)
                    att_turn(NT - 1)
                    end_stage(pe, "attn0")
                else:
                    for n, (kind, blk, m) in enumerate(proj1):
                        first = n == 0 or proj1[n - 1][1] != blk
                        last = n + 1 == len(proj1) or proj1[n + 1][1] != blk
                        if kind == "dt":
                            pe.wait_ge(S("ld_dtw"), 16)
                        elif first:
                            W = block_ready(1, 12 + blk)
                        if n >= 8:
                            pe.wait_ge(S("proj1_act" if n % 2 == 0 else "proj1_dve"), (n - 8) // 2 + 1)
                        m4_ = m % 4
                        if kind == "q":
                            ins = product(B[n % 8][:, 0:SEQ], [(W[:, k, m * P:m * P + P], hT[:, k, 0:SEQ]) for k in range(KD)])
                        elif kind in "zv":
                            ins = product(B[n % 8][:, :], [(hT[:, k, m * P:m * P + P], W[:, k, :]) for k in range(KD)])
                        elif kind == "dt":
                            for t in range(NT):
                                ins = product(B[n % 8][:, t * 16:t * 16 + 16],
                                              [(hT[:, k, t * P:t * P + P], dtw[:, k, :]) for k in range(KD)])
                        else:
                            ins = product(B[n % 8][:, :], [(W[:, k, m4_ * P:m4_ * P + P], hT[:, k, :]) for k in range(KD)])
                        ins.then_inc(S("proj1"), 1)
                        if last and kind != "dt":
                            pe.drain().then_inc(S("stream_free"), 1)
                    end_stage(pe, "proj1")
                    for m in range(8):
                        src = qC[:, m, :] if m < 4 else kC[:, m - 4, 0:SEQ]
                        pe.matmul(B[m][:, 0:SEQ], C["swap"], src, start=True, stop=True).then_inc(S("swapped1"), 1)
                    end_stage(pe, "conv1")

                    def o_turn(qt):
                        pe.wait_ge(S("o_ready"), qt + 1)
                        for c in range(4):
                            ins = turn(B[6 + qt][:, c * P:c * P + P], oC[:, c * P:c * P + P])
                        ins.then_inc(S("o_turned"), 1)

                    for u in range(4 * NL + 1):
                        if u < 4 * NL:
                            qt, h = u // 4, u % 4
                            for m in range(2):
                                n = 2 * u + m
                                wait(pe, "p1_ready", n - 1)
                                pe.matmul(B[n % 2][:, :], qC[64 * m:64 * m + 64, h, qt * P:qt * P + P],
                                          kC[64 * m:64 * m + 64, h, :], start=True, stop=True).then_inc(S("scores1"), 1)
                        if u:
                            w = u - 1
                            qt, h = w // 4, w % 4
                            pe.wait_ge(S("w_ready1"), w + 1)
                            wait(pe, "wT_ready", w - 1)
                            for t in range(NT):
                                ins = turn(B[2 + w % 2][:, t * P:t * P + P], pC[:, 2 * (w % 2), t * P:t * P + P])
                            ins.then_inc(S("w_turned"), 1)
                            pe.wait_ge(S("wT_ready"), w + 1)
                            ins = product(B[4 + qt][:, h * P:h * P + P],
                                          [(wTC[:, w % 2, t * P:t * P + P], vC[:, t, h * P:h * P + P]) for t in range(NT)])
                            if h == 3:
                                ins.then_inc(S("pv1_done"), 1)
                            if h == 0 and qt:
                                o_turn(qt - 1)
                    o_turn(NL - 1)
                    end_stage(pe, "attn1")
                    for t in range(NT):
                        pe.matmul(B[0][:, t * 16:t * 16 + 8], C["tri_le"], dta[:, t, 0:8], start=True, stop=True)
                        pe.matmul(B[0][:, t * 16 + 8:t * 16 + 16], C["tri_ge"], dta[:, t, 8:16], start=True, stop=True)
                        ins = pe.matmul(B[1][:, t * 16:t * 16 + 16], C["ones"], dta[:, t, :], start=True, stop=True)
                    ins.then_inc(S("acum_mm"), 1)
                    for c in range(NL):
                        for g in range(2):
                            ins = pe.matmul(B[2][:, (2 * c + g) * P:(2 * c + g) * P + P], hT[:, 4 + g, c * P:c * P + P],
                                            hT[:, 6 + g, c * P:c * P + P], start=True, stop=True)
                    ins.then_inc(S("cb_mm"), 1)
                    for t in range(NT):
                        for c in range(4):
                            ins = turn(B[3 + t][:, c * P:c * P + P], hT[:, c, t * P:t * P + P])
                        ins.then_inc(S("ssd_turned"), 1)
                    for t in range(NT):
                        bank = B[7] if t < 2 else B[0]
                        if t == 2:
                            pe.wait_ge(S("acum_ready"), 1)
                        for g in range(2):
                            o = (2 * (t % 2) + g) * P
                            ins = turn(bank[:, o:o + P], hT[:, 4 + g, t * P:t * P + P])
                        if t % 2:
                            ins.then_inc(S("ssd_turned"), 1)
                    pe.wait_ge(S("ssd_moved"), 7)
                    n_state = n_seg = 0
                    for d in range(2):
                        for idx, t in enumerate(chunks(d)):
                            if t < NL:
                                for g in range(2):
                                    n_seg += 1
                                    pe.wait_ge(S("tri_dta"), n_seg)
                                    pe.matmul(B[3 + g][:, :], C["ones"], tri_dta, start=True, stop=True).then_inc(S("seg_mm"), 1)
                                    pe.wait_ge(S("w_ready"), n_seg)
                                    for r in range(4):
                                        h = 4 * g + r
                                        ins = pe.matmul(B[6 + t][:, h * 64:h * 64 + 64], seg[:, r * P:r * P + P],
                                                        xdt[:, h * 64:h * 64 + 64], start=(d == 0 and h == 0),
                                                        stop=(d == 1 and h == 7), skip_group_check=True)
                                    ins.then_inc(S("y_mm"), 1)
                                pe.wait_ge(S("H_ready"), n_state)
                                for g in range(2):
                                    ins = pe.matmul(B[5][:, g * 256:g * 256 + 256], hT[:, 6 + g, t * P:t * P + P],
                                                    Hst[:, g * 256:g * 256 + 256], start=True, stop=True)
                                ins.then_inc(S("inter_mm"), 1)
                            if idx < 3:
                                n_state += 1
                                pe.wait_ge(S("xte_ready"), n_state)
                                for g in range(2):
                                    ins = pe.matmul(B[2][:, g * 256:g * 256 + 256], btok[:, t, g * P:g * P + P],
                                                    xte[:, g * 256:g * 256 + 256], start=True, stop=True)
                                ins.then_inc(S("state_mm"), 1)
                    for c in range(NL):
                        pe.wait_ge(S("ssd_y"), c + 1)
                        for m in range(4):
                            ins = turn(B[3 + c][:, m * P:m * P + P], yacc[:, c, m * P:m * P + P])
                        ins.then_inc(S("ssd_y_turned"), 1)
                    end_stage(pe, "ssd1")
                for h in range(2):
                    W = block_ready(l, 12 + n_in[l] + h)
                    for t in range(nt):
                        ins = product(B[h * nt + t][:, :], [(cat[:, k, t * P:t * P + P], W[:, k, :]) for k in range(KD)])
                        ins.then_inc(S("out"), 1)
                    pe.drain().then_inc(S("stream_free"), 1)
                end_stage(pe, f"out{l}")
                q = 2 * l + 1
                norm(q)
                pe.wait_ge(S("hT_act"), 4 * (nt // 2) + before("hT_act", q))
                pe.wait_ge(S("hT_dve"), 4 * (nt // 2) + before("hT_dve", q))
                for t in range(nt):
                    for half in range(2):
                        for k in range(4):
                            ins = turn(B[2 * t + half][:, k * P:k * P + P], hT[:, 4 * half + k, t * P:t * P + P])
                        ins.then_inc(S("row_turned"), 1)
                end_stage(pe, f"norm2{l}")
                pe.wait_ge(S("ld_router"), 32 + before("ld_router", l))
                for t in range(nt):
                    ins = product(B[0][:, t * NE:t * NE + NE], [(hT[:, k, t * P:t * P + P], router_w[:, k, :]) for k in range(KD)])
                ins.then_inc(S("logits"), 1)
                s = base[l] + 12 + n_in[l] + 2
                pe.wait_ge(S("ld_shared"), 32 + before("ld_shared", l))
                for m in range(2):
                    for up in range(2):
                        c0 = up * DE + m * P
                        ins = product(B[4 + 2 * m + up][:, 0:nt * P],
                                      [(stream[:, s % 2, k, c0:c0 + P], hT[:, k, 0:nt * P]) for k in range(KD)])
                        ins.then_inc(S("shared_gu"), 1)
                pe.drain().then_inc(S("stream_free"), 1)
                pe.wait_ge(S("Msel"), nt + before("Msel", l))
                for t in range(nt):
                    product(B[1][:, t * NE:t * NE + NE],
                            [(C["tri_lt"], Msel[:, t, :])] + [(C["ones"], Msel[:, u, :]) for u in range(t)])
                product(B[2][:, 0:NE], [(C["ones"], Msel[:, t, :]) for t in range(nt)]).then_inc(S("ranks"), 1)
                pe.wait_ge(S("more_col"), 1 + before("more_col", l))
                turn(B[0][0:1, 0:P], s1[:, 0:1]).then_inc(S("more_row"), 1)
                pe.wait_ge(S("ld_sdown"), 16 + before("ld_sdown", l))
                pe.wait_ge(S("act_shared"), 2 + before("act_shared", l))
                for t in range(nt):
                    for h in range(2):
                        n = 2 * t + h
                        wait(pe, "shared_out", n - 3, before("shared_out", l))
                        ins = product(B[4 + n % 4][:, :], [(actS[:, j, t * P:t * P + P], stream[:, 1 - s % 2, 2 * j + h, :]) for j in range(2)])
                        ins.then_inc(S("shared_y"), 1)
                    if t == nt - 1:
                        pe.drain().then_inc(S("stream_free"), 1)
                    pe.wait_ge(S("onehot"), t + 1 + before("onehot", l))
                    for k in range(TOPK):
                        ins = pe.matmul(B[3][:, 0:NCOL], lo_oh[:, k, :], hi_oh[:, k, :],
                                        start=(t == 0 and k == 0), stop=(t == nt - 1 and k == TOPK - 1), skip_group_check=True)
                    ins.then_inc(S("table"), 1)
                end_stage(pe, f"route{l}")

                def turn_x(i, n):
                    e, pair, slot = nth(l, i, n)
                    pe.wait_ge(S(f"xg_ld{slot}"), pair * 16 + 16)
                    for b, moved in ((0, "xgT_act"), (1, "xgT_dve")):
                        wait(pe, moved, e)
                        for k in range(4):
                            ins = turn(B[b][:, k * P:k * P + P], xg[:, slot, 4 * b + k::KD])
                        ins.then_inc(S("x_turned"), 1)

                def gate_up(i, n):
                    e, pair, slot = nth(l, i, n)
                    pe.wait_ge(S(f"gu_ld{slot}"), pair * 32 + 32)
                    pe.wait_ge(S("xgT_act"), e + 1)
                    pe.wait_ge(S("xgT_dve"), e + 1)
                    for w, c0 in ((wg, 0), (wu, DE)):
                        ins = product(B[2 + slot][:, c0:c0 + DE], [(xgT[:, slot, k * P:k * P + P], w[:, slot, k, :]) for k in range(KD)])
                    ins.then_inc(S("gu_done"), 1)

                def turn_act(i, n):
                    e, pair, slot = nth(l, i, n)
                    pe.wait_ge(S("act_ready"), e + 1)
                    for j in range(2):
                        ins = turn(B[4 + slot][:, j * P:j * P + P], act_[:, slot, j::2])
                    ins.then_inc(S("act_turned"), 1)

                def down(i, n):
                    e, pair, slot = nth(l, i, n)
                    pe.wait_ge(S("actT_ready"), e + 1)
                    pe.wait_ge(S(f"down_ld{slot}"), pair * 16 + 16)
                    for h, moved in ((0, "y_act"), (1, "y_dve")):
                        wait(pe, moved, e)
                        product(B[6 + h][:, :], [(actT[:, slot, j * P:j * P + P], wd[:, slot, j, h * 512:h * 512 + 512])
                                                 for j in range(2)]).then_inc(S("y_done"), 1)

                def pair_of(i):
                    for n in range(2):
                        gate_up(i, n)
                        if not (isinstance(i, int) and i == NE // 2 - 1 and n == 1):
                            turn_x(i, n + 1)
                        if not (isinstance(i, int) and i == 0 and n == 0):
                            down(i, n - 1)
                        turn_act(i, n)

                turn_x(0, 0)
                over_pairs(pe, pair_of)
                down(NE // 2 - 1, 1)
                end_stage(pe, f"experts{l}")
                more = pe.value_load(more_i[0:1, 0:1], min_val=0, max_val=OVB)
                with pe.If(more):
                    with pe.Fori(0, OVB) as i:
                        step = S(f"more_step{l}")
                        pe.wait_ge(S(f"more_dma{l}"), i * 32 + 16)
                        for b in range(2):
                            for k in range(4):
                                ins = turn(B[b][:, k * P:k * P + P], xg[:, 0, 4 * b + k::KD])
                        ins.then_inc(step, 1)
                        pe.wait_ge(step, i * MORE_STEPS + 5)
                        pe.wait_ge(S(f"more_w{l}"), i * 48 + 48)
                        for w, c0 in ((wg, 0), (wu, DE)):
                            ins = product(B[2][:, c0:c0 + DE], [(xgT[:, 0, k * P:k * P + P], w[:, 0, k, :]) for k in range(KD)])
                        ins.then_inc(step, 1)
                        pe.wait_ge(step, i * MORE_STEPS + 8)
                        for j in range(2):
                            ins = turn(B[4][:, j * P:j * P + P], act_[:, 0, j::2])
                        ins.then_inc(step, 1)
                        pe.wait_ge(step, i * MORE_STEPS + 10)
                        for h in range(2):
                            ins = product(B[6 + h][:, :], [(actT[:, 0, j * P:j * P + P], wd[:, 0, j, h * 512:h * 512 + 512]) for j in range(2)])
                        ins.then_inc(step, 1)
                end_stage(pe, f"more{l}")
                end_stage(pe, f"combine{l}")
            pe.drain()

        @block.vector
        def _(dve):
            link = linker(dve, "dve_chain")

            def tt(dst, x, y, op, name="dve_chain"):
                link(dve.tensor_tensor(dst, x, y, op), name)

            def ts(dst, x, s1_, s2_, op0, op1=None, name="dve_chain"):
                link(dve.tensor_scalar(dst, x, s1_, s2_, op0, op1) if op1 is not None
                     else dve.tensor_scalar(dst, x, s1_, s2_, op0), name)

            def stt(dst, x, s_, y, op0, op1, name="dve_chain"):
                link(dve.scalar_tensor_tensor(out=dst, in0=x, scalar=s_, in1=y, op0=op0, op1=op1), name)

            def red(dst, x, op, name="dve_chain"):
                link(dve.tensor_reduce(dst, x, AX, op), name)

            def copy(dst, x, name="dve_chain"):
                link(dve.tensor_copy(dst, x), name)

            def mean_square(q, n, width):
                ts(ss[:, 0:n], ss[:, 0:n], 1.0 / width, EPS, ALU.mult, ALU.add, "ms")
                dve.wait_ge(S("rstd"), 1 + before("rstd", q))

            def norm(q, which):
                nt = norm_tiles[q]
                dve.wait_ge(S("ss"), nt + before("ss", q))
                mean_square(q, nt, D)
                for t in range(1, nt, 2):
                    ts(xn[:, t, :], X[:, t, :], rstd[:, t:t + 1], None, ALU.mult, name="xn_dve")
                for k in range(1, KD, 2):
                    dve.wait_ge(S("xT"), k + 1 + before("xT", q))
                    for s in range(nt // 2):
                        ts(hT[:, k, s * H:s * H + H], B[k][:, s * H:s * H + H], mscale[:, which, k, s:s + 1],
                           modT[:, 2 * which, k, s:s + 1], ALU.mult, ALU.add, "hT_dve")

            def conv(u, src, w0, nch, c, name):
                x = src.rearrange("p (s w) -> p s w", s=2)
                u = u.rearrange("p (s w) -> p s w", s=2)
                ts(u, x[:, :, 0:H], VT[:, w0 + c:w0 + c + 1], VT[:, w0 + 4 * nch + c:w0 + 4 * nch + c + 1], ALU.mult, ALU.add)
                for j in range(1, 4):
                    stt(u, x[:, :, j:j + H], VT[:, w0 + j * nch + c:w0 + j * nch + c + 1], u, ALU.mult, ALU.add,
                        name if j == 3 else "dve_chain")

            def rope(x, bank, tmp, name):
                tt(tmp, bank[:, 0:H], C["sin"], ALU.mult)
                tt(x, x, C["cos"], ALU.mult)
                tt(x, x, tmp, ALU.add, name)

            dve.wait_ge(S("ld_small"), 16 * N_SMALL)
            dve.wait_ge(S("v_turned"), 1)
            copy(VT[:], B[7][:, 0:V_ROWS])
            ts(hbr, VT[:, V_BR:V_BR + 8], 0.5, None, ALU.mult)
            ts(hbi, VT[:, V_BI:V_BI + 8], 0.5, None, ALU.mult)
            ts(sink8, sinkb, 1.0 / SCALE, None, ALU.mult)
            ts(subg[:], subg[:], 1.0 - LAM_INIT, None, ALU.mult)
            for l in range(DEPTH):
                nt = NT if l == 0 else NL
                cat = catA if l == 0 else catC
                dve.wait_ge(S("ld_bmod"), 16 + before("ld_bmod", l))
                dve.sem_inc(S("mod_rows"), 2)
                with dve.Fori(0, 6) as i:
                    for j in range(2):
                        dve.wait_ge(S("stream_free"), i * 2 + (base[l] + j + 3))
                        row = modrow[:, bass.ds(i * 1024 + j * 512, 512)]
                        dve.tensor_tensor(row, B[j][0:2, :], row, ALU.add).then_inc(S("mod_rows"), 1)
                dve.wait_ge(S("mod_turned"), 1 + before("mod_turned", l))
                copy(modT[:].rearrange("p v k s -> p (v k s)"), B[2][:, 0:8 * KD], "modT")
                for w in range(2):
                    stt(mscale[:, w], modT[:, 2 * w + 1], 1.0, bc(gvec[:, w, l, :], 2, 2), ALU.add, ALU.mult)
                end_stage(dve, f"mod{l}")
                norm(2 * l, 0)
                end_stage(dve, f"norm1{l}")
                if l == 0:
                    dve.wait_ge(S("pads_zeroed"), 1)
                    for n in range(1, 14, 2):
                        dve.wait_ge(S("proj0"), n + 1)
                        src = B[n % 8][:, :]
                        if n < 8:
                            dst = catA[:, n, :]
                        elif n < 12:
                            dst = xap[:, n - 8, :].rearrange("p (s w) -> p s w", s=2)[:, :, 1:1 + H]
                            src = src.rearrange("p (s w) -> p s w", s=2)
                        else:
                            dst, src = vA, src.rearrange("p (t d) -> p t d", t=NT)
                        copy(dst, src, "proj0_dve")
                    end_stage(dve, "proj0")
                    for m in range(5):
                        dve.wait_ge(S("swapped0"), m + 1)
                        x = catA[:, 4 + m, 0:H] if m < 4 else ktmp[:, 0:H]
                        rope(x, B[m], rec[:, 0, 0:H], "rope0")
                    for c in range(4):
                        conv(uA[:, c, :], xap[:, c, :], V_CONVW, 4, c, "conv0")
                    lam = VT[:, V_LAM:V_LAM + 8]
                    stt(tmpc[:, 0:8], lam, -1.0, lam, ALU.mult, ALU.max, "lam_abs")
                    dve.wait_ge(S("lam_ln"), 1)
                    ts(tmpc[:, 24:32], lam, -1.0, 0.0, ALU.mult, ALU.max)
                    tt(tmpc[:, 24:32], tmpc[:, 24:32], tmpc[:, 16:24], ALU.add)
                    ts(lsc, tmpc[:, 24:32], -LRU_C / 2, None, ALU.mult)
                    ts(lnsc, tmpc[:, 24:32], LRU_C / 2, None, ALU.mult, name="lsc_ready")
                    for d in range(2):
                        for c in range(4):
                            n = d * 4 + c
                            dve.wait_ge(S("lru_th"), n + 1)
                            ts(ktmp, m4[:, c, :], 1.0, None, ALU.add)
                            link(dve.reciprocal(ktmp, ktmp))
                            tt(m4[:, c, :], m4[:, c, :], ktmp, ALU.mult, "lru_m")
                            dve.wait_ge(S("lru_i"), n + 1)
                            stt(z4[:, c, :], z4[:, c, :], 1.0, uA[:, c, :], ALU.add, ALU.mult)
                        for c in range(4):
                            n = d * 4 + c
                            dve.wait_ge(S("lru_sq"), n + 1)
                            dve.wait_ge(S("lru_a"), n + 1)
                            tt(z4[:, c, :], z4[:, c, :], m4[:, c, :], ALU.mult)
                            if d == 0:
                                link(dve.tensor_tensor_scan(rec[:, c, H:T], a4[:, c, H:T], z4[:, c, H:T], 0.0, ALU.mult, ALU.add))
                                link(dve.tensor_tensor_scan(rec[:, c, 0:H], a4[:, c, 0:H], z4[:, c, 0:H], rec[:, c, T - 1:T],
                                                            ALU.mult, ALU.add), "scan_done")
                            else:
                                link(dve.tensor_tensor_scan(m4[:, c, ::-1], a4[:, c, ::-1], z4[:, c, ::-1], 0.0, ALU.mult, ALU.add))
                                tt(rec[:, c, :], rec[:, c, :], m4[:, c, :], ALU.add)
                                dve.wait_ge(S("gelu"), 4)
                                tt(catA[:, c, :], catA[:, c, :], rec[:, c, :], ALU.mult)
                    end_stage(dve, "lru0")
                    for n in range(8 * NT + 1):
                        if n < 8 * NT:
                            nk = T if n < 8 * NL else CTX
                            dve.wait_ge(S("scores0"), n + 1)
                            red(tmpc[:, 32:33], B[n % 2][:, 0:nk], ALU.max)
                            ts(nmx[:, n:n + 1], tmpc[:, 32:33], sink8[:, n % 8:n % 8 + 1], -SCALE, ALU.max, ALU.mult, "nmax0")
                        if n:
                            m = n - 1
                            nk = T if m < 8 * NL else CTX
                            dve.wait_ge(S("p_turned"), m + 1)
                            copy(pTA[:, m % 2, 0:nk], B[2 + m % 2][:, 0:nk], "pT_ready")
                            if m % 8 == 7:
                                qt = m // 8
                                tt(tmpc[:, 0:8], nmx[:, qt * 8:qt * 8 + 8], sinkb, ALU.add, "sink_in")
                                dve.wait_ge(S("sink_exp"), qt + 1)
                                tt(tmpc[:, 16:24], tmpc[:, 8:16], rsum[:, qt * 8:qt * 8 + 8], ALU.add)
                                link(dve.reciprocal(tmpc[:, 24:32], tmpc[:, 16:24]))
                                dve.wait_ge(S("pv_done"), qt + 1)
                                wait(dve, "att_turned", qt)
                                tt(attA.rearrange("p (h d) -> p h d", h=8), B[4 + qt % 2][:, :].rearrange("p (h d) -> p h d", h=8),
                                   bc(tmpc[:, 24:32], 2, 64), ALU.mult, "att_ready")
                    dve.wait_ge(S("att_turned"), NT)
                    end_stage(dve, "attn0")
                else:
                    dve.wait_ge(S("pads_zeroed"), 2)
                    for n in range(1, len(proj1), 2):
                        dve.wait_ge(S("proj1"), n + 1)
                        dst, src = proj1_move(n)
                        copy(dst, src, "proj1_dve")
                    end_stage(dve, "proj1")
                    tt(dt_[:], dtraw, bc(dtb, 1, NT), ALU.add)
                    stt(dta[:], dt_[:], -1.0, dt_[:], ALU.mult, ALU.max)
                    for i in range(2):
                        tt(tmpc[:, 0:64], lamv[:, 128 * i:128 * i + 64], lamv[:, 128 * i + 64:128 * i + 128], ALU.mult)
                        red(lamc[:, i:i + 1], tmpc[:, 0:64], ALU.add, "dve_chain" if i == 0 else "dt_in")
                    for c in range(8):
                        conv(hT[:, c, :], xbc[:, c, :], V_DCONVW, 8, c, "conv1")
                    for m in range(8):
                        dve.wait_ge(S("swapped1"), m + 1)
                        rope(qC[:, m, :] if m < 4 else kC[:, m - 4, 0:H], B[m], ropeC, "rope1")
                    dve.wait_ge(S("dt_ln"), 1)
                    stt(dt_[:], dt_[:], 0.0, dta[:], ALU.max, ALU.add)
                    stt(dta[:], dt_[:], -1.0, bc(alog, 1, NT), ALU.mult, ALU.mult)
                    tt(lamc[:, 2:3], lamc[:, 1:2], lamc[:, 0:1], ALU.subtract)
                    ts(lamc[:, 2:3], lamc[:, 2:3], -LAM_INIT, None, ALU.add)
                    end_stage(dve, "conv1")

                    def weights(u):
                        dve.wait_ge(S("p1_ready"), 2 * u + 2)
                        link(dve.reciprocal(tmpc[:, 0:2], rsum[:, 2 * u:2 * u + 2]))
                        tt(tmpc[:, 2:3], tmpc[:, 1:2], lamc[:, 2:3], ALU.mult)
                        p0, p1 = pC[:, 2 * (u % 2), :], pC[:, 2 * (u % 2) + 1, :]
                        ts(p0, p0, tmpc[:, 0:1], None, ALU.mult)
                        stt(p0, p1, tmpc[:, 2:3], p0, ALU.mult, ALU.add, "w_ready1")

                    for u in range(4 * NL + 1):
                        if u < 4 * NL:
                            for m in range(2):
                                n = 2 * u + m
                                dve.wait_ge(S("scores1"), n + 1)
                                red(tmpc[:, 4:5], B[n % 2][:, :], ALU.max)
                                ts(nmx[:, n:n + 1], tmpc[:, 4:5], -SCALE, None, ALU.mult, name="nmax1")
                        if u:
                            weights(u - 1)
                            if u % 4 == 0:
                                qt = u // 4 - 1
                                dve.wait_ge(S("pv1_done"), qt + 1)
                                wait(dve, "o_turned", qt)
                                copy(oC, B[4 + qt][:, :])
                                tt(sqC, oC, oC, ALU.mult)
                                red(ss, sqC.rearrange("p (h e) -> p h e", h=4), ALU.add)
                                mean_square(f"d{qt}", 4, P)
                                o3 = oC.rearrange("p (h e) -> p h e", h=4)
                                tt(o3, o3, bc(rstd, 2, P), ALU.mult)
                                tt(o3, o3, bc(subg[:], 1, 4), ALU.mult, "o_ready")
                                dve.wait_ge(S("o_turned"), qt + 1) if qt == NL - 1 else None
                    for qt in range(NL):
                        copy(catC[:, 0:4, qt * P:qt * P + P], B[6 + qt][:, :].rearrange("p (c q) -> p c q", c=4))
                    end_stage(dve, "attn1")
                    flat = "p t h -> p (t h)"
                    dve.wait_ge(S("acum_mm"), 1)
                    copy(acum[:].rearrange(flat), B[0][:, 0:NT * 16])
                    ts(nac_, acum[:].rearrange(flat), -1.0, None, ALU.mult)
                    copy(etot[:].rearrange(flat), B[1][:, 0:NT * 16])
                    tt(tend[:], etot[:], acum[:], ALU.subtract, "acum_ready")
                    dve.wait_ge(S("cb_mm"), 1)
                    copy(cbT.rearrange("p a b -> p (a b)"), B[2][:, :], "ssd_moved")
                    for t in range(NT):
                        dve.wait_ge(S("ssd_turned"), t + 1)
                        copy(xtok[:, t, :], B[3 + t][:, :], "ssd_moved")
                    for i in range(2):
                        dve.wait_ge(S("ssd_turned"), NT + i + 1)
                        copy(btok[:, 2 * i:2 * i + 2, :].rearrange("p a b -> p (a b)"), (B[7] if i == 0 else B[0])[:, :], "ssd_moved")
                    dve.wait_ge(S("acum_exp"), 1)
                    tt(tend[:], tend[:], dt_[:], ALU.mult)
                    by_head = "p (h d) -> p h d"
                    for c in range(NL):
                        tt(yacc[:, c, :].rearrange(by_head, h=8), xtok[:, c, :].rearrange(by_head, h=8), bc(dskip, 2, 64), ALU.mult)
                    n_seg = n_state = n_inter = 0
                    for d in range(2):
                        hd = slice(8 * d, 8 * d + 8)
                        tri, mask = (C["tri_le"], C["mask_lo"]) if d == 0 else (C["tri_ge"], C["mask_hi"])
                        for idx, t in enumerate(chunks(d)):
                            x3 = xtok[:, t, :].rearrange(by_head, h=8)
                            if t < NL:
                                wait(dve, "y_mm", n_seg)
                                tt(xdt.rearrange(by_head, h=8), x3, bc(dt_[:, t, hd], 2, 64), ALU.mult)
                                for g in range(2):
                                    h0 = 8 * d + 4 * g
                                    tt(tri_dta.rearrange("p (r q) -> p r q", r=4), bc(tri, 1, 4), bc(dta[:, t, h0:h0 + 4], 2, P),
                                       ALU.mult, "tri_dta")
                                    dve.wait_ge(S("seg_mm"), n_seg + 1)
                                    wait(dve, "y_mm", n_seg)
                                    for r in range(4):
                                        col = t * 16 + h0 + r
                                        stt(seg[:, r * P:r * P + P], B[3 + g][:, r * P:r * P + P], nac_[:, col:col + 1], mask,
                                            ALU.add, ALU.add, "seg_ready" if r == 3 else "dve_chain")
                                    dve.wait_ge(S("seg_exp"), n_seg + 1)
                                    s3 = seg.rearrange("p (r q) -> p r q", r=4)
                                    tt(s3, s3, bc(cbT[:, 2 * t + g, :], 1, 4), ALU.mult, "w_ready")
                                    n_seg += 1
                                n_inter += 1
                                dve.wait_ge(S("inter_mm"), n_inter)
                                tt(ytmp.rearrange(by_head, h=8), B[5][:, :].rearrange(by_head, h=8), bc(eac[:, t, hd], 2, 64), ALU.mult)
                                tt(yacc[:, t, :], yacc[:, t, :], ytmp, ALU.add)
                            if idx < 3:
                                tt(xte.rearrange(by_head, h=8), x3, bc(tend[:, t, hd], 2, 64), ALU.mult, "xte_ready")
                                n_state += 1
                                dve.wait_ge(S("state_mm"), n_state)
                                if idx == 0:
                                    copy(Hst, B[2][:, :], "H_ready")
                                else:
                                    tt(Hst.rearrange(by_head, h=8), Hst.rearrange(by_head, h=8), bc(etot[:, t, hd], 2, 64), ALU.mult)
                                    tt(Hst, Hst, B[2][:, :], ALU.add, "H_ready")
                    dve.wait_ge(S("y_mm"), n_seg)
                    for c in range(NL):
                        y = yacc[:, c, :]
                        tt(y, y, B[6 + c][:, :], ALU.add)
                        tt(y, y, zC[:, c, :], ALU.mult)
                        tt(ytmp, y, y, ALU.mult)
                        red(ss[:, 0:2], ytmp.rearrange("p (g e) -> p g e", g=2), ALU.add)
                        mean_square(f"s{c}", 2, 256)
                        y2 = y.rearrange("p (g e) -> p g e", g=2)
                        tt(y2, y2, bc(rstd[:, 0:2], 2, 256), ALU.mult)
                        tt(y, y, normg[:], ALU.mult, "ssd_y")
                    for c in range(NL):
                        dve.wait_ge(S("ssd_y_turned"), c + 1)
                        copy(catC[:, 4:8, c * P:c * P + P], B[3 + c][:, :].rearrange("p (m q) -> p m q", m=4))
                    end_stage(dve, "ssd1")
                outtmp = hT[:, 0, :]
                for h in range(2):
                    for t in range(nt):
                        n = h * nt + t
                        dve.wait_ge(S("out"), n + 1 + before("out", l))
                        tt(outtmp, B[n][:, :], G[:, 0, t // 2, h * 512:h * 512 + 512], ALU.mult)
                        xs = X[:, t, h * 512:h * 512 + 512]
                        tt(xs, xs, outtmp, ALU.add)
                end_stage(dve, f"out{l}")
                norm(2 * l + 1, 1)
                for t in range(nt):
                    dve.wait_ge(S("row_turned"), 2 * t + 2 + before("row_turned", l))
                    copy(row_half(t, 1), B[2 * t + 1][:, :].rearrange("q (k p) -> q k p", k=4), "hrow_dve")
                end_stage(dve, f"norm2{l}")

                dve.wait_ge(S("ld_router"), 32 + before("ld_router", l))
                dve.wait_ge(S("scores"), 1 + before("scores", l))
                ohk = "p (k e) -> p k e"
                for t in range(nt):
                    tt(selv, scores[:, t, :], router_b[:], ALU.add)
                    for g in range(NG):
                        link(dve.max(srt[:, g, :], selv[:, 8 * g:8 * g + 8]), wait=(g == NG - 1))
                    tt(gsc, srt[:, :, 0], srt[:, :, 1], ALU.add)
                    link(dve.max(gtop, gsc))
                    link(dve.max_index(i8, gtop, gsc))
                    copy(gidx, i8)
                    tt(goh, bc(C["iota"][:, 0:NG], 1, TOPG), bc(gidx[:, 0:TOPG], 2, NG), ALU.is_equal)
                    red(gmask, goh.rearrange("p a g -> p g a"), ALU.max)
                    s3 = selv.rearrange("p (g e) -> p g e", g=NG)
                    tt(s3, s3, bc(gmask, 2, 8), ALU.mult)
                    ts(gmask, gmask, 1.0, -NEG, ALU.subtract, ALU.mult)
                    tt(s3, s3, bc(gmask, 2, 8), ALU.add)
                    link(dve.max(top8, selv))
                    link(dve.max_index(i8, top8, selv))
                    copy(idx8, i8)
                    o3 = oh[:, t, :].rearrange(ohk, k=TOPK)
                    tt(o3, bc(C["iota"][:, 0:NE], 1, TOPK), bc(idx8, 2, NE), ALU.is_equal)
                    red(Msel[:, t, :], oh[:, t, :].rearrange("p (k e) -> p e k", k=TOPK), ALU.add, "Msel")
                    tt(ohtmp.rearrange(ohk, k=TOPK), o3, bc(scores[:, t, :], 1, TOPK), ALU.mult)
                    red(gates[:, t, :], ohtmp.rearrange(ohk, k=TOPK), ALU.add)
                    red(c8[:, 0:1], gates[:, t, :], ALU.add)
                    link(dve.reciprocal(c8[:, 1:2], c8[:, 0:1]))
                    ts(gates[:, t, :], gates[:, t, :], c8[:, 1:2], SCALED, ALU.mult, ALU.mult)
                for m in range(2):
                    dve.wait_ge(S("shared_silu"), m + 1 + before("shared_silu", l))
                    dve.wait_ge(S("shared_gu"), 2 * m + 2 + before("shared_gu", l))
                    tt(actS[:, m, 0:nt * P], sS[:, m, 0:nt * P], B[5 + 2 * m][:, 0:nt * P], ALU.mult, "act_shared")
                dve.wait_ge(S("ranks"), 1 + before("ranks", l))
                copy(rank[:, 0:nt, :].rearrange("p t e -> p (t e)"), B[1][:, 0:nt * NE])
                copy(cnt, B[2][:, 0:NE])
                ts(t64a, cnt, 128.0, None, ALU.is_gt)
                stt(t64a, cnt, 256.0, t64a, ALU.is_gt, ALU.add)
                stt(t64a, cnt, 384.0, t64a, ALU.is_gt, ALU.add)
                link(dve.tensor_tensor_scan(ends, C["ones"][:, 0:NE], t64a, 0.0, ALU.mult, ALU.add))
                tt(v1, ends, t64a, ALU.subtract)
                tt(v1, v1, C["iota"][:, 0:NE], ALU.subtract)
                ts(v1, v1, float(NE - 1), None, ALU.add)
                copy(more_i[:], ends[:, NE - 1:NE])
                ts(t64b, ends, C["pcol"], None, ALU.is_le)
                red(s1[:, 1:2], t64b, ALU.add)
                ts(s1[:, 0:1], s1[:, 1:2], float(NE - 1), None, ALU.min, name="more_col")
                dve.wait_ge(S("more_row"), 1 + before("more_row", l))
                copy(moree_i[:], B[0][0:1, 0:P])
                for t in range(nt):
                    o3 = oh[:, t, :].rearrange(ohk, k=TOPK)
                    m3 = ohtmp.rearrange(ohk, k=TOPK)
                    tt(m3, o3, bc(rank[:, t, :], 1, TOPK), ALU.mult)
                    red(r8, m3, ALU.add)
                    tt(m3, o3, bc(v1, 1, TOPK), ALU.mult)
                    red(q8, m3, ALU.add)
                    tt(m3, o3, bc(C["iota"][:, 0:NE], 1, TOPK), ALU.mult)
                    red(idx8, m3, ALU.add)
                    ts(b8, r8, 128.0, None, ALU.is_ge)
                    copy(c8, b8)
                    stt(b8, r8, 256.0, b8, ALU.is_ge, ALU.add)
                    stt(b8, r8, 384.0, b8, ALU.is_ge, ALU.add)
                    tt(q8, q8, c8, ALU.mult)
                    tt(q8, q8, b8, ALU.add)
                    tt(q8, q8, idx8, ALU.add)
                    stt(r8, b8, -128.0, r8, ALU.mult, ALU.add)
                    wait(dve, "table", t, before("table", l))
                    tt(lo_oh, bc(C["iota"], 1, TOPK), bc(r8, 2, P), ALU.is_equal)
                    tt(hi_oh, bc(C["iota"][:, 0:NCOL], 1, TOPK), bc(q8, 2, NCOL), ALU.is_equal)
                    tt(hi_oh, hi_oh, bc(C["rowid"][:, t * TOPK:(t + 1) * TOPK], 2, NCOL), ALU.mult, "onehot")
                    for h in range(2):
                        n = 2 * t + h
                        dve.wait_ge(S("shared_y"), n + 1 + before("shared_y", l))
                        tt(ohtmp, B[4 + n % 4][:, :], G[:, 1, t // 2, h * 512:h * 512 + 512], ALU.mult, "shared_out")
                        xs = X[:, t, h * 512:h * 512 + 512]
                        tt(xs, xs, ohtmp, ALU.add)
                dve.wait_ge(S("table"), nt + before("table", l))
                copy(tabf, B[3][:, 0:NCOL])
                ts(tab2, tabf, 0.5, BIG, ALU.is_lt, ALU.mult)
                stt(tabf, tabf, -1.0, tab2, ALU.add, ALU.add)
                copy(rows_i[:], tabf)
                ts(toks_i[:], rows_i[:], 3, None, ALU.logical_shift_right)
                end_stage(dve, f"route{l}")

                def x_evac(i, n):
                    e, pair, slot = nth(l, i, n)
                    dve.wait_ge(S("x_turned"), e * 2 + 2)
                    dve.tensor_copy(xgT[:, slot, 512:1024], B[1][:, :]).then_inc(S("xgT_dve"), 1)

                def y_evac(i, n):
                    e, pair, slot = nth(l, i, n)
                    dve.wait_ge(S("y_done"), e * 2 + 2)
                    wait(dve, f"y_stored{slot}", pair * 16)
                    dve.tensor_copy(ysb[:, slot, 512:1024], B[7][:, :]).then_inc(S("y_dve"), 1)

                def pair_of(i):
                    for n in range(2):
                        e, pair, slot = nth(l, i, n)
                        dve.wait_ge(S("sg_ready"), e + 1)
                        dve.tensor_tensor(act_[:, slot, :], sg[:, slot, :], B[2 + slot][:, DE:2 * DE], ALU.mult).then_inc(S("act_ready"), 1)
                        if not (isinstance(i, int) and i == NE // 2 - 1 and n == 1):
                            x_evac(i, n + 1)
                        if not (isinstance(i, int) and i == 0 and n == 0):
                            y_evac(i, n - 1)
                        dve.wait_ge(S("act_turned"), e + 1)
                        dve.tensor_copy(actT[:, slot, :], B[4 + slot][:, 0:2 * P]).then_inc(S("actT_ready"), 1)

                x_evac(0, 0)
                over_pairs(dve, pair_of)
                y_evac(NE // 2 - 1, 1)
                end_stage(dve, f"experts{l}")
                more = dve.value_load(more_i[0:1, 0:1], min_val=0, max_val=OVB)
                with dve.If(more):
                    with dve.Fori(0, OVB) as i:
                        step = S(f"more_step{l}")
                        dve.wait_ge(step, i * MORE_STEPS + 3)
                        for b in range(2):
                            dve.tensor_copy(xgT[:, 0, b * 512:b * 512 + 512], B[b][:, :]).then_inc(step, 1)
                        dve.wait_ge(step, i * MORE_STEPS + 7)
                        dve.tensor_tensor(act_[:, 0, :], sg[:, 0, :], B[2][:, DE:2 * DE], ALU.mult).then_inc(step, 1)
                        dve.wait_ge(step, i * MORE_STEPS + 9)
                        dve.tensor_copy(actT[:, 0, :], B[4][:, 0:2 * P]).then_inc(step, 1)
                        dve.wait_ge(step, i * MORE_STEPS + 11)
                        for b in range(2):
                            dve.tensor_copy(ysb[:, 0, b * 512:b * 512 + 512], B[6 + b][:, :]).then_inc(step, 1)
                end_stage(dve, f"more{l}")
                for t in range(nt):
                    for q in range(2):
                        dve.wait_ge(S(f"ych_ld{q}"), 16 * (t + 1) + 16 * NT * l)
                        for k in range(4):
                            y, w = ych[:, q, k * D:(k + 1) * D], gates[:, t, 4 * q + k:4 * q + k + 1]
                            name = "ych_used" if k == 3 else "dve_chain"
                            if q == 0 and k == 0:
                                ts(acc, y, w, None, ALU.mult)
                            else:
                                stt(acc, y, w, acc, ALU.mult, ALU.add, name)
                    tt(acc, acc, G[:, 1, t // 2, :], ALU.mult)
                    tt(X[:, t, :], X[:, t, :], acc, ALU.add)
                end_stage(dve, f"combine{l}")
            dve.wait_ge(S("ss"), NL + before("ss", 4))
            mean_square(4, NL, D)
            dve.wait_ge(S("ld_gfin"), 16)
            for t in range(NL):
                stt(xn[:, t, :], X[:, t, :], rstd[:, t:t + 1], G[:, 0, 0, :], ALU.mult, ALU.mult, "out_ready")
            dve.drain()


_INS = ["x", "c", "ctx", "c_ctx", "w_mod", "b_mod", "g_mix", "g_ffn", "g_final", "ab_w_in", "ab_w_out", "ab_conv_w",
        "ab_conv_b", "ab_w_r", "ab_b_r", "ab_w_i", "ab_b_i", "ab_lam", "ab_sink", "cd_w_in", "cd_w_out", "cd_lam",
        "cd_subln_g", "cd_conv_w", "cd_conv_b", "cd_dt_bias", "cd_a_log", "cd_d_skip", "cd_norm_g", "w_router",
        "b_router", "w_e_gate", "w_e_up", "w_e_down", "ws_gate", "ws_up", "ws_down"]


def kernel(**inputs):
    import concourse.bacc as bacc
    from concourse.bass_utils import run_bass_kernel_spmd

    nc = bacc.Bacc("TRN2", target_bir_lowering=False, num_devices=1)
    arrays, aps = {}, {}
    for name in _INS:
        arrays[f"in_{name}"] = np.ascontiguousarray(inputs[name])
    arrays["in_con"] = const_table()
    arrays["in_sel"] = select_rows()
    for name, v in arrays.items():
        aps[name[3:]] = nc.dram_tensor(name, v.shape, mybir.dt.from_np(v.dtype), kind="ExternalInput").ap()
    out = nc.dram_tensor("out_0", (1, SEQ, D), F32, kind="ExternalOutput").ap()
    build(nc, aps, out)
    r = run_bass_kernel_spmd(nc, [arrays], core_ids=[0])
    return r.results[0]["out_0"]
```

```python
from contextlib import ExitStack
import math

import numpy as np

import concourse.bass as bass
from concourse import mybir

F32 = mybir.dt.float32
I32 = mybir.dt.int32
U32 = mybir.dt.uint32
ALU = mybir.AluOpType
ACT = mybir.ActivationFunctionType
AX = mybir.AxisListType.X

P = 128
D = 1024
KD = D // P
SEQ = 256
CTX = 256
T = SEQ + CTX
NT = T // P
NL = SEQ // P
DEPTH = 2
EPS = 1e-6
NE = 64
NG = 8
TOPG = 4
TOPK = 8
DE = 256
SCALED = 2.5
OVB = 32
MORE_STEPS = 13
NCOL = NE + OVB
BIG = float(1 << 20)
NEG = -1e30
SCALE = 0.125
LAM_INIT = 0.8 - 0.6 * math.exp(-0.3)
GRID_W = 64
H = SEQ
PADW = SEQ + 3
LRU_C = 8.0


def chunks(d):
    return (2, 3, 0, 1) if d == 0 else (3, 2, 1, 0)


STAGES = []
for _l in range(DEPTH):
    STAGES += [f"{n}{_l}" for n in (
        ("mod", "norm1", "proj", "lru", "attn", "out") if _l == 0 else
        ("mod", "norm1", "proj", "conv", "attn", "ssd", "out"))]
    STAGES += [f"{n}{_l}" for n in ("norm2", "route", "experts", "more", "combine")]

CONSTS = ["ident", "swap", "cos", "sin", "tri_le", "tri_ge", "tri_lt", "ones", "mask_lo", "mask_hi",
          "iota", "rowid", "pcol"]
CWID = dict(cos=SEQ, sin=SEQ, rowid=NT * TOPK, pcol=1)


def const_columns():
    at, n = {}, 0
    for c in CONSTS:
        w = CWID.get(c, P)
        at[c] = (n, n + w)
        n += w
    return at, n


def const_table():
    at, n = const_columns()
    t = np.zeros((P, n), np.float32)

    def put(name, a):
        t[:, at[name][0]:at[name][1]] = a

    r = np.arange(P)
    put("ident", np.eye(P))
    put("swap", np.eye(P)[(r // 64) * 64 + (r % 64 + 32) % 64])
    half = 16
    inv = (np.float32(10000.0) ** (-np.arange(half, dtype=np.float32) / np.float32(half))).astype(np.float32)
    tok = np.arange(SEQ)
    row, col = (tok // GRID_W).astype(np.float32), (tok % GRID_W).astype(np.float32)
    ang = np.concatenate([row[:, None] * inv, col[:, None] * inv], axis=-1).astype(np.float32)
    put("cos", np.cos(ang).T[r % 32])
    put("sin", np.sin(ang).T[r % 32] * np.where(r % 64 < 32, -1.0, 1.0)[:, None])
    a, b = r[:, None], r[None, :]
    put("tri_le", a <= b)
    put("tri_ge", a >= b)
    put("tri_lt", a < b)
    put("ones", 1.0)
    put("mask_lo", np.where(b < a, NEG, 0.0))
    put("mask_hi", np.where(b > a, NEG, 0.0))
    put("iota", np.broadcast_to(b, (P, P)))
    k = np.arange(NT * TOPK)[None, :]
    put("rowid", ((k // TOPK) * P + a) * TOPK + k % TOPK + 1)
    put("pcol", a)
    return t


def select_rows():
    s = np.zeros((2, 2, P), np.float32)
    s[0, 0] = 1.0
    s[1, 1] = 1.0
    return s.reshape(2, 2 * P)


V_CONVW, V_CONVB, V_BR, V_BI, V_LAM, V_DCONVW, V_DCONVB = 0, 16, 20, 28, 36, 44, 76
V_ROWS = 84
N_SMALL = 4 + 2 * DEPTH + 7 + 6


def build(nc, a, out):
    at, ncon = const_columns()
    ctx = ExitStack()
    with ctx:
        def sb(name, shape, dt=F32):
            return ctx.enter_context(nc.sbuf_tensor(name, shape, dt))

        sems = {}

        def S(name):
            if name not in sems:
                sems[name] = ctx.enter_context(nc.semaphore(name))
            return sems[name]

        X = sb("X", [P, NT, D])
        hT = sb("hT", [P, KD, T])
        G = sb("G", [P, 2, 2, D])
        stream = sb("stream", [P, 2, KD, 512])
        wg = sb("wg", [P, 2, KD, DE])
        wu = sb("wu", [P, 2, KD, DE])
        wd = sb("wd", [P, 2, 2, D])
        con = sb("con", [P, ncon])
        C = {n: con[:, at[n][0]:at[n][1]] for n in CONSTS}
        sel = sb("sel", [2, 2 * P])
        VT = sb("VT", [P, V_ROWS])
        craw = sb("craw", [P, 2, KD])
        csT = sb("csT", [P, KD, 2])
        gvec = sb("gvec", [P, 2, DEPTH, KD])
        modT = sb("modT", [P, 4, KD, 2])
        mscale = sb("mscale", [P, 2, KD, 2])
        half_exp = sb("half_exp", [P, 8])
        router_w = sb("router_w", [P, KD, NE])
        router_b = sb("router_b", [P, NE])
        gates = sb("gates", [P, NT, TOPK])
        small = sb("small", [P, 320])
        rows_i = sb("rows_i", [P, NCOL], I32)
        toks_i = sb("toks_i", [P, NCOL], I32)
        gat_i = sb("gat_i", [P, 4], I32)
        sca_i = sb("sca_i", [P, 4], I32)
        more_i = sb("more_i", [P, 1], I32)
        moree_i = sb("moree_i", [1, P], I32)
        RW = 14336
        R = sb("R", [P, RW])
        B = [ctx.enter_context(nc.psum_tensor(f"B{i}", [P, 512], F32)) for i in range(8)]

        h_rows = nc.dram_tensor("h_rows", (T, D), F32, kind="Internal").ap()
        mod_dram = nc.dram_tensor("mod_dram", (2, 6 * D), F32, kind="Internal").ap()
        y_rows = nc.dram_tensor("y_rows", (T * TOPK, D), F32, kind="Internal").ap()

        def rv(off, *dims):
            n = math.prod(dims)
            assert off + n <= RW
            v = R[:, off:off + n]
            if len(dims) == 2:
                return v.rearrange("p (a b) -> p a b", b=dims[1])
            if len(dims) == 3:
                return v.rearrange("p (a b c) -> p a b c", b=dims[1], c=dims[2])
            return v

        def bc(ap, axis, n):
            v = ap.unsqueeze(axis)
            shape = list(v.shape)
            shape[axis] = n
            return v.to_broadcast(shape)

        modrow = R[0:2, 8192:8192 + 6 * D]
        modbias = R[0:2, 0:6 * D]
        xn = rv(0, NT, D)
        vraw = R[0:V_ROWS, 0:P]
        catA = rv(0, 8, T)
        bdiag = rv(4096, 16, P)
        kd = rv(6144, 2, T)
        ktmp = rv(7168, T)
        vA = rv(7680, NT, P)
        xap = rv(8192, 4, 2 * PADW)
        uA = hT[:, 0:4, :]
        rec = hT[:, 4:8, :]
        a4, m4, z4 = rv(8192, 4, T), rv(10240, 4, T), rv(12288, 4, T)
        pA, pTA, attA = rv(8192, 2, T), rv(9216, 2, T), rv(10240, 512)
        catC = rv(0, 8, SEQ)
        qC = rv(2048, 4, SEQ)
        zC = rv(3072, NL, 512)
        kC = rv(4096, 4, T)
        vC = rv(6144, NT, 512)
        xbc = rv(8192, 8, 2 * PADW)
        ropeC = rv(12336, SEQ)
        dtraw = rv(12592, NT, 16)
        dtw = rv(12656, KD, 16)
        pC = rv(8192, 4, T)
        wTC = rv(10240, 2, T)
        oC = rv(11264, 512)
        sqC = rv(11776, 512)
        xtok = rv(8192, NT, 512)
        btok = rv(10240, NT, 256)
        cbT = rv(11264, 4, P)
        seg = rv(11776, 512)
        tri_dta = rv(4096, 512)
        xdt = rv(4608, 512)
        xte = rv(5120, 512)
        Hst = rv(5632, 512)
        yacc = rv(6144, NL, 512)
        ytmp = rv(7168, 512)
        oh = rv(4096, NT, TOPK * NE)
        lo_oh = rv(6144, TOPK, P)
        hi_oh = rv(7168, TOPK, NCOL)
        ohtmp = rv(7936, 512)
        actS = rv(8448, 2, T)
        sS = rv(9472, 2, T)
        scores = rv(10496, NT, NE)
        Msel = rv(10752, NT, NE)
        rank = rv(11008, NT, NE)
        cnt = rv(11264, NE)
        tabf = rv(11328, NCOL)
        tab2 = rv(11424, NCOL)
        selv = rv(11520, NE)
        t64a = rv(11584, NE)
        t64b = rv(11648, NE)
        srt = rv(11712, NG, 8)
        ends = rv(11776, NE)
        v1 = rv(11840, NE)
        gsc = rv(11904, 8)
        gtop = rv(11912, 8)
        gidx = rv(11920, 8)
        goh = rv(11928, TOPG, NG)
        gmask = rv(11960, 8)
        top8 = rv(11968, 8)
        idx8 = rv(11976, 8)
        r8 = rv(11984, 8)
        q8 = rv(11992, 8)
        b8 = rv(12000, 8)
        c8 = rv(12008, 8)
        i8 = rv(12016, 8).bitcast(U32)
        s1 = rv(12024, 8)
        xg = rv(0, 4, D)
        xgT = rv(4096, 2, D)
        ysb = rv(6144, 4, D)
        sg = rv(10240, 2, DE)
        act_ = rv(10752, 2, DE)
        actT = rv(11264, 2, 2 * P)
        ych = rv(0, 2, 4 * D)
        acc = rv(8192, D)

        ss = small[:, 0:4]
        rstd = small[:, 4:8]
        nmx = small[:, 8:40]
        rsum = small[:, 40:72]
        sinkb = small[:, 72:80]
        sink8 = small[:, 80:88]
        lsc = small[:, 88:96]
        lnsc = small[:, 96:104]
        hbr = small[:, 104:112]
        hbi = small[:, 112:120]
        dskip = small[:, 120:128]
        alog = small[:, 128:144]
        dtb = small[:, 144:160]
        lamc = small[:, 160:168]
        tmpc = small[:, 168:232]
        nac_ = small[:, 232:296]
        ovf = small[:, 296:300]
        dt_ = sb("dt_", [P, NT, 16])
        dta = sb("dta", [P, NT, 16])
        acum = sb("acum", [P, NT, 16])
        eac = sb("eac", [P, NT, 16])
        tend = sb("tend", [P, NT, 16])
        etot = sb("etot", [P, NT, 16])
        subg = sb("subg", [P, P])
        normg = sb("normg", [P, 512])
        mod1_stage = normg[0:2, :]
        lamv = sb("lamv", [P, 256])

        stage_no = {s: i for i, s in enumerate(STAGES)}

        def end_stage(eng, name):
            eng.drain().then_inc(S("stage_ended"), 1)
            eng.wait_ge(S("stage_ended"), 4 * (stage_no[name] + 1))

        def after_stage(eng, name):
            eng.wait_ge(S("stage_ended"), 4 * (stage_no[name] + 1))

        def linker(eng, own):
            count = {}

            def link(ins, name=own, wait=True):
                ins.then_inc(S(name), 1)
                count[name] = count.get(name, 0) + 1
                if wait:
                    eng.wait_ge(S(name), count[name])
                return count[name]
            return link

        def wait(eng, name, value, earlier=0):
            if not (isinstance(value, int) and value <= 0):
                eng.wait_ge(S(name), value + earlier)

        def nth(l, i, n):
            e = i * 4 + (n + NE * l)
            return e, n % 2, i * 2 + (n // 2 + NE // 2 * l), n % 4, i + (n // 4 + NE // 4 * l)

        def is_expert(i, n):
            return not isinstance(i, int) or 0 <= 4 * i + n < NE

        def over_fours(eng, body):
            body(0)
            with eng.Fori(1, NE // 4 - 1) as i:
                body(i)
            body(NE // 4 - 1)

        norm_tiles = [NT, NT, NT, NL, NL]

        first_layer = dict(
            ld_router=32, ld_shared=32, ld_sdown=16, hrow_act=NT, hrow_dve=NT, h_stored=16 * NT,
            ych_used=2 * NT, g_bcast=8, row_turned=2 * NT, logits=1, scores=1, shared_gu=4, shared_silu=2,
            mod_turned=1, modT=1, Msel=NT, ranks=1, more_col=1, more_row=1, act_shared=2,
            shared_out=2 * NT, shared_y=2 * NT, onehot=NT, table=NT, out=2 * NT)
        ms_order = [0, 1, 2, "d0", "d1", "s0", "s1", 3, 4]

        def before(name, key):
            if name in first_layer:
                return first_layer[name] * key
            if name in ("ms", "rstd"):
                return ms_order.index(key)
            per_tile = {"ss": 1.0, "xn_act": 0.5, "xn_dve": 0.5, "hT_act": 2.0, "hT_dve": 2.0}
            if name == "xT":
                return KD * key
            return int(per_tile[name] * sum(norm_tiles[:key]))

        proj1 = ([("q", 0, m) for m in range(4)] + [("z", 1, t) for t in range(NL)]
                 + [("k", 2, m) for m in range(4)] + [("v", 3, t) for t in range(NT)]
                 + [("xbc", 4, m) for m in range(4)] + [("xbc", 5, 4 + m) for m in range(4)]
                 + [("dt", None, 0)])

        def gate_banks(l):
            return [(gi, s, h, (3 + gi * 4 + s * 2 + h) % 8)
                    for gi in range(2) for s in range(2 if l == 0 else 1) for h in range(2)]

        def row_half(t, half):
            return xn[:, t, :].rearrange("q (p k) -> q k p", k=KD)[:, 4 * half:4 * half + 4, :]

        def proj1_move(n):
            kind, _, m = proj1[n]
            bank = B[n % 8]
            if kind == "q":
                return qC[:, m, :], bank[:, 0:SEQ]
            if kind == "xbc":
                return (xbc[:, m, :].rearrange("p (s w) -> p s w", s=2)[:, :, 1:1 + H],
                        bank[:, :].rearrange("p (s w) -> p s w", s=2))
            if kind == "dt":
                return dtraw, bank[:, 0:NT * 16].rearrange("p (t h) -> p t h", t=NT)
            return {"z": zC, "k": kC, "v": vC}[kind][:, m, :], bank[:, :]

        n_in = [4, 6]
        HALF = 6
        first_in = [12, 12 + n_in[0] + HALF + 4 + HALF]
        mod1_blocks = [12 + n_in[0] + j for j in range(HALF)] + [12 + n_in[0] + HALF + 4 + j for j in range(HALF)]
        first_out = [12 + n_in[0] + HALF, first_in[1] + n_in[1]]
        first_shared = [first_out[0] + 2, first_out[1] + 2]
        assert first_in[1] % 2 == 0

        def loads_before(s):
            return sum(1 for b in range(s % 2, s + 1, 2) if not any(f <= b < f + 2 for f in first_shared))

        block = ctx.enter_context(nc.Block())

        @block.sync
        def _(sp):

            def small_load(dst, src):
                sp.dma_start(dst, src).then_inc(S("ld_small"), 16)

            small_load(con[:], a["con"])
            small_load(sel[:], a["sel"])
            small_load(craw[:, 0, :], a["c"][0, :].rearrange("(p k) -> p k", k=KD))
            small_load(craw[:, 1, :], a["c_ctx"].rearrange("(p k) -> p k", k=KD))
            for l in range(DEPTH):
                for i, n in enumerate(("g_mix", "g_ffn")):
                    small_load(gvec[:, i, l, :], a[n][l].rearrange("(p k) -> p k", k=KD))
            for src, r0 in ((a["ab_conv_w"][0], V_CONVW), (a["ab_conv_b"], V_CONVB), (a["ab_b_r"][0], V_BR),
                            (a["ab_b_i"][0], V_BI), (a["ab_lam"][0], V_LAM), (a["cd_conv_w"][0], V_DCONVW),
                            (a["cd_conv_b"], V_DCONVB)):
                rows = src.rearrange("r (c p) -> (r c) p", p=P)
                small_load(R[r0:r0 + rows.shape[0], 0:P], rows)
            for dst, src in ((sinkb, a["ab_sink"][0:1, :]), (dskip, a["cd_d_skip"][0:1, :]),
                             (alog, a["cd_a_log"].rearrange("a d h -> a (d h)")),
                             (dtb, a["cd_dt_bias"].rearrange("a d h -> a (d h)")),
                             (lamv[:], a["cd_lam"].rearrange("a d h -> a (d h)")),
                             (subg[:], a["cd_subln_g"][0:1, :])):
                small_load(dst, src.to_broadcast([P, src.shape[1]]))

            def load_block(s, slot, src, ncols=512):
                sp.wait_ge(S("stream_free"), s + 1)
                sp.dma_start(stream[:, slot, :, 0:ncols], src).then_inc(S(f"stream_ld{slot}"), 16)

            def load_mod1(j):
                load_block(mod1_blocks[j], mod1_blocks[j] % 2,
                           a["w_mod"][1].rearrange("(p k) n -> p k n", k=KD)[:, :, j * 512:j * 512 + 512])

            def load_expert(l, i, n):
                e, slot, _, _, _ = nth(l, i, n)
                wait(sp, "gu_done", e - 1)
                el = i * 4 + n
                one = (lambda w: w[l, el]) if isinstance(i, int) else (lambda w: w[l, bass.ds(el, 1)].squeeze(0))
                sp.dma_start(wg[:, slot], one(a["w_e_gate"]).rearrange("(p k) f -> p k f", k=KD)).then_inc(S(f"gu_ld{slot}"), 16)
                sp.dma_start(wu[:, slot], one(a["w_e_up"]).rearrange("(p k) f -> p k f", k=KD)).then_inc(S(f"gu_ld{slot}"), 16)
                wait(sp, "y_done", e * 2 - 2)
                sp.dma_start(wd[:, slot], one(a["w_e_down"]).rearrange("(p j) n -> p j n", j=2)).then_inc(S(f"down_ld{slot}"), 16)

            for l in range(DEPTH):
                nt = NT if l == 0 else NL
                if l:
                    after_stage(sp, f"combine{l - 1}")
                b_mod = a["b_mod"][l:l + 1, :].to_broadcast([2, 6 * D])
                if l == 0:
                    sp.dma_start(modrow, b_mod).then_inc(S("ld_bmod"), 16)
                else:
                    sp.wait_ge(S("mod1_stored"), 16 * 12)
                    sp.dma_start(modrow, mod_dram).then_inc(S("ld_bmod"), 16)
                    sp.dma_start(modbias, b_mod).then_inc(S("ld_bmod"), 16)
                    sp.dma_start(normg[:], a["cd_norm_g"][0:1, :].to_broadcast([P, 512])).then_inc(S("ld_normg"), 16)
                sp.dma_start(router_w[:], a["w_router"][l].rearrange("(p k) e -> p k e", k=KD)).then_inc(S("ld_router"), 16)
                sp.dma_start(router_b[:], a["b_router"][l:l + 1, :].to_broadcast([P, NE])).then_inc(S("ld_router"), 16)
                if l == 0:
                    w_mod = a["w_mod"][0].rearrange("(p k) n -> p k n", k=KD)
                    with sp.Fori(0, 6) as i:
                        for j in range(2):
                            load_block(i * 2 + j, j, w_mod[:, :, bass.ds(i * 1024 + j * 512, 512)])
                    sp.dma_start(X[:, 0:NL, :], a["x"][0].rearrange("(t p) d -> p t d", p=P)).then_inc(S("ld_x"), 16)
                    sp.dma_start(X[:, NL:NT, :], a["ctx"][0].rearrange("(t p) d -> p t d", p=P)).then_inc(S("ld_x"), 16)
                s = first_in[l]
                w_in = (a["ab_w_in"] if l == 0 else a["cd_w_in"])[0].rearrange("(p k) n -> p k n", k=KD)
                for n in range(n_in[l]):
                    width = 256 if (l == 0 and n == 3) else 512
                    load_block(s, s % 2, w_in[:, :, n * 512:n * 512 + width], width)
                    s += 1
                    if n == 1:
                        load_expert(l, 0, 0)
                        load_expert(l, 0, 1)
                        after_stage(sp, f"norm1{l}")
                        if l == 0:
                            sp.wait_ge(S("bdiag_zeroed"), 1)
                            for d in range(2):
                                for m, nm in enumerate(("ab_w_r", "ab_w_i")):
                                    src = a[nm][0, d].rearrange("(c b) i j -> b i c j", b=2)
                                    for b in range(2):
                                        q = d * 8 + m * 4
                                        sp.dma_start(bdiag[64 * b:64 * b + 64, q:q + 4, 64 * b:64 * b + 64],
                                                     src[b]).then_inc(S("ld_bdiag"), 16)
                        else:
                            sp.dma_start(dtw, w_in[:, :, 3072:3088]).then_inc(S("ld_dtw"), 16)
                if l == 0:
                    for j in range(HALF):
                        load_mod1(j)
                s = first_out[l]
                w_out = (a["ab_w_out"] if l == 0 else a["cd_w_out"])[0].rearrange("(k p) n -> p k n", p=P)
                for n in range(2):
                    load_block(s, s % 2, w_out[:, :, n * 512:n * 512 + 512])
                    s += 1
                sp.wait_ge(S("stream_free"), s + 1)
                for n, nm in enumerate(("ws_gate", "ws_up")):
                    sp.dma_start(stream[:, s % 2, :, n * DE:(n + 1) * DE],
                                 a[nm][l].rearrange("(p k) n -> p k n", k=KD)).then_inc(S("ld_shared"), 16)
                s += 1
                sp.wait_ge(S("stream_free"), s + 1)
                sp.dma_start(stream[:, s % 2, 0:4, :],
                             a["ws_down"][l].rearrange("(j p) (h n) -> p j h n", p=P, h=2)).then_inc(S("ld_sdown"), 16)
                for t in range(nt):
                    sp.wait_ge(S("hrow_act"), t + 1 + before("hrow_act", l))
                    sp.wait_ge(S("hrow_dve"), t + 1 + before("hrow_dve", l))
                    sp.dma_start(h_rows[t * P:(t + 1) * P, :], xn[:, t, :]).then_inc(S("h_stored"), 16)
                if l == 0:
                    for j in range(HALF, HALF + 2):
                        load_mod1(j)
                for n in range(2, 4):
                    load_expert(l, 0, n)
                with sp.Fori(1, NE // 4) as i:
                    for n in range(4):
                        load_expert(l, i, n)
                after_stage(sp, f"experts{l}")
                more = sp.value_load(more_i[0:1, 0:1], min_val=0, max_val=OVB)
                with sp.If(more):
                    with sp.Fori(0, OVB) as i:
                        e = sp.value_load(moree_i[0:1, bass.ds(i, 1)], min_val=0, max_val=NE - 1)
                        sp.wait_ge(S(f"more_step{l}"), i * MORE_STEPS + 2)
                        sp.dma_start(wg[:, 0], a["w_e_gate"][l, bass.ds(e, 1)].squeeze(0).rearrange("(p k) f -> p k f", k=KD)).then_inc(S(f"more_w{l}"), 16)
                        sp.dma_start(wu[:, 0], a["w_e_up"][l, bass.ds(e, 1)].squeeze(0).rearrange("(p k) f -> p k f", k=KD)).then_inc(S(f"more_w{l}"), 16)
                        sp.dma_start(wd[:, 0], a["w_e_down"][l, bass.ds(e, 1)].squeeze(0).rearrange("(p j) n -> p j n", j=2)).then_inc(S(f"more_w{l}"), 16)
                after_stage(sp, f"more{l}")
                yv = y_rows.rearrange("(t p q k) d -> t q p (k d)", p=P, q=2, k=4)
                for t in range(nt):
                    for q in range(2):
                        wait(sp, "ych_used", 2 * t + q - 1, before("ych_used", l))
                        sp.dma_start(ych[:, q, :], yv[t, q]).then_inc(S(f"ych_ld{q}"), 16)
                    if l == 0:
                        load_mod1(HALF + 2 + t)
            after_stage(sp, f"combine{DEPTH - 1}")
            sp.dma_start(G[:, 0, 0, :], a["g_final"].unsqueeze(0).to_broadcast([P, D])).then_inc(S("ld_gfin"), 16)
            for t in range(NL):
                sp.wait_ge(S("out_ready"), t + 1)
                sp.dma_start(out[0, t * P:(t + 1) * P, :], xn[:, t, :]).then_inc(S("out_stored"), 16)
            sp.wait_ge(S("out_stored"), 16 * NL)

        @block.gpsimd
        def _(pool):
            link = linker(pool, "pool_chain")

            def waited():
                pool.sem_inc(S("pool_waited"), 1)

            def rsqrt(q, n=4):
                pool.wait_ge(S("ms"), 1 + before("ms", q))
                pool.tensor_tensor(rstd[:, 0:n], ss[:, 0:n], half_exp[:, 0:n], ALU.pow).then_inc(S("rstd"), 1)

            link(pool.memset(half_exp[:], -0.5))
            for l in range(DEPTH):
                nt = NT if l == 0 else NL
                end_stage(pool, f"mod{l}")
                rsqrt(2 * l, NT)
                end_stage(pool, f"norm1{l}")
                if l == 0:
                    link(pool.memset(xap, 0.0), "pads_zeroed")
                    link(pool.memset(bdiag, 0.0), "bdiag_zeroed")
                    for s in ("proj0", "lru0", "attn0", "out0"):
                        end_stage(pool, s)
                else:
                    link(pool.memset(xbc, 0.0), "pads_zeroed")
                    end_stage(pool, "proj1")
                    end_stage(pool, "conv1")
                    for qt in range(NL):
                        rsqrt(f"d{qt}")
                    end_stage(pool, "attn1")
                    for c in range(NL):
                        rsqrt(f"s{c}", 2)
                    end_stage(pool, "ssd1")
                    end_stage(pool, "out1")
                rsqrt(2 * l + 1, nt)
                end_stage(pool, f"norm2{l}")
                pool.wait_ge(S("h_stored"), 16 * nt + before("h_stored", l))
                link(pool.memset(xg, 0.0))
                end_stage(pool, f"route{l}")

                def gather(i, n):
                    e, _, _, slot, _ = nth(l, i, n)
                    if not is_expert(i, n):
                        return
                    wait(pool, "x_turned", e * 2 - 6)
                    waited()
                    pool.tensor_copy(gat_i[:, slot:slot + 1], toks_i[:, bass.ds(i * 4 + n, 1)]).then_inc(S("gat_idx"), 1)
                    pool.wait_ge(S("gat_idx"), e + 1)
                    waited()
                    pool.indirect_dma_start(out=xg[:, slot, :], out_offset=None, in_=h_rows,
                                            in_offset=bass.IndirectOffsetOnAxis(gat_i[:, slot:slot + 1], 0),
                                            bounds_check=nt * P - 1, oob_is_err=False).then_inc(S(f"xg_ld{slot}"), 16)

                def scatter(i, n):
                    e, _, _, slot, turns = nth(l, i, n)
                    if not is_expert(i, n):
                        return
                    wait(pool, f"y_stored{slot}", turns * 16)
                    waited()
                    pool.tensor_copy(sca_i[:, slot:slot + 1], rows_i[:, bass.ds(i * 4 + n, 1)]).then_inc(S("sca_idx"), 1)
                    pool.wait_ge(S("sca_idx"), e + 1)
                    pool.wait_ge(S("y_act"), e + 1)
                    pool.wait_ge(S("y_dve"), e + 1)
                    waited()
                    pool.indirect_dma_start(out=y_rows, out_offset=bass.IndirectOffsetOnAxis(sca_i[:, slot:slot + 1], 0),
                                            in_=ysb[:, slot, :], in_offset=None,
                                            bounds_check=nt * P * TOPK - 1, oob_is_err=False).then_inc(S(f"y_stored{slot}"), 16)

                def four(i):
                    for n in range(4):
                        gather(i, n + 3)
                        if is_expert(i, n - 1):
                            scatter(i, n - 1)

                for n in range(3):
                    gather(0, n)
                over_fours(pool, four)
                scatter(NE // 4 - 1, 3)
                for n in range(4):
                    pool.wait_ge(S(f"y_stored{n}"), 16 * (NE // 4) * (l + 1))
                end_stage(pool, f"experts{l}")
                more = pool.value_load(more_i[0:1, 0:1], min_val=0, max_val=OVB)
                with pool.If(more):
                    with pool.Fori(0, OVB) as i:
                        step = S(f"more_step{l}")
                        pool.tensor_copy(gat_i[:, 0:1], toks_i[:, bass.ds(i + NE, 1)]).then_inc(step, 1)
                        pool.tensor_copy(sca_i[:, 0:1], rows_i[:, bass.ds(i + NE, 1)]).then_inc(step, 1)
                        pool.wait_ge(step, i * MORE_STEPS + 2)
                        waited()
                        pool.indirect_dma_start(out=xg[:, 0, :], out_offset=None, in_=h_rows,
                                                in_offset=bass.IndirectOffsetOnAxis(gat_i[:, 0:1], 0),
                                                bounds_check=nt * P - 1, oob_is_err=False).then_inc(S(f"more_dma{l}"), 16)
                        pool.wait_ge(step, i * MORE_STEPS + 13)
                        waited()
                        pool.indirect_dma_start(out=y_rows, out_offset=bass.IndirectOffsetOnAxis(sca_i[:, 0:1], 0),
                                                in_=ysb[:, 0, :], in_offset=None,
                                                bounds_check=nt * P * TOPK - 1, oob_is_err=False).then_inc(S(f"more_dma{l}"), 16)
                        pool.wait_ge(S(f"more_dma{l}"), i * 32 + 32)
                end_stage(pool, f"more{l}")
                end_stage(pool, f"combine{l}")
            rsqrt(4, NL)
            pool.drain()

        @block.scalar
        def _(act):
            link = linker(act, "act_chain")

            def squares(q):
                for t in range(norm_tiles[q]):
                    link(act.activation(xn[:, t, :], X[:, t, :], ACT.Square, accum_out=ss[:, t:t + 1]), "ss")

            def norm(q, which):
                nt = norm_tiles[q]
                squares(q)
                act.wait_ge(S("rstd"), 1 + before("rstd", q))
                for t in range(0, nt, 2):
                    link(act.activation(xn[:, t, :], X[:, t, :], ACT.Copy, scale=rstd[:, t:t + 1]), "xn_act")
                for k in range(0, KD, 2):
                    act.wait_ge(S("xT"), k + 1 + before("xT", q))
                    for s in range(nt // 2):
                        link(act.activation(hT[:, k, s * H:s * H + H], B[k][:, s * H:s * H + H], ACT.Identity,
                                            scale=mscale[:, which, k, s:s + 1], bias=modT[:, 2 * which, k, s:s + 1]), "hT_act")

            def store_mod1(j):
                act.wait_ge(S("mod1_mm"), j + 1)
                wait(act, "mod1_stored", 16 * j)
                link(act.activation(mod1_stage, B[6 + j % 2][0:2, :], ACT.Copy), "mod1_moved")
                act.dma_start(mod_dram[:, j * 512:j * 512 + 512], mod1_stage).then_inc(S("mod1_stored"), 16)

            act.wait_ge(S("ld_small"), 16 * N_SMALL)
            link(act.activation(csT[:].rearrange("p k s -> p s k"), craw[:], ACT.Silu), "c_silu")
            act.wait_ge(S("ld_x"), 32)
            for l in range(DEPTH):
                nt = NT if l == 0 else NL
                for n, (gi, s, h, bank) in enumerate(gate_banks(l)):
                    act.wait_ge(S("g_bcast"), n + 1 + before("g_bcast", l))
                    link(act.activation(G[:, gi, s, h * 512:h * 512 + 512], B[bank][:, :], ACT.Copy))
                end_stage(act, f"mod{l}")
                norm(2 * l, 0)
                end_stage(act, f"norm1{l}")
                if l == 0:
                    act.wait_ge(S("pads_zeroed"), 1)
                    for n in range(0, 14, 2):
                        act.wait_ge(S("proj0"), n + 1)
                        src = B[n % 8][:, :]
                        if n < 8:
                            dst = catA[:, n, :]
                        elif n < 12:
                            dst = xap[:, n - 8, :].rearrange("p (s w) -> p s w", s=2)[:, :, 1:1 + H]
                            src = src.rearrange("p (s w) -> p s w", s=2)
                        else:
                            dst = ktmp
                        link(act.activation(dst, src, ACT.Copy), "proj0_act")
                    end_stage(act, "proj0")
                    for m in range(4):
                        link(act.activation(catA[:, m, :], catA[:, m, :], ACT.Gelu_apprx_tanh), "gelu")
                    act.wait_ge(S("rope0"), 5)
                    for g in range(2):
                        for b in range(2):
                            link(act.activation(kd[64 * b:64 * b + 64, g, :], ktmp[64 * g:64 * g + 64, :], ACT.Copy))
                    act.wait_ge(S("lam_abs"), 1)
                    link(act.activation(tmpc[:, 8:16], tmpc[:, 0:8], ACT.Exp, scale=-1.0))
                    link(act.activation(tmpc[:, 16:24], tmpc[:, 8:16], ACT.Ln, bias=1.0), "lam_ln")
                    store_mod1(0)
                    act.wait_ge(S("lsc_ready"), 1)
                    for d in range(2):
                        wait(act, "scan_done", 4 * d)
                        for c in range(4):
                            n = d * 4 + c
                            act.wait_ge(S("lru_mm"), 2 * n + 1)
                            link(act.activation(a4[:, c, :], B[(2 * n) % 6][:, :], ACT.Tanh, scale=0.5, bias=hbr[:, n:n + 1]), "lru_r")
                            link(act.activation(m4[:, c, :], a4[:, c, :], ACT.Tanh, scale=lnsc[:, n:n + 1], bias=lnsc[:, n:n + 1]), "lru_th")
                            link(act.activation(a4[:, c, :], a4[:, c, :], ACT.Exp, scale=lsc[:, n:n + 1], bias=lsc[:, n:n + 1]), "lru_a")
                            act.wait_ge(S("lru_mm"), 2 * n + 2)
                            link(act.activation(z4[:, c, :], B[(2 * n + 1) % 6][:, :], ACT.Tanh, scale=0.5, bias=hbi[:, n:n + 1]), "lru_i")
                        for c in range(4):
                            n = d * 4 + c
                            act.wait_ge(S("lru_m"), n + 1)
                            link(act.activation(m4[:, c, :], m4[:, c, :], ACT.Sqrt, scale=0.25), "lru_sq")
                        for j in ((1, 2) if d == 0 else (3, 4, 5)):
                            store_mod1(j)
                    end_stage(act, "lru0")
                    for n in range(8 * NT + 7):
                        if n < 8 * NT:
                            nk = T if n < 8 * NL else CTX
                            act.wait_ge(S("nmax0"), n + 1)
                            wait(act, "p_turned", n - 1)
                            link(act.activation(pA[:, n % 2, 0:nk], B[n % 2][:, 0:nk], ACT.Exp, scale=SCALE, bias=nmx[:, n:n + 1],
                                                accum_out=rsum[:, n:n + 1]), "p_ready")
                        if n > 2 and n % 8 == 2:
                            act.wait_ge(S("sink_in"), n // 8)
                            link(act.activation(tmpc[:, 8:16], tmpc[:, 0:8], ACT.Exp), "sink_exp")
                        if n > 6 and n % 8 == 6:
                            qt = n // 8 - 1
                            act.wait_ge(S("att_turned"), qt + 1)
                            link(act.activation(catA[:, 4:8, qt * P:qt * P + P],
                                                B[6 + qt % 2][:, :].rearrange("p (c q) -> p c q", c=4), ACT.Copy), "att_cat")
                    end_stage(act, "attn0")
                    end_stage(act, "out0")
                else:
                    act.wait_ge(S("pads_zeroed"), 2)
                    for n in range(0, len(proj1), 2):
                        act.wait_ge(S("proj1"), n + 1)
                        dst, src = proj1_move(n)
                        link(act.activation(dst, src, ACT.Copy), "proj1_act")
                    end_stage(act, "proj1")
                    for c in range(8):
                        act.wait_ge(S("conv1"), c + 1)
                        link(act.activation(hT[:, c, :], hT[:, c, :], ACT.Silu))
                    link(act.activation(zC, zC, ACT.Silu))
                    act.wait_ge(S("dt_in"), 1)
                    link(act.activation(dta[:], dta[:], ACT.Exp, scale=-1.0))
                    link(act.activation(alog, alog, ACT.Exp))
                    link(act.activation(lamc[:, 0:2], lamc[:, 0:2], ACT.Exp))
                    link(act.activation(dta[:], dta[:], ACT.Ln, bias=1.0), "dt_ln")
                    end_stage(act, "conv1")
                    for u in range(4 * NL + 1):
                        if u < 4 * NL:
                            wait(act, "w_turned", u - 1)
                            for m in range(2):
                                n = 2 * u + m
                                act.wait_ge(S("nmax1"), n + 1)
                                link(act.activation(pC[:, 2 * (u % 2) + m, :], B[n % 2][:, :], ACT.Exp, scale=SCALE, bias=nmx[:, n:n + 1],
                                                    accum_out=rsum[:, n:n + 1]), "p1_ready")
                        if u:
                            act.wait_ge(S("w_turned"), u)
                            link(act.activation(wTC[:, (u - 1) % 2, :], B[2 + (u - 1) % 2][:, :], ACT.Copy), "wT_ready")
                    end_stage(act, "attn1")
                    act.wait_ge(S("acum_ready"), 1)
                    link(act.activation(eac[:], acum[:], ACT.Exp))
                    link(act.activation(tend[:], tend[:], ACT.Exp))
                    link(act.activation(etot[:], etot[:], ACT.Exp), "acum_exp")
                    for n in range(2 * NL * 2):
                        act.wait_ge(S("seg_ready"), n + 1)
                        link(act.activation(seg, seg, ACT.Exp), "seg_exp")
                    end_stage(act, "ssd1")
                    end_stage(act, "out1")
                norm(2 * l + 1, 1)
                for t in range(nt):
                    act.wait_ge(S("row_turned"), 2 * t + 1 + before("row_turned", l))
                    link(act.activation(row_half(t, 0), B[2 * t][:, :].rearrange("q (k p) -> q k p", k=4), ACT.Copy), "hrow_act")
                end_stage(act, f"norm2{l}")
                act.wait_ge(S("logits"), 1 + before("logits", l))
                link(act.activation(scores[:, 0:nt, :], B[0][:, 0:nt * NE].rearrange("p (t e) -> p t e", e=NE), ACT.Sigmoid), "scores")
                for m in range(2):
                    act.wait_ge(S("shared_gu"), 2 * m + 1 + before("shared_gu", l))
                    link(act.activation(sS[:, m, 0:nt * P], B[4 + 2 * m][:, 0:nt * P], ACT.Silu), "shared_silu")
                end_stage(act, f"route{l}")

                def x_evac(i, n):
                    e, half, _, _, _ = nth(l, i, n)
                    act.wait_ge(S("x_turned"), e * 2 + 1)
                    act.activation(xgT[:, half, 0:512], B[0][:, :], ACT.Copy).then_inc(S("xgT_act"), 1)

                def y_evac(i, n):
                    e, _, _, slot, turns = nth(l, i, n)
                    act.wait_ge(S("y_done"), e * 2 + 1)
                    wait(act, f"y_stored{slot}", turns * 16)
                    act.activation(ysb[:, slot, 0:512], B[6][:, :], ACT.Copy).then_inc(S("y_act"), 1)

                def four(i):
                    for n in range(4):
                        e, half, _, _, _ = nth(l, i, n)
                        act.wait_ge(S("gu_done"), e + 1)
                        act.activation(sg[:, half, :], B[2 + half][:, 0:DE], ACT.Silu).then_inc(S("sg_ready"), 1)
                        if is_expert(i, n + 1):
                            x_evac(i, n + 1)
                        if is_expert(i, n - 1):
                            y_evac(i, n - 1)

                x_evac(0, 0)
                over_fours(act, four)
                y_evac(NE // 4 - 1, 3)
                end_stage(act, f"experts{l}")
                more = act.value_load(more_i[0:1, 0:1], min_val=0, max_val=OVB)
                with act.If(more):
                    with act.Fori(0, OVB) as i:
                        act.wait_ge(S(f"more_step{l}"), i * MORE_STEPS + 6)
                        act.activation(sg[:, 0, :], B[2][:, 0:DE], ACT.Silu).then_inc(S(f"more_step{l}"), 1)
                end_stage(act, f"more{l}")
                if l == 0:
                    for j in range(HALF, 2 * HALF):
                        store_mod1(j)
                end_stage(act, f"combine{l}")
            squares(4)
            act.drain()

        @block.tensor
        def _(pe):
            def product(out, pairs, start=True):
                for n, (lhsT, rhs) in enumerate(pairs):
                    ins = pe.matmul(out, lhsT, rhs, start=(start and n == 0), stop=(n == len(pairs) - 1))
                return ins

            def turn(out, in_, n=P):
                return pe.transpose(out, in_, C["ident"][0:n, 0:n])

            def block_ready(s):
                pe.wait_ge(S(f"stream_ld{s % 2}"), 16 * loads_before(s))
                return stream[:, s % 2]

            def mod1(j):
                W = block_ready(mod1_blocks[j])
                wait(pe, "mod1_moved", j - 1)
                product(B[6 + j % 2][0:2, :], [(csT[:, k, :], W[:, k, :]) for k in range(KD)]).then_inc(S("mod1_mm"), 1)
                pe.drain().then_inc(S("stream_free"), 1)

            def norm(q):
                nt = norm_tiles[q]
                pe.wait_ge(S("xn_act"), nt // 2 + before("xn_act", q))
                pe.wait_ge(S("xn_dve"), nt // 2 + before("xn_dve", q))
                for k in range(KD):
                    for t in range(nt):
                        ins = turn(B[k][:, t * P:t * P + P], xn[:, t, k::KD])
                    ins.then_inc(S("xT"), 1)

            pe.wait_ge(S("ld_small"), 16 * N_SMALL)
            pe.sem_inc(S("stream_free"), 2)
            turn(B[7][:, 0:V_ROWS], vraw, V_ROWS).then_inc(S("v_turned"), 1)
            pe.wait_ge(S("c_silu"), 1)
            for l in range(DEPTH):
                nt = NT if l == 0 else NL
                cat = catA if l == 0 else catC
                if l == 0:
                    with pe.Fori(0, 6) as i:
                        for j in range(2):
                            pe.wait_ge(S(f"stream_ld{j}"), i * 16 + 16)
                            pe.wait_ge(S("mod_rows"), i * 2 + j + 1)
                            product(B[j][0:2, :], [(csT[:, k, :], stream[:, j, k, :]) for k in range(KD)]).then_inc(S("stream_free"), 1)
                pe.wait_ge(S("mod_rows"), 14 + l)
                for v, split in enumerate((0, 1, 3, 4)):
                    for k in range(KD):
                        ins = turn(B[2][:, (v * KD + k) * 2:(v * KD + k) * 2 + 2],
                                   modrow[:, split * D + k:(split + 1) * D:KD], 2)
                ins.then_inc(S("mod_turned"), 1)
                for gi, s, h, bank in gate_banks(l):
                    if bank == 2:
                        pe.wait_ge(S("modT"), 1 + before("modT", l))
                    c0 = (2 + 3 * gi) * D + h * 512
                    pe.matmul(B[bank][:, :], sel[:, s * P:s * P + P], modrow[:, c0:c0 + 512],
                              start=True, stop=True).then_inc(S("g_bcast"), 1)
                end_stage(pe, f"mod{l}")
                norm(2 * l)
                end_stage(pe, f"norm1{l}")
                if l == 0:
                    for n in range(14):
                        blk, m = n // 4, n % 4
                        if m == 0:
                            W = block_ready(first_in[0] + blk)
                        if n >= 8:
                            pe.wait_ge(S("proj0_act" if n % 2 == 0 else "proj0_dve"), (n - 8) // 2 + 1)
                        if n < 13:
                            ins = product(B[n % 8][:, :], [(W[:, k, m * P:m * P + P], hT[:, k, :]) for k in range(KD)])
                        else:
                            for t in range(NT):
                                ins = product(B[n % 8][:, t * P:t * P + P],
                                              [(hT[:, k, t * P:t * P + P], W[:, k, P:2 * P]) for k in range(KD)])
                        ins.then_inc(S("proj0"), 1)
                        if m == 3 or n == 13:
                            pe.drain().then_inc(S("stream_free"), 1)
                    end_stage(pe, "proj0")
                    for m in range(5):
                        src = catA[:, 4 + m, 0:H] if m < 4 else ktmp[:, 0:H]
                        pe.matmul(B[m][:, 0:H], C["swap"], src, start=True, stop=True).then_inc(S("swapped0"), 1)
                    mod1(0)
                    pe.wait_ge(S("ld_bdiag"), 16 * 8)
                    pe.wait_ge(S("rope0"), 5)
                    for d in range(2):
                        for c in range(4):
                            n = d * 4 + c
                            if d == 0:
                                pe.wait_ge(S("conv0"), c + 1)
                            wait(pe, "lru_r", n - 2)
                            pe.matmul(B[(2 * n) % 6][:, :], bdiag[:, d * 8 + c, :], uA[:, c, :], start=True, stop=True).then_inc(S("lru_mm"), 1)
                            wait(pe, "lru_i", n - 2)
                            pe.matmul(B[(2 * n + 1) % 6][:, :], bdiag[:, d * 8 + 4 + c, :], uA[:, c, :], start=True, stop=True).then_inc(S("lru_mm"), 1)
                        for j in ((1, 2) if d == 0 else (3, 4, 5)):
                            mod1(j)
                    end_stage(pe, "lru0")

                    def att_turn(qt):
                        pe.wait_ge(S("att_ready"), qt + 1)
                        wait(pe, "att_cat", qt - 1)
                        for c in range(4):
                            ins = turn(B[6 + qt % 2][:, c * P:c * P + P], attA[:, c * P:c * P + P])
                        ins.then_inc(S("att_turned"), 1)

                    for n in range(8 * NT + 2):
                        if n < 8 * NT:
                            qt, h = n // 8, n % 8
                            b, g = 64 * (h % 2), h // 4
                            k0, nk = (0, T) if qt < NL else (SEQ, CTX)
                            wait(pe, "p_ready", n - 1)
                            masked = {0: P, 1: 0}.get(qt)
                            for c0, c1 in {0: ((0, P), (P, 2 * P), (2 * P, T)), 1: ((0, P), (P, T))}.get(qt, ((0, nk),)):
                                q_ap, k_ap = catA[b:b + 64, 4 + h // 2, qt * P:qt * P + P], kd[b:b + 64, g, k0 + c0:k0 + c1]
                                if c0 == masked:
                                    pe.matmul(B[n % 2][:, c0:c1], C["ident"], C["mask_hi" if qt == 0 else "mask_lo"],
                                              start=True, stop=False)
                                ins = pe.matmul(B[n % 2][:, c0:c1], q_ap, k_ap, start=(c0 != masked), stop=True)
                            ins.then_inc(S("scores0"), 1)
                        if 0 < n <= 8 * NT:
                            m = n - 1
                            nk = NT if m < 8 * NL else NL
                            pe.wait_ge(S("p_ready"), m + 1)
                            wait(pe, "pT_ready", m - 1)
                            for t in range(nk):
                                ins = turn(B[2 + m % 2][:, t * P:t * P + P], pA[:, m % 2, t * P:t * P + P])
                            ins.then_inc(S("p_turned"), 1)
                        if n > 1:
                            m = n - 2
                            qt, h = m // 8, m % 8
                            nk, t0 = (NT, 0) if qt < NL else (NL, NL)
                            pe.wait_ge(S("pT_ready"), m + 1)
                            if h == 0:
                                wait(pe, "att_ready", qt - 1)
                            g = h // 4
                            ins = product(B[4 + qt % 2][:, h * 64:h * 64 + 64],
                                          [(pTA[:, m % 2, t * P:t * P + P], vA[:, t0 + t, g * 64:g * 64 + 64]) for t in range(nk)])
                            if h == 7:
                                ins.then_inc(S("pv_done"), 1)
                            else:
                                ins.then_inc(S("pv_step"), 1)
                            if h == 3 and qt:
                                att_turn(qt - 1)
                    att_turn(NT - 1)
                    end_stage(pe, "attn0")
                else:
                    for n, (kind, blk, m) in enumerate(proj1):
                        first = n == 0 or proj1[n - 1][1] != blk
                        last = n + 1 == len(proj1) or proj1[n + 1][1] != blk
                        if kind == "dt":
                            pe.wait_ge(S("ld_dtw"), 16)
                        elif first:
                            W = block_ready(first_in[1] + blk)
                        if n >= 8:
                            pe.wait_ge(S("proj1_act" if n % 2 == 0 else "proj1_dve"), (n - 8) // 2 + 1)
                        m4_ = m % 4
                        if kind == "q":
                            ins = product(B[n % 8][:, 0:SEQ], [(W[:, k, m * P:m * P + P], hT[:, k, 0:SEQ]) for k in range(KD)])
                        elif kind in "zv":
                            ins = product(B[n % 8][:, :], [(hT[:, k, m * P:m * P + P], W[:, k, :]) for k in range(KD)])
                        elif kind == "dt":
                            for t in range(NT):
                                ins = product(B[n % 8][:, t * 16:t * 16 + 16],
                                              [(hT[:, k, t * P:t * P + P], dtw[:, k, :]) for k in range(KD)])
                        else:
                            ins = product(B[n % 8][:, :], [(W[:, k, m4_ * P:m4_ * P + P], hT[:, k, :]) for k in range(KD)])
                        ins.then_inc(S("proj1"), 1)
                        if last and kind != "dt":
                            pe.drain().then_inc(S("stream_free"), 1)
                    end_stage(pe, "proj1")
                    for m in range(8):
                        src = qC[:, m, :] if m < 4 else kC[:, m - 4, 0:SEQ]
                        pe.matmul(B[m][:, 0:SEQ], C["swap"], src, start=True, stop=True).then_inc(S("swapped1"), 1)
                    end_stage(pe, "conv1")

                    def o_turn(qt):
                        pe.wait_ge(S("o_ready"), qt + 1)
                        for c in range(4):
                            ins = turn(B[6 + qt][:, c * P:c * P + P], oC[:, c * P:c * P + P])
                        ins.then_inc(S("o_turned"), 1)

                    for u in range(4 * NL + 1):
                        if u < 4 * NL:
                            qt, h = u // 4, u % 4
                            for m in range(2):
                                n = 2 * u + m
                                wait(pe, "p1_ready", n - 1)
                                pe.matmul(B[n % 2][:, :], qC[64 * m:64 * m + 64, h, qt * P:qt * P + P],
                                          kC[64 * m:64 * m + 64, h, :], start=True, stop=True).then_inc(S("scores1"), 1)
                        if u:
                            w = u - 1
                            qt, h = w // 4, w % 4
                            pe.wait_ge(S("w_ready1"), w + 1)
                            wait(pe, "wT_ready", w - 1)
                            for t in range(NT):
                                ins = turn(B[2 + w % 2][:, t * P:t * P + P], pC[:, 2 * (w % 2), t * P:t * P + P])
                            ins.then_inc(S("w_turned"), 1)
                            pe.wait_ge(S("wT_ready"), w + 1)
                            ins = product(B[4 + qt][:, h * P:h * P + P],
                                          [(wTC[:, w % 2, t * P:t * P + P], vC[:, t, h * P:h * P + P]) for t in range(NT)])
                            if h == 3:
                                ins.then_inc(S("pv1_done"), 1)
                            if h == 0 and qt:
                                o_turn(qt - 1)
                    o_turn(NL - 1)
                    end_stage(pe, "attn1")
                    for t in range(NT):
                        pe.matmul(B[0][:, t * 16:t * 16 + 8], C["tri_le"], dta[:, t, 0:8], start=True, stop=True)
                        pe.matmul(B[0][:, t * 16 + 8:t * 16 + 16], C["tri_ge"], dta[:, t, 8:16], start=True, stop=True)
                        ins = pe.matmul(B[1][:, t * 16:t * 16 + 16], C["ones"], dta[:, t, :], start=True, stop=True)
                    ins.then_inc(S("acum_mm"), 1)
                    for c in range(NL):
                        for g in range(2):
                            ins = pe.matmul(B[2][:, (2 * c + g) * P:(2 * c + g) * P + P], hT[:, 4 + g, c * P:c * P + P],
                                            hT[:, 6 + g, c * P:c * P + P], start=True, stop=True)
                    ins.then_inc(S("cb_mm"), 1)
                    for t in range(NT):
                        for c in range(4):
                            ins = turn(B[3 + t][:, c * P:c * P + P], hT[:, c, t * P:t * P + P])
                        ins.then_inc(S("ssd_turned"), 1)
                    for t in range(NT):
                        bank = B[7] if t < 2 else B[0]
                        if t == 2:
                            pe.wait_ge(S("acum_ready"), 1)
                        for g in range(2):
                            o = (2 * (t % 2) + g) * P
                            ins = turn(bank[:, o:o + P], hT[:, 4 + g, t * P:t * P + P])
                        if t % 2:
                            ins.then_inc(S("ssd_turned"), 1)
                    pe.wait_ge(S("ssd_moved"), 7)
                    n_state = n_seg = 0
                    for d in range(2):
                        for idx, t in enumerate(chunks(d)):
                            if t < NL:
                                for g in range(2):
                                    n_seg += 1
                                    pe.wait_ge(S("tri_dta"), n_seg)
                                    pe.matmul(B[3 + g][:, :], C["ones"], tri_dta, start=True, stop=True).then_inc(S("seg_mm"), 1)
                                    pe.wait_ge(S("w_ready"), n_seg)
                                    for r in range(4):
                                        h = 4 * g + r
                                        ins = pe.matmul(B[6 + t][:, h * 64:h * 64 + 64], seg[:, r * P:r * P + P],
                                                        xdt[:, h * 64:h * 64 + 64], start=(d == 0 and h == 0),
                                                        stop=(d == 1 and h == 7), skip_group_check=True)
                                    ins.then_inc(S("y_mm"), 1)
                                pe.wait_ge(S("H_ready"), n_state)
                                for g in range(2):
                                    ins = pe.matmul(B[5][:, g * 256:g * 256 + 256], hT[:, 6 + g, t * P:t * P + P],
                                                    Hst[:, g * 256:g * 256 + 256], start=True, stop=True)
                                ins.then_inc(S("inter_mm"), 1)
                            if idx < 3:
                                n_state += 1
                                pe.wait_ge(S("xte_ready"), n_state)
                                for g in range(2):
                                    ins = pe.matmul(B[2][:, g * 256:g * 256 + 256], btok[:, t, g * P:g * P + P],
                                                    xte[:, g * 256:g * 256 + 256], start=True, stop=True)
                                ins.then_inc(S("state_mm"), 1)
                    for c in range(NL):
                        pe.wait_ge(S("ssd_y"), c + 1)
                        for m in range(4):
                            ins = turn(B[3 + c][:, m * P:m * P + P], yacc[:, c, m * P:m * P + P])
                        ins.then_inc(S("ssd_y_turned"), 1)
                    end_stage(pe, "ssd1")
                for h in range(2):
                    W = block_ready(first_out[l] + h)
                    for t in range(nt):
                        ins = product(B[h * nt + t][:, :], [(cat[:, k, t * P:t * P + P], W[:, k, :]) for k in range(KD)])
                        ins.then_inc(S("out"), 1)
                    pe.drain().then_inc(S("stream_free"), 1)
                end_stage(pe, f"out{l}")
                q = 2 * l + 1
                norm(q)
                pe.wait_ge(S("hT_act"), 4 * (nt // 2) + before("hT_act", q))
                pe.wait_ge(S("hT_dve"), 4 * (nt // 2) + before("hT_dve", q))
                for t in range(nt):
                    for half in range(2):
                        for k in range(4):
                            ins = turn(B[2 * t + half][:, k * P:k * P + P], hT[:, 4 * half + k, t * P:t * P + P])
                        ins.then_inc(S("row_turned"), 1)
                end_stage(pe, f"norm2{l}")
                pe.wait_ge(S("ld_router"), 32 + before("ld_router", l))
                for t in range(nt):
                    ins = product(B[0][:, t * NE:t * NE + NE], [(hT[:, k, t * P:t * P + P], router_w[:, k, :]) for k in range(KD)])
                ins.then_inc(S("logits"), 1)
                s = first_shared[l]
                pe.wait_ge(S("ld_shared"), 32 + before("ld_shared", l))
                for m in range(2):
                    for up in range(2):
                        c0 = up * DE + m * P
                        ins = product(B[4 + 2 * m + up][:, 0:nt * P],
                                      [(stream[:, s % 2, k, c0:c0 + P], hT[:, k, 0:nt * P]) for k in range(KD)])
                        ins.then_inc(S("shared_gu"), 1)
                pe.drain().then_inc(S("stream_free"), 1)
                pe.wait_ge(S("Msel"), nt + before("Msel", l))
                for t in range(nt):
                    product(B[1][:, t * NE:t * NE + NE],
                            [(C["tri_lt"], Msel[:, t, :])] + [(C["ones"], Msel[:, u, :]) for u in range(t)])
                product(B[2][:, 0:NE], [(C["ones"], Msel[:, t, :]) for t in range(nt)]).then_inc(S("ranks"), 1)
                pe.wait_ge(S("more_col"), 1 + before("more_col", l))
                turn(B[0][0:1, 0:P], s1[:, 0:1]).then_inc(S("more_row"), 1)
                pe.wait_ge(S("ld_sdown"), 16 + before("ld_sdown", l))
                pe.wait_ge(S("act_shared"), 2 + before("act_shared", l))
                for t in range(nt):
                    for h in range(2):
                        n = 2 * t + h
                        wait(pe, "shared_out", n - 3, before("shared_out", l))
                        ins = product(B[4 + n % 4][:, :], [(actS[:, j, t * P:t * P + P], stream[:, 1 - s % 2, 2 * j + h, :]) for j in range(2)])
                        ins.then_inc(S("shared_y"), 1)
                    if t == nt - 1:
                        pe.drain().then_inc(S("stream_free"), 1)
                    pe.wait_ge(S("onehot"), t + 1 + before("onehot", l))
                    for k in range(TOPK):
                        ins = pe.matmul(B[3][:, 0:NCOL], lo_oh[:, k, :], hi_oh[:, k, :],
                                        start=(t == 0 and k == 0), stop=(t == nt - 1 and k == TOPK - 1), skip_group_check=True)
                    ins.then_inc(S("table"), 1)
                end_stage(pe, f"route{l}")

                def turn_x(i, n):
                    e, _, _, slot, turns = nth(l, i, n)
                    pe.wait_ge(S(f"xg_ld{slot}"), turns * 16 + 16)
                    for b, moved in ((0, "xgT_act"), (1, "xgT_dve")):
                        wait(pe, moved, e)
                        for k in range(4):
                            ins = turn(B[b][:, k * P:k * P + P], xg[:, slot, 4 * b + k::KD])
                        ins.then_inc(S("x_turned"), 1)

                def gate_up(i, n):
                    e, half, turns, _, _ = nth(l, i, n)
                    pe.wait_ge(S(f"gu_ld{half}"), turns * 32 + 32)
                    pe.wait_ge(S("xgT_act"), e + 1)
                    pe.wait_ge(S("xgT_dve"), e + 1)
                    for w, c0 in ((wg, 0), (wu, DE)):
                        ins = product(B[2 + half][:, c0:c0 + DE], [(xgT[:, half, k * P:k * P + P], w[:, half, k, :]) for k in range(KD)])
                    ins.then_inc(S("gu_done"), 1)

                def turn_act(i, n):
                    e, half, _, _, _ = nth(l, i, n)
                    pe.wait_ge(S("act_ready"), e + 1)
                    for j in range(2):
                        ins = turn(B[4 + half][:, j * P:j * P + P], act_[:, half, j::2])
                    ins.then_inc(S("act_turned"), 1)

                def down(i, n):
                    e, half, turns, _, _ = nth(l, i, n)
                    pe.wait_ge(S("actT_ready"), e + 1)
                    pe.wait_ge(S(f"down_ld{half}"), turns * 16 + 16)
                    for h, moved in ((0, "y_act"), (1, "y_dve")):
                        wait(pe, moved, e)
                        product(B[6 + h][:, :], [(actT[:, half, j * P:j * P + P], wd[:, half, j, h * 512:h * 512 + 512])
                                                 for j in range(2)]).then_inc(S("y_done"), 1)

                def four(i):
                    for n in range(4):
                        gate_up(i, n)
                        if is_expert(i, n + 1):
                            turn_x(i, n + 1)
                        if is_expert(i, n - 1):
                            down(i, n - 1)
                        turn_act(i, n)

                turn_x(0, 0)
                over_fours(pe, four)
                down(NE // 4 - 1, 3)
                end_stage(pe, f"experts{l}")
                more = pe.value_load(more_i[0:1, 0:1], min_val=0, max_val=OVB)
                with pe.If(more):
                    with pe.Fori(0, OVB) as i:
                        step = S(f"more_step{l}")
                        pe.wait_ge(S(f"more_dma{l}"), i * 32 + 16)
                        for b in range(2):
                            for k in range(4):
                                ins = turn(B[b][:, k * P:k * P + P], xg[:, 0, 4 * b + k::KD])
                        ins.then_inc(step, 1)
                        pe.wait_ge(step, i * MORE_STEPS + 5)
                        pe.wait_ge(S(f"more_w{l}"), i * 48 + 48)
                        for w, c0 in ((wg, 0), (wu, DE)):
                            ins = product(B[2][:, c0:c0 + DE], [(xgT[:, 0, k * P:k * P + P], w[:, 0, k, :]) for k in range(KD)])
                        ins.then_inc(step, 1)
                        pe.wait_ge(step, i * MORE_STEPS + 8)
                        for j in range(2):
                            ins = turn(B[4][:, j * P:j * P + P], act_[:, 0, j::2])
                        ins.then_inc(step, 1)
                        pe.wait_ge(step, i * MORE_STEPS + 10)
                        for h in range(2):
                            ins = product(B[6 + h][:, :], [(actT[:, 0, j * P:j * P + P], wd[:, 0, j, h * 512:h * 512 + 512]) for j in range(2)])
                        ins.then_inc(step, 1)
                end_stage(pe, f"more{l}")
                if l == 0:
                    for j in range(HALF, 2 * HALF):
                        mod1(j)
                end_stage(pe, f"combine{l}")
            pe.drain()

        @block.vector
        def _(dve):
            link = linker(dve, "dve_chain")

            def tt(dst, x, y, op, name="dve_chain"):
                link(dve.tensor_tensor(dst, x, y, op), name)

            def ts(dst, x, s1_, s2_, op0, op1=None, name="dve_chain"):
                link(dve.tensor_scalar(dst, x, s1_, s2_, op0, op1) if op1 is not None
                     else dve.tensor_scalar(dst, x, s1_, s2_, op0), name)

            def stt(dst, x, s_, y, op0, op1, name="dve_chain"):
                link(dve.scalar_tensor_tensor(out=dst, in0=x, scalar=s_, in1=y, op0=op0, op1=op1), name)

            def red(dst, x, op, name="dve_chain"):
                link(dve.tensor_reduce(dst, x, AX, op), name)

            def copy(dst, x, name="dve_chain"):
                link(dve.tensor_copy(dst, x), name)

            def mean_square(q, n, width):
                ts(ss[:, 0:n], ss[:, 0:n], 1.0 / width, EPS, ALU.mult, ALU.add, "ms")
                dve.wait_ge(S("rstd"), 1 + before("rstd", q))

            def norm(q, which):
                nt = norm_tiles[q]
                dve.wait_ge(S("ss"), nt + before("ss", q))
                mean_square(q, nt, D)
                for t in range(1, nt, 2):
                    ts(xn[:, t, :], X[:, t, :], rstd[:, t:t + 1], None, ALU.mult, name="xn_dve")
                for k in range(1, KD, 2):
                    dve.wait_ge(S("xT"), k + 1 + before("xT", q))
                    for s in range(nt // 2):
                        ts(hT[:, k, s * H:s * H + H], B[k][:, s * H:s * H + H], mscale[:, which, k, s:s + 1],
                           modT[:, 2 * which, k, s:s + 1], ALU.mult, ALU.add, "hT_dve")

            def conv(u, src, w0, nch, c, name):
                x = src.rearrange("p (s w) -> p s w", s=2)
                u = u.rearrange("p (s w) -> p s w", s=2)
                ts(u, x[:, :, 0:H], VT[:, w0 + c:w0 + c + 1], VT[:, w0 + 4 * nch + c:w0 + 4 * nch + c + 1], ALU.mult, ALU.add)
                for j in range(1, 4):
                    stt(u, x[:, :, j:j + H], VT[:, w0 + j * nch + c:w0 + j * nch + c + 1], u, ALU.mult, ALU.add,
                        name if j == 3 else "dve_chain")

            def rope(x, bank, tmp, name):
                tt(tmp, bank[:, 0:H], C["sin"], ALU.mult)
                tt(x, x, C["cos"], ALU.mult)
                tt(x, x, tmp, ALU.add, name)

            dve.wait_ge(S("ld_small"), 16 * N_SMALL)
            dve.wait_ge(S("v_turned"), 1)
            copy(VT[:], B[7][:, 0:V_ROWS])
            ts(hbr, VT[:, V_BR:V_BR + 8], 0.5, None, ALU.mult)
            ts(hbi, VT[:, V_BI:V_BI + 8], 0.5, None, ALU.mult)
            ts(sink8, sinkb, 1.0 / SCALE, None, ALU.mult)
            ts(subg[:], subg[:], 1.0 - LAM_INIT, None, ALU.mult)
            for l in range(DEPTH):
                nt = NT if l == 0 else NL
                cat = catA if l == 0 else catC
                if l == 0:
                    dve.wait_ge(S("ld_bmod"), 16)
                    dve.sem_inc(S("mod_rows"), 2)
                    with dve.Fori(0, 6) as i:
                        for j in range(2):
                            dve.wait_ge(S("stream_free"), i * 2 + (j + 3))
                            row = modrow[:, bass.ds(i * 1024 + j * 512, 512)]
                            dve.tensor_tensor(row, B[j][0:2, :], row, ALU.add).then_inc(S("mod_rows"), 1)
                else:
                    dve.wait_ge(S("ld_bmod"), 48)
                    dve.tensor_tensor(modrow, modrow, modbias, ALU.add).then_inc(S("mod_rows"), 1)
                dve.wait_ge(S("mod_turned"), 1 + before("mod_turned", l))
                copy(modT[:].rearrange("p v k s -> p (v k s)"), B[2][:, 0:8 * KD], "modT")
                for w in range(2):
                    stt(mscale[:, w], modT[:, 2 * w + 1], 1.0, bc(gvec[:, w, l, :], 2, 2), ALU.add, ALU.mult)
                end_stage(dve, f"mod{l}")
                norm(2 * l, 0)
                end_stage(dve, f"norm1{l}")
                if l == 0:
                    dve.wait_ge(S("pads_zeroed"), 1)
                    for n in range(1, 14, 2):
                        dve.wait_ge(S("proj0"), n + 1)
                        src = B[n % 8][:, :]
                        if n < 8:
                            dst = catA[:, n, :]
                        elif n < 12:
                            dst = xap[:, n - 8, :].rearrange("p (s w) -> p s w", s=2)[:, :, 1:1 + H]
                            src = src.rearrange("p (s w) -> p s w", s=2)
                        else:
                            dst, src = vA, src.rearrange("p (t d) -> p t d", t=NT)
                        copy(dst, src, "proj0_dve")
                    end_stage(dve, "proj0")
                    for m in range(5):
                        dve.wait_ge(S("swapped0"), m + 1)
                        x = catA[:, 4 + m, 0:H] if m < 4 else ktmp[:, 0:H]
                        rope(x, B[m], rec[:, 0, 0:H], "rope0")
                    for c in range(4):
                        conv(uA[:, c, :], xap[:, c, :], V_CONVW, 4, c, "conv0")
                    lam = VT[:, V_LAM:V_LAM + 8]
                    stt(tmpc[:, 0:8], lam, -1.0, lam, ALU.mult, ALU.max, "lam_abs")
                    dve.wait_ge(S("lam_ln"), 1)
                    ts(tmpc[:, 24:32], lam, -1.0, 0.0, ALU.mult, ALU.max)
                    tt(tmpc[:, 24:32], tmpc[:, 24:32], tmpc[:, 16:24], ALU.add)
                    ts(lsc, tmpc[:, 24:32], -LRU_C / 2, None, ALU.mult)
                    ts(lnsc, tmpc[:, 24:32], LRU_C / 2, None, ALU.mult, name="lsc_ready")
                    for d in range(2):
                        for c in range(4):
                            n = d * 4 + c
                            dve.wait_ge(S("lru_th"), n + 1)
                            dve.wait_ge(S("lru_a"), n + 1)
                            tt(ktmp, a4[:, c, :], a4[:, c, :], ALU.mult)
                            stt(m4[:, c, :], ktmp, 1.0, m4[:, c, :], ALU.add, ALU.mult, "lru_m")
                            dve.wait_ge(S("lru_i"), n + 1)
                            stt(z4[:, c, :], z4[:, c, :], 1.0, uA[:, c, :], ALU.add, ALU.mult)
                        for c in range(4):
                            n = d * 4 + c
                            dve.wait_ge(S("lru_sq"), n + 1)
                            tt(z4[:, c, :], z4[:, c, :], m4[:, c, :], ALU.mult)
                            if d == 0:
                                link(dve.tensor_tensor_scan(rec[:, c, H:T], a4[:, c, H:T], z4[:, c, H:T], 0.0, ALU.mult, ALU.add))
                                link(dve.tensor_tensor_scan(rec[:, c, 0:H], a4[:, c, 0:H], z4[:, c, 0:H], rec[:, c, T - 1:T],
                                                            ALU.mult, ALU.add), "scan_done")
                            else:
                                link(dve.tensor_tensor_scan(m4[:, c, ::-1], a4[:, c, ::-1], z4[:, c, ::-1], 0.0, ALU.mult, ALU.add))
                                tt(rec[:, c, :], rec[:, c, :], m4[:, c, :], ALU.add)
                                dve.wait_ge(S("gelu"), 4)
                                tt(catA[:, c, :], catA[:, c, :], rec[:, c, :], ALU.mult)
                    end_stage(dve, "lru0")
                    for n in range(8 * NT + 3):
                        if n < 8 * NT:
                            nk = T if n < 8 * NL else CTX
                            dve.wait_ge(S("scores0"), n + 1)
                            red(tmpc[:, 32:33], B[n % 2][:, 0:nk], ALU.max)
                            ts(nmx[:, n:n + 1], tmpc[:, 32:33], sink8[:, n % 8:n % 8 + 1], -SCALE, ALU.max, ALU.mult, "nmax0")
                        if 0 < n <= 8 * NT:
                            m = n - 1
                            nk = T if m < 8 * NL else CTX
                            dve.wait_ge(S("p_turned"), m + 1)
                            wait(dve, "pv_done", (m - 1) // 8)
                            wait(dve, "pv_step", m - 1 - (m - 1) // 8)
                            copy(pTA[:, m % 2, 0:nk], B[2 + m % 2][:, 0:nk], "pT_ready")
                        if n > 2 and n % 8 == 2:
                            qt = n // 8 - 1
                            tt(tmpc[:, 0:8], nmx[:, qt * 8:qt * 8 + 8], sinkb, ALU.add, "sink_in")
                            dve.wait_ge(S("sink_exp"), qt + 1)
                            tt(tmpc[:, 16:24], tmpc[:, 8:16], rsum[:, qt * 8:qt * 8 + 8], ALU.add)
                            link(dve.reciprocal(tmpc[:, 24:32], tmpc[:, 16:24]))
                            dve.wait_ge(S("pv_done"), qt + 1)
                            wait(dve, "att_turned", qt)
                            tt(attA.rearrange("p (h d) -> p h d", h=8), B[4 + qt % 2][:, :].rearrange("p (h d) -> p h d", h=8),
                               bc(tmpc[:, 24:32], 2, 64), ALU.mult, "att_ready")
                    dve.wait_ge(S("att_turned"), NT)
                    end_stage(dve, "attn0")
                else:
                    dve.wait_ge(S("pads_zeroed"), 2)
                    for n in range(1, len(proj1), 2):
                        dve.wait_ge(S("proj1"), n + 1)
                        dst, src = proj1_move(n)
                        copy(dst, src, "proj1_dve")
                    end_stage(dve, "proj1")
                    tt(dt_[:], dtraw, bc(dtb, 1, NT), ALU.add)
                    stt(dta[:], dt_[:], -1.0, dt_[:], ALU.mult, ALU.max)
                    for i in range(2):
                        tt(tmpc[:, 0:64], lamv[:, 128 * i:128 * i + 64], lamv[:, 128 * i + 64:128 * i + 128], ALU.mult)
                        red(lamc[:, i:i + 1], tmpc[:, 0:64], ALU.add, "dve_chain" if i == 0 else "dt_in")
                    for c in range(8):
                        conv(hT[:, c, :], xbc[:, c, :], V_DCONVW, 8, c, "conv1")
                    for m in range(8):
                        dve.wait_ge(S("swapped1"), m + 1)
                        rope(qC[:, m, :] if m < 4 else kC[:, m - 4, 0:H], B[m], ropeC, "rope1")
                    dve.wait_ge(S("dt_ln"), 1)
                    stt(dt_[:], dt_[:], 0.0, dta[:], ALU.max, ALU.add)
                    stt(dta[:], dt_[:], -1.0, bc(alog, 1, NT), ALU.mult, ALU.mult)
                    tt(lamc[:, 2:3], lamc[:, 1:2], lamc[:, 0:1], ALU.subtract)
                    ts(lamc[:, 2:3], lamc[:, 2:3], -LAM_INIT, None, ALU.add)
                    end_stage(dve, "conv1")

                    def weights(u):
                        dve.wait_ge(S("p1_ready"), 2 * u + 2)
                        link(dve.reciprocal(tmpc[:, 0:2], rsum[:, 2 * u:2 * u + 2]))
                        tt(tmpc[:, 2:3], tmpc[:, 1:2], lamc[:, 2:3], ALU.mult)
                        p0, p1 = pC[:, 2 * (u % 2), :], pC[:, 2 * (u % 2) + 1, :]
                        ts(p0, p0, tmpc[:, 0:1], None, ALU.mult)
                        stt(p0, p1, tmpc[:, 2:3], p0, ALU.mult, ALU.add, "w_ready1")

                    for u in range(4 * NL + 1):
                        if u < 4 * NL:
                            for m in range(2):
                                n = 2 * u + m
                                dve.wait_ge(S("scores1"), n + 1)
                                red(tmpc[:, 4:5], B[n % 2][:, :], ALU.max)
                                ts(nmx[:, n:n + 1], tmpc[:, 4:5], -SCALE, None, ALU.mult, name="nmax1")
                        if u:
                            weights(u - 1)
                            if u % 4 == 0:
                                qt = u // 4 - 1
                                dve.wait_ge(S("pv1_done"), qt + 1)
                                wait(dve, "o_turned", qt)
                                copy(oC, B[4 + qt][:, :])
                                tt(sqC, oC, oC, ALU.mult)
                                red(ss, sqC.rearrange("p (h e) -> p h e", h=4), ALU.add)
                                mean_square(f"d{qt}", 4, P)
                                o3 = oC.rearrange("p (h e) -> p h e", h=4)
                                tt(o3, o3, bc(rstd, 2, P), ALU.mult)
                                tt(o3, o3, bc(subg[:], 1, 4), ALU.mult, "o_ready")
                                dve.wait_ge(S("o_turned"), qt + 1) if qt == NL - 1 else None
                    for qt in range(NL):
                        copy(catC[:, 0:4, qt * P:qt * P + P], B[6 + qt][:, :].rearrange("p (c q) -> p c q", c=4))
                    end_stage(dve, "attn1")
                    flat = "p t h -> p (t h)"
                    dve.wait_ge(S("acum_mm"), 1)
                    copy(acum[:].rearrange(flat), B[0][:, 0:NT * 16])
                    ts(nac_, acum[:].rearrange(flat), -1.0, None, ALU.mult)
                    copy(etot[:].rearrange(flat), B[1][:, 0:NT * 16])
                    tt(tend[:], etot[:], acum[:], ALU.subtract, "acum_ready")
                    dve.wait_ge(S("cb_mm"), 1)
                    copy(cbT.rearrange("p a b -> p (a b)"), B[2][:, :], "ssd_moved")
                    for t in range(NT):
                        dve.wait_ge(S("ssd_turned"), t + 1)
                        copy(xtok[:, t, :], B[3 + t][:, :], "ssd_moved")
                    for i in range(2):
                        dve.wait_ge(S("ssd_turned"), NT + i + 1)
                        copy(btok[:, 2 * i:2 * i + 2, :].rearrange("p a b -> p (a b)"), (B[7] if i == 0 else B[0])[:, :], "ssd_moved")
                    dve.wait_ge(S("acum_exp"), 1)
                    tt(tend[:], tend[:], dt_[:], ALU.mult)
                    by_head = "p (h d) -> p h d"
                    for c in range(NL):
                        tt(yacc[:, c, :].rearrange(by_head, h=8), xtok[:, c, :].rearrange(by_head, h=8), bc(dskip, 2, 64), ALU.mult)
                    n_seg = n_state = n_inter = 0
                    for d in range(2):
                        hd = slice(8 * d, 8 * d + 8)
                        tri, mask = (C["tri_le"], C["mask_lo"]) if d == 0 else (C["tri_ge"], C["mask_hi"])
                        for idx, t in enumerate(chunks(d)):
                            x3 = xtok[:, t, :].rearrange(by_head, h=8)
                            if t < NL:
                                wait(dve, "y_mm", n_seg)
                                tt(xdt.rearrange(by_head, h=8), x3, bc(dt_[:, t, hd], 2, 64), ALU.mult)
                                for g in range(2):
                                    h0 = 8 * d + 4 * g
                                    tt(tri_dta.rearrange("p (r q) -> p r q", r=4), bc(tri, 1, 4), bc(dta[:, t, h0:h0 + 4], 2, P),
                                       ALU.mult, "tri_dta")
                                    dve.wait_ge(S("seg_mm"), n_seg + 1)
                                    wait(dve, "y_mm", n_seg)
                                    for r in range(4):
                                        col = t * 16 + h0 + r
                                        stt(seg[:, r * P:r * P + P], B[3 + g][:, r * P:r * P + P], nac_[:, col:col + 1], mask,
                                            ALU.add, ALU.add, "seg_ready" if r == 3 else "dve_chain")
                                    dve.wait_ge(S("seg_exp"), n_seg + 1)
                                    s3 = seg.rearrange("p (r q) -> p r q", r=4)
                                    tt(s3, s3, bc(cbT[:, 2 * t + g, :], 1, 4), ALU.mult, "w_ready")
                                    n_seg += 1
                                n_inter += 1
                                dve.wait_ge(S("inter_mm"), n_inter)
                                tt(ytmp.rearrange(by_head, h=8), B[5][:, :].rearrange(by_head, h=8), bc(eac[:, t, hd], 2, 64), ALU.mult)
                                tt(yacc[:, t, :], yacc[:, t, :], ytmp, ALU.add)
                            if idx < 3:
                                tt(xte.rearrange(by_head, h=8), x3, bc(tend[:, t, hd], 2, 64), ALU.mult, "xte_ready")
                                n_state += 1
                                dve.wait_ge(S("state_mm"), n_state)
                                if idx == 0:
                                    copy(Hst, B[2][:, :], "H_ready")
                                else:
                                    tt(Hst.rearrange(by_head, h=8), Hst.rearrange(by_head, h=8), bc(etot[:, t, hd], 2, 64), ALU.mult)
                                    tt(Hst, Hst, B[2][:, :], ALU.add, "H_ready")
                    dve.wait_ge(S("y_mm"), n_seg)
                    for c in range(NL):
                        y = yacc[:, c, :]
                        tt(y, y, B[6 + c][:, :], ALU.add)
                        tt(y, y, zC[:, c, :], ALU.mult)
                        tt(ytmp, y, y, ALU.mult)
                        red(ss[:, 0:2], ytmp.rearrange("p (g e) -> p g e", g=2), ALU.add)
                        mean_square(f"s{c}", 2, 256)
                        y2 = y.rearrange("p (g e) -> p g e", g=2)
                        tt(y2, y2, bc(rstd[:, 0:2], 2, 256), ALU.mult)
                        dve.wait_ge(S("ld_normg"), 16)
                        tt(y, y, normg[:], ALU.mult, "ssd_y")
                    for c in range(NL):
                        dve.wait_ge(S("ssd_y_turned"), c + 1)
                        copy(catC[:, 4:8, c * P:c * P + P], B[3 + c][:, :].rearrange("p (m q) -> p m q", m=4))
                    end_stage(dve, "ssd1")
                outtmp = hT[:, 0, :]
                for h in range(2):
                    for t in range(nt):
                        n = h * nt + t
                        dve.wait_ge(S("out"), n + 1 + before("out", l))
                        tt(outtmp, B[n][:, :], G[:, 0, t // 2, h * 512:h * 512 + 512], ALU.mult)
                        xs = X[:, t, h * 512:h * 512 + 512]
                        tt(xs, xs, outtmp, ALU.add)
                end_stage(dve, f"out{l}")
                norm(2 * l + 1, 1)
                for t in range(nt):
                    dve.wait_ge(S("row_turned"), 2 * t + 2 + before("row_turned", l))
                    copy(row_half(t, 1), B[2 * t + 1][:, :].rearrange("q (k p) -> q k p", k=4), "hrow_dve")
                end_stage(dve, f"norm2{l}")

                dve.wait_ge(S("ld_router"), 32 + before("ld_router", l))
                dve.wait_ge(S("scores"), 1 + before("scores", l))
                ohk = "p (k e) -> p k e"
                for t in range(nt):
                    tt(selv, scores[:, t, :], router_b[:], ALU.add)
                    for g in range(NG):
                        link(dve.max(srt[:, g, :], selv[:, 8 * g:8 * g + 8]), wait=(g == NG - 1))
                    tt(gsc, srt[:, :, 0], srt[:, :, 1], ALU.add)
                    link(dve.max(gtop, gsc))
                    link(dve.max_index(i8, gtop, gsc))
                    copy(gidx, i8)
                    tt(goh, bc(C["iota"][:, 0:NG], 1, TOPG), bc(gidx[:, 0:TOPG], 2, NG), ALU.is_equal)
                    red(gmask, goh.rearrange("p a g -> p g a"), ALU.max)
                    s3 = selv.rearrange("p (g e) -> p g e", g=NG)
                    tt(s3, s3, bc(gmask, 2, 8), ALU.mult)
                    ts(gmask, gmask, 1.0, -NEG, ALU.subtract, ALU.mult)
                    tt(s3, s3, bc(gmask, 2, 8), ALU.add)
                    link(dve.max(top8, selv))
                    link(dve.max_index(i8, top8, selv))
                    copy(idx8, i8)
                    o3 = oh[:, t, :].rearrange(ohk, k=TOPK)
                    tt(o3, bc(C["iota"][:, 0:NE], 1, TOPK), bc(idx8, 2, NE), ALU.is_equal)
                    red(Msel[:, t, :], oh[:, t, :].rearrange("p (k e) -> p e k", k=TOPK), ALU.add, "Msel")
                    tt(ohtmp.rearrange(ohk, k=TOPK), o3, bc(scores[:, t, :], 1, TOPK), ALU.mult)
                    red(gates[:, t, :], ohtmp.rearrange(ohk, k=TOPK), ALU.add)
                    red(c8[:, 0:1], gates[:, t, :], ALU.add)
                    link(dve.reciprocal(c8[:, 1:2], c8[:, 0:1]))
                    ts(gates[:, t, :], gates[:, t, :], c8[:, 1:2], SCALED, ALU.mult, ALU.mult)
                for m in range(2):
                    dve.wait_ge(S("shared_silu"), m + 1 + before("shared_silu", l))
                    dve.wait_ge(S("shared_gu"), 2 * m + 2 + before("shared_gu", l))
                    tt(actS[:, m, 0:nt * P], sS[:, m, 0:nt * P], B[5 + 2 * m][:, 0:nt * P], ALU.mult, "act_shared")
                dve.wait_ge(S("ranks"), 1 + before("ranks", l))
                copy(rank[:, 0:nt, :].rearrange("p t e -> p (t e)"), B[1][:, 0:nt * NE])
                copy(cnt, B[2][:, 0:NE])
                ts(t64a, cnt, 128.0, None, ALU.is_gt)
                stt(t64a, cnt, 256.0, t64a, ALU.is_gt, ALU.add)
                stt(t64a, cnt, 384.0, t64a, ALU.is_gt, ALU.add)
                link(dve.tensor_tensor_scan(ends, C["ones"][:, 0:NE], t64a, 0.0, ALU.mult, ALU.add))
                tt(v1, ends, t64a, ALU.subtract)
                tt(v1, v1, C["iota"][:, 0:NE], ALU.subtract)
                ts(v1, v1, float(NE - 1), None, ALU.add)
                copy(more_i[:], ends[:, NE - 1:NE])
                ts(t64b, ends, C["pcol"], None, ALU.is_le)
                red(s1[:, 1:2], t64b, ALU.add)
                ts(s1[:, 0:1], s1[:, 1:2], float(NE - 1), None, ALU.min, name="more_col")
                dve.wait_ge(S("more_row"), 1 + before("more_row", l))
                copy(moree_i[:], B[0][0:1, 0:P])
                for t in range(nt):
                    o3 = oh[:, t, :].rearrange(ohk, k=TOPK)
                    m3 = ohtmp.rearrange(ohk, k=TOPK)
                    tt(m3, o3, bc(rank[:, t, :], 1, TOPK), ALU.mult)
                    red(r8, m3, ALU.add)
                    tt(m3, o3, bc(v1, 1, TOPK), ALU.mult)
                    red(q8, m3, ALU.add)
                    tt(m3, o3, bc(C["iota"][:, 0:NE], 1, TOPK), ALU.mult)
                    red(idx8, m3, ALU.add)
                    ts(b8, r8, 128.0, None, ALU.is_ge)
                    copy(c8, b8)
                    stt(b8, r8, 256.0, b8, ALU.is_ge, ALU.add)
                    stt(b8, r8, 384.0, b8, ALU.is_ge, ALU.add)
                    tt(q8, q8, c8, ALU.mult)
                    tt(q8, q8, b8, ALU.add)
                    tt(q8, q8, idx8, ALU.add)
                    stt(r8, b8, -128.0, r8, ALU.mult, ALU.add)
                    wait(dve, "table", t, before("table", l))
                    tt(lo_oh, bc(C["iota"], 1, TOPK), bc(r8, 2, P), ALU.is_equal)
                    tt(hi_oh, bc(C["iota"][:, 0:NCOL], 1, TOPK), bc(q8, 2, NCOL), ALU.is_equal)
                    tt(hi_oh, hi_oh, bc(C["rowid"][:, t * TOPK:(t + 1) * TOPK], 2, NCOL), ALU.mult, "onehot")
                    for h in range(2):
                        n = 2 * t + h
                        dve.wait_ge(S("shared_y"), n + 1 + before("shared_y", l))
                        tt(ohtmp, B[4 + n % 4][:, :], G[:, 1, t // 2, h * 512:h * 512 + 512], ALU.mult, "shared_out")
                        xs = X[:, t, h * 512:h * 512 + 512]
                        tt(xs, xs, ohtmp, ALU.add)
                dve.wait_ge(S("table"), nt + before("table", l))
                copy(tabf, B[3][:, 0:NCOL])
                ts(tab2, tabf, 0.5, BIG, ALU.is_lt, ALU.mult)
                stt(tabf, tabf, -1.0, tab2, ALU.add, ALU.add)
                copy(rows_i[:], tabf)
                ts(toks_i[:], rows_i[:], 3, None, ALU.logical_shift_right)
                end_stage(dve, f"route{l}")

                def x_evac(i, n):
                    e, half, _, _, _ = nth(l, i, n)
                    dve.wait_ge(S("x_turned"), e * 2 + 2)
                    dve.tensor_copy(xgT[:, half, 512:1024], B[1][:, :]).then_inc(S("xgT_dve"), 1)

                def y_evac(i, n):
                    e, _, _, slot, turns = nth(l, i, n)
                    dve.wait_ge(S("y_done"), e * 2 + 2)
                    wait(dve, f"y_stored{slot}", turns * 16)
                    dve.tensor_copy(ysb[:, slot, 512:1024], B[7][:, :]).then_inc(S("y_dve"), 1)

                def four(i):
                    for n in range(4):
                        e, half, _, _, _ = nth(l, i, n)
                        dve.wait_ge(S("sg_ready"), e + 1)
                        dve.tensor_tensor(act_[:, half, :], sg[:, half, :], B[2 + half][:, DE:2 * DE], ALU.mult).then_inc(S("act_ready"), 1)
                        if is_expert(i, n + 1):
                            x_evac(i, n + 1)
                        if is_expert(i, n - 1):
                            y_evac(i, n - 1)
                        dve.wait_ge(S("act_turned"), e + 1)
                        dve.tensor_copy(actT[:, half, :], B[4 + half][:, 0:2 * P]).then_inc(S("actT_ready"), 1)

                x_evac(0, 0)
                over_fours(dve, four)
                y_evac(NE // 4 - 1, 3)
                end_stage(dve, f"experts{l}")
                more = dve.value_load(more_i[0:1, 0:1], min_val=0, max_val=OVB)
                with dve.If(more):
                    with dve.Fori(0, OVB) as i:
                        step = S(f"more_step{l}")
                        dve.wait_ge(step, i * MORE_STEPS + 3)
                        for b in range(2):
                            dve.tensor_copy(xgT[:, 0, b * 512:b * 512 + 512], B[b][:, :]).then_inc(step, 1)
                        dve.wait_ge(step, i * MORE_STEPS + 7)
                        dve.tensor_tensor(act_[:, 0, :], sg[:, 0, :], B[2][:, DE:2 * DE], ALU.mult).then_inc(step, 1)
                        dve.wait_ge(step, i * MORE_STEPS + 9)
                        dve.tensor_copy(actT[:, 0, :], B[4][:, 0:2 * P]).then_inc(step, 1)
                        dve.wait_ge(step, i * MORE_STEPS + 11)
                        for b in range(2):
                            dve.tensor_copy(ysb[:, 0, b * 512:b * 512 + 512], B[6 + b][:, :]).then_inc(step, 1)
                end_stage(dve, f"more{l}")
                for t in range(nt):
                    for q in range(2):
                        dve.wait_ge(S(f"ych_ld{q}"), 16 * (t + 1) + 16 * NT * l)
                        for k in range(4):
                            y, w = ych[:, q, k * D:(k + 1) * D], gates[:, t, 4 * q + k:4 * q + k + 1]
                            name = "ych_used" if k == 3 else "dve_chain"
                            if q == 0 and k == 0:
                                ts(acc, y, w, None, ALU.mult)
                            else:
                                stt(acc, y, w, acc, ALU.mult, ALU.add, name)
                    tt(acc, acc, G[:, 1, t // 2, :], ALU.mult)
                    tt(X[:, t, :], X[:, t, :], acc, ALU.add)
                end_stage(dve, f"combine{l}")
            dve.wait_ge(S("ss"), NL + before("ss", 4))
            mean_square(4, NL, D)
            dve.wait_ge(S("ld_gfin"), 16)
            for t in range(NL):
                stt(xn[:, t, :], X[:, t, :], rstd[:, t:t + 1], G[:, 0, 0, :], ALU.mult, ALU.mult, "out_ready")
            dve.drain()


_INS = ["x", "c", "ctx", "c_ctx", "w_mod", "b_mod", "g_mix", "g_ffn", "g_final", "ab_w_in", "ab_w_out", "ab_conv_w",
        "ab_conv_b", "ab_w_r", "ab_b_r", "ab_w_i", "ab_b_i", "ab_lam", "ab_sink", "cd_w_in", "cd_w_out", "cd_lam",
        "cd_subln_g", "cd_conv_w", "cd_conv_b", "cd_dt_bias", "cd_a_log", "cd_d_skip", "cd_norm_g", "w_router",
        "b_router", "w_e_gate", "w_e_up", "w_e_down", "ws_gate", "ws_up", "ws_down"]


def kernel(**inputs):
    import concourse.bacc as bacc
    from concourse.bass_utils import run_bass_kernel_spmd

    nc = bacc.Bacc("TRN2", target_bir_lowering=False, num_devices=1)
    arrays, aps = {}, {}
    for name in _INS:
        arrays[f"in_{name}"] = np.ascontiguousarray(inputs[name])
    arrays["in_con"] = const_table()
    arrays["in_sel"] = select_rows()
    for name, v in arrays.items():
        aps[name[3:]] = nc.dram_tensor(name, v.shape, mybir.dt.from_np(v.dtype), kind="ExternalInput").ap()
    out = nc.dram_tensor("out_0", (1, SEQ, D), F32, kind="ExternalOutput").ap()
    build(nc, aps, out)
    r = run_bass_kernel_spmd(nc, [arrays], core_ids=[0])
    return r.results[0]["out_0"]
```

```python
from contextlib import ExitStack
import math

import numpy as np

import concourse.bass as bass
from concourse import mybir

F32 = mybir.dt.float32
I32 = mybir.dt.int32
U32 = mybir.dt.uint32
ALU = mybir.AluOpType
ACT = mybir.ActivationFunctionType
AX = mybir.AxisListType.X

P = 128
D = 1024
KD = D // P
SEQ = 256
CTX = 256
T = SEQ + CTX
NT = T // P
NL = SEQ // P
DEPTH = 2
EPS = 1e-6
NE = 64
NG = 8
TOPG = 4
TOPK = 8
DE = 256
SCALED = 2.5
OVB = 32
MORE_STEPS = 13
NCOL = NE + OVB
BIG = float(1 << 20)
NEG = -1e30
SPLIT = 896
SCALE = 0.125
LAM_INIT = 0.8 - 0.6 * math.exp(-0.3)
GRID_W = 64
H = SEQ
PADW = SEQ + 3
LRU_C = 8.0


def chunks(d):
    return (2, 3, 0, 1) if d == 0 else (3, 2, 1, 0)


STAGES = []
for _l in range(DEPTH):
    STAGES += [f"{n}{_l}" for n in (
        ("mod", "norm1", "proj", "lru", "attn", "out") if _l == 0 else
        ("mod", "norm1", "proj", "conv", "attn", "ssd", "out"))]
    STAGES += [f"{n}{_l}" for n in ("norm2", "route", "experts", "more", "combine")]

CONSTS = ["ident", "swap", "cos", "sin", "tri_le", "tri_ge", "tri_lt", "ones", "mask_lo", "mask_hi",
          "iota", "rowid", "pcol"]
CWID = dict(cos=SEQ, sin=SEQ, rowid=NT * TOPK, pcol=1)


def const_columns():
    at, n = {}, 0
    for c in CONSTS:
        w = CWID.get(c, P)
        at[c] = (n, n + w)
        n += w
    return at, n


def const_table():
    at, n = const_columns()
    t = np.zeros((P, n), np.float32)

    def put(name, a):
        t[:, at[name][0]:at[name][1]] = a

    r = np.arange(P)
    put("ident", np.eye(P))
    put("swap", np.eye(P)[(r // 64) * 64 + (r % 64 + 32) % 64])
    half = 16
    inv = (np.float32(10000.0) ** (-np.arange(half, dtype=np.float32) / np.float32(half))).astype(np.float32)
    tok = np.arange(SEQ)
    row, col = (tok // GRID_W).astype(np.float32), (tok % GRID_W).astype(np.float32)
    ang = np.concatenate([row[:, None] * inv, col[:, None] * inv], axis=-1).astype(np.float32)
    put("cos", np.cos(ang).T[r % 32])
    put("sin", np.sin(ang).T[r % 32] * np.where(r % 64 < 32, -1.0, 1.0)[:, None])
    a, b = r[:, None], r[None, :]
    put("tri_le", a <= b)
    put("tri_ge", a >= b)
    put("tri_lt", a < b)
    put("ones", 1.0)
    put("mask_lo", np.where(b < a, NEG, 0.0))
    put("mask_hi", np.where(b > a, NEG, 0.0))
    put("iota", np.broadcast_to(b, (P, P)))
    k = np.arange(NT * TOPK)[None, :]
    put("rowid", ((k // TOPK) * P + a) * TOPK + k % TOPK + 1)
    put("pcol", a)
    return t


V_CONVW, V_CONVB, V_BR, V_BI, V_LAM, V_DCONVW, V_DCONVB = 0, 16, 20, 28, 36, 44, 76
V_ROWS = 84
N_SMALL = 1 + 2 * DEPTH + 7 + 6


def build(nc, a, out):
    at, ncon = const_columns()
    ctx = ExitStack()
    with ctx:
        def sb(name, shape, dt=F32):
            return ctx.enter_context(nc.sbuf_tensor(name, shape, dt))

        sems = {}

        def S(name):
            if name not in sems:
                sems[name] = ctx.enter_context(nc.semaphore(name))
            return sems[name]

        X = sb("X", [P, NT, D])
        hT = sb("hT", [P, KD, T])
        G = sb("G", [P, 2, 2, D])
        stream = sb("stream", [P, 2, KD, 512])
        wg = sb("wg", [P, 2, KD, DE])
        wu = sb("wu", [P, 2, KD, DE])
        wd = sb("wd", [P, 2, 2, D])
        con = sb("con", [P, ncon])
        C = {n: con[:, at[n][0]:at[n][1]] for n in CONSTS}
        VT = sb("VT", [P, V_ROWS])
        craw = sb("craw", [P, 2, KD])
        csT = sb("csT", [P, KD, 2])
        gvec = sb("gvec", [P, 2, DEPTH, KD])
        modT = sb("modT", [P, 4, KD, 2])
        mscale = sb("mscale", [P, 2, KD, 2])
        half_exp = sb("half_exp", [P, 8])
        router_w = sb("router_w", [P, KD, NE])
        router_b = sb("router_b", [P, NE])
        gates = sb("gates", [P, NT, TOPK])
        small = sb("small", [P, 320])
        rows_i = sb("rows_i", [P, NCOL], I32)
        toks_i = sb("toks_i", [P, NCOL], I32)
        gat_i = sb("gat_i", [P, 4], I32)
        sca_i = sb("sca_i", [P, 4], I32)
        more_i = sb("more_i", [P, 1], I32)
        moree_i = sb("moree_i", [1, P], I32)
        RW = 14336
        R = sb("R", [P, RW])
        B = [ctx.enter_context(nc.psum_tensor(f"B{i}", [P, 512], F32)) for i in range(8)]

        h_rows = nc.dram_tensor("h_rows", (T, D), F32, kind="Internal").ap()
        mod_dram = nc.dram_tensor("mod_dram", (DEPTH, 2, 6 * D), F32, kind="Internal").ap()
        y_rows = nc.dram_tensor("y_rows", (T * TOPK, D), F32, kind="Internal").ap()

        def rv(off, *dims):
            n = math.prod(dims)
            assert off + n <= RW
            v = R[:, off:off + n]
            if len(dims) == 2:
                return v.rearrange("p (a b) -> p a b", b=dims[1])
            if len(dims) == 3:
                return v.rearrange("p (a b c) -> p a b c", b=dims[1], c=dims[2])
            return v

        def bc(ap, axis, n):
            v = ap.unsqueeze(axis)
            shape = list(v.shape)
            shape[axis] = n
            return v.to_broadcast(shape)

        gate_rows = [G, rv(9216, 2, 1, D)]
        gate_bias = [wd[:, 1], rv(11264, 2, D)]
        mod_cols = rv(13312, 2, 4, KD)
        mod_cols_bias = rv(13376, 4, KD)
        xn = rv(0, NT, D)
        vraw = R[0:V_ROWS, 0:P]
        catA = rv(0, 8, T)
        bdiag = rv(4096, 16, P)
        kd = rv(6144, 2, T)
        ktmp = rv(7168, T)
        vA = rv(7680, NT, P)
        xap = rv(8192, 4, 2 * PADW)
        uA = hT[:, 0:4, :]
        rec = hT[:, 4:8, :]
        a4, m4, z4 = rv(8192, 4, T), rv(10240, 4, T), rv(12288, 4, T)
        pA, pTA, attA = rv(8192, 2, T), rv(9216, 2, T), rv(10240, 512)
        catC = rv(0, 8, SEQ)
        qC = rv(2048, 4, SEQ)
        zC = rv(3072, NL, 512)
        kC = rv(4096, 4, T)
        vC = rv(6144, NT, 512)
        xbc = rv(8192, 8, 2 * PADW)
        ropeC = rv(12336, SEQ)
        dtraw = rv(12592, NT, 16)
        dtw = rv(12656, KD, 16)
        pC = rv(8192, 4, T)
        wTC = rv(10240, 2, T)
        oC = rv(11264, 512)
        sqC = rv(11776, 512)
        xtok = rv(8192, NT, 512)
        btok = rv(10240, NT, 256)
        cbT = rv(11264, 4, P)
        seg = rv(11776, 2, 512)
        xdt = rv(12800, 2, 512)
        tri_dta = rv(4096, 2, 512)
        xte = rv(5120, 512)
        Hst = rv(5632, 512)
        yacc = rv(6144, NL, 512)
        ytmp = rv(7168, 512)
        oh = rv(4096, NT, TOPK * NE)
        lo_oh = rv(6144, TOPK, P)
        hi_oh = rv(7168, TOPK, NCOL)
        ohtmp = rv(6144, NT * TOPK * NE)
        shtmp = rv(7936, 512)
        actS = rv(8448, 2, T)
        sS = rv(9472, 2, T)
        scores = rv(10496, NT, NE)
        Msel = rv(10752, NT, NE)
        rank = rv(11008, NT, NE)
        cnt = rv(11264, NE)
        tabf = rv(11328, NCOL)
        tab2 = rv(11424, NCOL)
        selv = rv(11520, NT, NE)
        srt = rv(11776, NT * NG, 8)
        t64a, t64b = srt[:, 0:8, :].rearrange("p a b -> p (a b)"), srt[:, 8:16, :].rearrange("p a b -> p (a b)")
        ends, v1 = srt[:, 16:24, :].rearrange("p a b -> p (a b)"), srt[:, 24:32, :].rearrange("p a b -> p (a b)")
        small_route = [12032]

        def of_tiles(*dims):
            small_route[0] += math.prod(dims)
            assert small_route[0] <= 12288
            return rv(small_route[0] - math.prod(dims), *dims)

        gsc, top8 = of_tiles(NT, 8), of_tiles(NT, 8)
        gidx, gmask = of_tiles(NT, 8), of_tiles(NT, 8)
        idx8, r8, q8 = of_tiles(NT, 8), of_tiles(NT, 8), of_tiles(NT, 8)
        b8 = gsc
        c8 = gidx
        s1 = of_tiles(8)
        goh = ohtmp[:, 0:NT * TOPG * NG].rearrange("p (t a g) -> p t a g", t=NT, a=TOPG)
        i8 = ohtmp[:, NT * TOPG * NG:NT * (TOPG * NG + 8)].rearrange("p (t k) -> p t k", t=NT).bitcast(U32)
        sdown = rv(12288, 2, D)
        xg = rv(0, 4, D)
        xgT = rv(4096, 2, D)
        ysb = rv(6144, 4, D)
        sg = rv(10240, 2, DE)
        act_ = rv(10752, 2, DE)
        actT = rv(11264, 2, 2 * P)
        ych = rv(0, 2, 4 * D)
        acc = rv(8192, D)

        ss = small[:, 0:4]
        rstd = small[:, 4:8]
        nmx = small[:, 8:40]
        rsum = small[:, 40:72]
        sinkb = small[:, 72:80]
        sink8 = small[:, 80:88]
        lsc = small[:, 88:96]
        lnsc = small[:, 96:104]
        hbr = small[:, 104:112]
        hbi = small[:, 112:120]
        dskip = small[:, 120:128]
        alog = small[:, 128:144]
        dtb = small[:, 144:160]
        lamc = small[:, 160:168]
        tmpc = small[:, 168:232]
        nac_ = small[:, 232:296]
        dt_ = sb("dt_", [P, NT, 16])
        dta = sb("dta", [P, NT, 16])
        acum = sb("acum", [P, NT, 16])
        eac = sb("eac", [P, NT, 16])
        tend = sb("tend", [P, NT, 16])
        etot = sb("etot", [P, NT, 16])
        subg = sb("subg", [P, P])
        normg = sb("normg", [P, 512])
        mod_stage = normg[0:2, :]
        lamv = sb("lamv", [P, 256])

        stage_no = {s: i for i, s in enumerate(STAGES)}

        def end_stage(eng, name):
            eng.drain().then_inc(S("stage_ended"), 1)
            eng.wait_ge(S("stage_ended"), 4 * (stage_no[name] + 1))

        def after_stage(eng, name):
            eng.wait_ge(S("stage_ended"), 4 * (stage_no[name] + 1))

        def linker(eng, own):
            count = {}

            def link(ins, name=own, wait=True):
                ins.then_inc(S(name), 1)
                count[name] = count.get(name, 0) + 1
                if wait:
                    eng.wait_ge(S(name), count[name])
                return count[name]
            return link

        def wait(eng, name, value, earlier=0):
            if not (isinstance(value, int) and value <= 0):
                eng.wait_ge(S(name), value + earlier)

        def nth(l, i, n):
            e = i * 4 + (n + NE * l)
            return e, n % 2, i * 2 + (n // 2 + NE // 2 * l), n % 4, i + (n // 4 + NE // 4 * l)

        def is_expert(i, n):
            return not isinstance(i, int) or 0 <= 4 * i + n < NE

        def over_fours(eng, body):
            body(0)
            with eng.Fori(1, NE // 4 - 1) as i:
                body(i)
            body(NE // 4 - 1)

        def combine(eng, link, l, c0, c1):
            nt = NT if l == 0 else NL
            name = "ych_used" if eng is nc.vector else "ych_pool"
            a_ = acc[:, c0:c1]
            for t in range(nt):
                for q in range(2):
                    eng.wait_ge(S(f"ych_ld{q}"), 16 * (t + 1) + 16 * NT * l)
                    for k in range(4):
                        y, w = ych[:, q, k * D + c0:k * D + c1], gates[:, t, 4 * q + k:4 * q + k + 1]
                        if eng is nc.gpsimd:
                            link(eng.tensor_tensor(a_ if q == 0 and k == 0 else y, y, w.to_broadcast([P, c1 - c0]), ALU.mult))
                            if q or k:
                                link(eng.tensor_tensor(a_, a_, y, ALU.add), name if k == 3 else "pool_chain")
                        elif q == 0 and k == 0:
                            link(eng.tensor_scalar(a_, y, w, None, ALU.mult))
                        else:
                            ins = eng.scalar_tensor_tensor(out=a_, in0=y, scalar=w, in1=a_, op0=ALU.mult, op1=ALU.add)
                            if k == 3:
                                link(ins, name)
                            else:
                                link(ins)
                link(eng.tensor_tensor(a_, a_, G[:, 1, t // 2, c0:c1], ALU.mult))
                link(eng.tensor_tensor(X[:, t, c0:c1], X[:, t, c0:c1], a_, ALU.add))

        norm_tiles = [NT, NT, NT, NL, NL]

        first_layer = dict(
            ld_router=32, ld_shared=32, ld_sdown=16, hrow_act=NT, hrow_dve=NT, h_stored=16 * NT,
            ych_used=2 * NT, row_turned=2 * NT, logits=1, scores=1, shared_gu=4, shared_silu=2,
            ranks=1, more_col=1, more_row=1, act_shared=2,
            shared_out=2 * NT, shared_y=2 * NT, onehot=NT, rows_onehot=NT, table=NT, out=2 * NT)
        ms_order = [0, 1, 2, "d0", "d1", "s0", "s1", 3, 4]

        def before(name, key):
            if name in first_layer:
                return first_layer[name] * key
            if name in ("ms", "rstd"):
                return ms_order.index(key)
            per_tile = {"ss": 1.0, "xn_act": 0.5, "xn_dve": 0.5, "hT_act": 2.0, "hT_dve": 2.0}
            if name == "xT":
                return KD * key
            return int(per_tile[name] * sum(norm_tiles[:key]))

        SEGS = [(d, t, g) for d in range(2) for t in chunks(d)[2:] for g in range(2)]

        proj1 = ([("q", 0, m) for m in range(4)] + [("z", 1, t) for t in range(NL)]
                 + [("k", 2, m) for m in range(4)] + [("v", 3, t) for t in range(NT)]
                 + [("xbc", 4, m) for m in range(4)] + [("xbc", 5, 4 + m) for m in range(4)]
                 + [("dt", None, 0)])

        def row_half(t, half):
            return xn[:, t, :].rearrange("q (p k) -> q k p", k=KD)[:, 4 * half:4 * half + 4, :]

        def proj1_move(n):
            kind, _, m = proj1[n]
            bank = B[n % 8]
            if kind == "q":
                return qC[:, m, :], bank[:, 0:SEQ]
            if kind == "xbc" and m >= 6:
                return xbc[:, m, 1:1 + H], bank[:, 0:H]
            if kind == "xbc":
                return (xbc[:, m, :].rearrange("p (s w) -> p s w", s=2)[:, :, 1:1 + H],
                        bank[:, :].rearrange("p (s w) -> p s w", s=2))
            if kind == "dt":
                return dtraw, bank[:, 0:NT * 16].rearrange("p (t h) -> p t h", t=NT)
            return {"z": zC, "k": kC, "v": vC}[kind][:, m, :], bank[:, :]

        n_in = [4, 6]
        MOD1_LRU, MOD1_ATT, MOD1_NORM, MOD1_ROUTE, MOD1_COMBINE = ((0,), (1,), (2, 3, 4)), 5, 6, range(7, 8), range(8, 12)
        order = ([("mod0", j) for j in range(12)] + [("in0", j) for j in range(n_in[0])]
                 + [("mod1", j) for j in range(6)] + [("out0", 0), ("out0", 1), ("mod1", MOD1_NORM), ("shared0", 0)]
                 + [("mod1", j) for j in [*MOD1_ROUTE, *MOD1_COMBINE]] + [("in1", j) for j in range(n_in[1])]
                 + [("out1", 0), ("out1", 1), ("shared1", 0)])
        first_in, first_out, first_shared = (
            [order.index((f"{n}{l}", 0)) for l in range(DEPTH)] for n in ("in", "out", "shared"))
        mod1_blocks = [order.index(("mod1", j)) for j in range(12)]

        def mod1_bank(j):
            return B[3 * (j % 2) if j in MOD1_ROUTE else 6 + j % 2]

        def loads_before(s):
            return sum(1 for b in range(s % 2, s + 1, 2) if b not in first_shared)

        block = ctx.enter_context(nc.Block())

        @block.sync
        def _(sp):
            def load_block(s, slot, src, ncols=512):
                sp.wait_ge(S("stream_free"), s + 1)
                sp.dma_start(stream[:, slot, :, 0:ncols], src).then_inc(S(f"stream_ld{slot}"), 16)

            def load_mod1(j):
                load_block(mod1_blocks[j], mod1_blocks[j] % 2,
                           a["w_mod"][1].rearrange("(p k) n -> p k n", k=KD)[:, :, j * 512:j * 512 + 512])

            def load_expert(l, i, n):
                e, slot, _, _, _ = nth(l, i, n)
                wait(sp, "gu_done", e - 1)
                el = i * 4 + n
                one = (lambda w: w[l, el]) if isinstance(i, int) else (lambda w: w[l, bass.ds(el, 1)].squeeze(0))
                sp.dma_start(wg[:, slot], one(a["w_e_gate"]).rearrange("(p k) f -> p k f", k=KD)).then_inc(S(f"gu_ld{slot}"), 16)
                sp.dma_start(wu[:, slot], one(a["w_e_up"]).rearrange("(p k) f -> p k f", k=KD)).then_inc(S(f"gu_ld{slot}"), 16)
                wait(sp, "y_done", e * 2 - 2)
                if l == 0 and isinstance(i, int) and i == 0 and n == 1:
                    sp.wait_ge(S("gates_ready"), 4)
                sp.dma_start(wd[:, slot], one(a["w_e_down"]).rearrange("(p j) n -> p j n", j=2)).then_inc(S(f"down_ld{slot}"), 16)

            def load_mod(l):
                sp.wait_ge(S("mod_stored"), 16 * 12 * (l + 1))
                b_mod = a["b_mod"][l]
                cols = "(v p k) -> p v k"
                for i, v in ((0, 0), (2, 3)):
                    for s in range(2):
                        sp.dma_start(mod_cols[:, s, i:i + 2, :],
                                     mod_dram[l, s].rearrange(cols, v=6, k=KD)[:, v:v + 2, :]).then_inc(S("ld_mod"), 16)
                    sp.dma_start(mod_cols_bias[:, i:i + 2, :], b_mod.rearrange(cols, v=6, k=KD)[:, v:v + 2, :]).then_inc(S("ld_mod"), 16)

            def load_gates(l):
                ns = 2 - l
                for gi in range(2):
                    c0 = (2 + 3 * gi) * D
                    for s in range(ns):
                        sp.dma_start(gate_rows[l][:, gi, s, :],
                                     mod_dram[l, s:s + 1, c0:c0 + D].to_broadcast([P, D])).then_inc(S("ld_gates"), 16)
                    sp.dma_start(gate_bias[l][:, gi, :], a["b_mod"][l:l + 1, c0:c0 + D].to_broadcast([P, D])).then_inc(S("ld_gates"), 16)

            sp.dma_start(craw[:, 0, :], a["c"][0, :].rearrange("(p k) -> p k", k=KD)).then_inc(S("ld_c"), 16)
            sp.dma_start(craw[:, 1, :], a["c_ctx"].rearrange("(p k) -> p k", k=KD)).then_inc(S("ld_c"), 16)
            w_mod = a["w_mod"][0].rearrange("(p k) n -> p k n", k=KD)
            for j in range(2):
                load_block(j, j, w_mod[:, :, j * 512:j * 512 + 512])

            def small_load(dst, src):
                sp.dma_start(dst, src).then_inc(S("ld_small"), 16)

            small_load(con[:], a["con"])
            for l in range(DEPTH):
                for i, n in enumerate(("g_mix", "g_ffn")):
                    small_load(gvec[:, i, l, :], a[n][l].rearrange("(p k) -> p k", k=KD))
            for src, r0 in ((a["ab_conv_w"][0], V_CONVW), (a["ab_conv_b"], V_CONVB), (a["ab_b_r"][0], V_BR),
                            (a["ab_b_i"][0], V_BI), (a["ab_lam"][0], V_LAM), (a["cd_conv_w"][0], V_DCONVW),
                            (a["cd_conv_b"], V_DCONVB)):
                rows = src.rearrange("r (c p) -> (r c) p", p=P)
                small_load(R[r0:r0 + rows.shape[0], 0:P], rows)
            for dst, src in ((sinkb, a["ab_sink"][0:1, :]), (dskip, a["cd_d_skip"][0:1, :]),
                             (alog, a["cd_a_log"].rearrange("a d h -> a (d h)")),
                             (dtb, a["cd_dt_bias"].rearrange("a d h -> a (d h)")),
                             (lamv[:], a["cd_lam"].rearrange("a d h -> a (d h)")),
                             (subg[:], a["cd_subln_g"][0:1, :])):
                small_load(dst, src.to_broadcast([P, src.shape[1]]))

            for l in range(DEPTH):
                nt = NT if l == 0 else NL
                if l:
                    after_stage(sp, f"combine{l - 1}")
                if l:
                    sp.dma_start(normg[:], a["cd_norm_g"][0:1, :].to_broadcast([P, 512])).then_inc(S("ld_normg"), 16)
                sp.dma_start(router_w[:], a["w_router"][l].rearrange("(p k) e -> p k e", k=KD)).then_inc(S("ld_router"), 16)
                sp.dma_start(router_b[:], a["b_router"][l:l + 1, :].to_broadcast([P, NE])).then_inc(S("ld_router"), 16)
                if l == 0:
                    with sp.Fori(1, 6) as i:
                        for j in range(2):
                            load_block(i * 2 + j, j, w_mod[:, :, bass.ds(i * 1024 + j * 512, 512)])
                    sp.dma_start(X[:, 0:NL, :], a["x"][0].rearrange("(t p) d -> p t d", p=P)).then_inc(S("ld_x"), 16)
                    sp.dma_start(X[:, NL:NT, :], a["ctx"][0].rearrange("(t p) d -> p t d", p=P)).then_inc(S("ld_x"), 16)
                    load_mod(0)
                s = first_in[l]
                w_in = (a["ab_w_in"] if l == 0 else a["cd_w_in"])[0].rearrange("(p k) n -> p k n", k=KD)
                for n in range(n_in[l]):
                    width = 256 if (l == 0 and n == 3) else 512
                    load_block(s, s % 2, w_in[:, :, n * 512:n * 512 + width], width)
                    s += 1
                    if n == 1 and l == 0:
                        load_gates(0)
                    if n == 1:
                        load_expert(l, 0, 0)
                        load_expert(l, 0, 1)
                        after_stage(sp, f"norm1{l}")
                        if l == 0:
                            sp.wait_ge(S("pads_zeroed"), 2)
                            for d in range(2):
                                for m, nm in enumerate(("ab_w_r", "ab_w_i")):
                                    src = a[nm][0, d].rearrange("(c b) i j -> b i c j", b=2)
                                    for b in range(2):
                                        q = d * 8 + m * 4
                                        sp.dma_start(bdiag[64 * b:64 * b + 64, q:q + 4, 64 * b:64 * b + 64],
                                                     src[b]).then_inc(S("ld_bdiag"), 16)
                        else:
                            sp.dma_start(dtw, w_in[:, :, 3072:3088]).then_inc(S("ld_dtw"), 16)
                if l == 0:
                    for j in range(6):
                        load_mod1(j)
                s = first_out[l]
                w_out = (a["ab_w_out"] if l == 0 else a["cd_w_out"])[0].rearrange("(k p) n -> p k n", p=P)
                for n in range(2):
                    load_block(s, s % 2, w_out[:, :, n * 512:n * 512 + 512])
                    s += 1
                if l == 0:
                    load_mod1(MOD1_NORM)
                    s += 1
                sp.wait_ge(S("stream_free"), s + 1)
                for n, nm in enumerate(("ws_gate", "ws_up")):
                    sp.dma_start(stream[:, s % 2, :, n * DE:(n + 1) * DE],
                                 a[nm][l].rearrange("(p k) n -> p k n", k=KD)).then_inc(S("ld_shared"), 16)
                for t in range(nt):
                    sp.wait_ge(S("hrow_act"), t + 1 + before("hrow_act", l))
                    sp.wait_ge(S("hrow_dve"), t + 1 + before("hrow_dve", l))
                    sp.dma_start(h_rows[t * P:(t + 1) * P, :], xn[:, t, :]).then_inc(S("h_stored"), 16)
                sp.dma_start(sdown, a["ws_down"][l].rearrange("(j p) n -> p j n", p=P)).then_inc(S("ld_sdown"), 16)
                if l == 0:
                    for j in [*MOD1_ROUTE, *MOD1_COMBINE[:2]]:
                        load_mod1(j)
                for n in range(2, 4):
                    load_expert(l, 0, n)
                with sp.Fori(1, NE // 4) as i:
                    for n in range(4):
                        load_expert(l, i, n)
                after_stage(sp, f"experts{l}")
                more = sp.value_load(more_i[0:1, 0:1], min_val=0, max_val=OVB)
                with sp.If(more):
                    with sp.Fori(0, OVB) as i:
                        e = sp.value_load(moree_i[0:1, bass.ds(i, 1)], min_val=0, max_val=NE - 1)
                        sp.wait_ge(S(f"more_step{l}"), i * MORE_STEPS + 2)
                        sp.dma_start(wg[:, 0], a["w_e_gate"][l, bass.ds(e, 1)].squeeze(0).rearrange("(p k) f -> p k f", k=KD)).then_inc(S(f"more_w{l}"), 16)
                        sp.dma_start(wu[:, 0], a["w_e_up"][l, bass.ds(e, 1)].squeeze(0).rearrange("(p k) f -> p k f", k=KD)).then_inc(S(f"more_w{l}"), 16)
                        sp.dma_start(wd[:, 0], a["w_e_down"][l, bass.ds(e, 1)].squeeze(0).rearrange("(p j) n -> p j n", j=2)).then_inc(S(f"more_w{l}"), 16)
                after_stage(sp, f"more{l}")
                yv = y_rows.rearrange("(t p q k) d -> t q p (k d)", p=P, q=2, k=4)
                for t in range(nt):
                    for q in range(2):
                        wait(sp, "ych_used", 2 * t + q - 1, before("ych_used", l))
                        wait(sp, "ych_pool", 2 * t + q - 1, before("ych_used", l))
                        sp.dma_start(ych[:, q, :], yv[t, q]).then_inc(S(f"ych_ld{q}"), 16)
                    if l == 0:
                        for j in MOD1_COMBINE[2 + t:3 + t]:
                            load_mod1(j)
                if l == 0:
                    load_mod(1)
                    load_gates(1)
            after_stage(sp, f"combine{DEPTH - 1}")
            sp.dma_start(G[:, 0, 0, :], a["g_final"].unsqueeze(0).to_broadcast([P, D])).then_inc(S("ld_gfin"), 16)
            for t in range(NL):
                sp.wait_ge(S("out_ready"), t + 1)
                sp.dma_start(out[0, t * P:(t + 1) * P, :], xn[:, t, :]).then_inc(S("out_stored"), 16)
            sp.wait_ge(S("out_stored"), 16 * NL)

        @block.gpsimd
        def _(pool):
            link = linker(pool, "pool_chain")

            def waited():
                pool.sem_inc(S("pool_waited"), 1)

            def add_gates(l):
                pool.wait_ge(S("ld_gates"), 16 * 6 if l == 0 else 16 * 10)
                for gi in range(2):
                    for s in range(2 - l):
                        link(pool.tensor_tensor(G[:, gi, s, :], gate_rows[l][:, gi, s, :], gate_bias[l][:, gi, :], ALU.add), "gates_ready")

            def rsqrt(q, n=4):
                pool.wait_ge(S("ms"), 1 + before("ms", q))
                pool.tensor_tensor(rstd[:, 0:n], ss[:, 0:n], half_exp[:, 0:n], ALU.pow).then_inc(S("rstd"), 1)

            link(pool.memset(half_exp[:], -0.5))
            for l in range(DEPTH):
                nt = NT if l == 0 else NL
                end_stage(pool, f"mod{l}")
                rsqrt(2 * l, NT)
                if l:
                    add_gates(l)
                end_stage(pool, f"norm1{l}")
                if l == 0:
                    link(pool.memset(xap, 0.0), "pads_zeroed")
                    link(pool.memset(bdiag, 0.0), "pads_zeroed")
                    add_gates(0)
                    for s in ("proj0", "lru0", "attn0", "out0"):
                        end_stage(pool, s)
                else:
                    link(pool.memset(xbc, 0.0), "pads_zeroed")
                    end_stage(pool, "proj1")
                    end_stage(pool, "conv1")
                    for qt in range(NL):
                        rsqrt(f"d{qt}")
                    end_stage(pool, "attn1")
                    by_head = "p (h d) -> p h d"

                    def decay(n):
                        d, t, g = SEGS[n]
                        hd = slice(8 * d, 8 * d + 8)
                        if g == 0:
                            wait(pool, "y_mm", n - 2)
                            link(pool.tensor_tensor(xdt[:, n // 2 % 2, :].rearrange(by_head, h=8), xtok[:, t, :].rearrange(by_head, h=8),
                                                    bc(dt_[:, t, hd], 2, 64), ALU.mult))
                        h0 = 8 * d + 4 * g
                        wait(pool, "seg_mm", n - 1)
                        link(pool.tensor_tensor(tri_dta[:, n % 2, :].rearrange("p (r q) -> p r q", r=4),
                                                bc(C["tri_le" if d == 0 else "tri_ge"], 1, 4),
                                                bc(dta[:, t, h0:h0 + 4], 2, P), ALU.mult), "tri_dta")

                    pool.wait_ge(S("ssd_moved"), 5)
                    decay(0)
                    pool.wait_ge(S("tend_ready"), 1)
                    for n, (d, t, g) in enumerate(SEGS):
                        k = n % 4
                        c = chunks(d)[k]
                        if k < 3:
                            wait(pool, "state_mm", 3 * d + k)
                            link(pool.tensor_tensor(xte.rearrange(by_head, h=8), xtok[:, c, :].rearrange(by_head, h=8),
                                                    bc(tend[:, c, 8 * d:8 * d + 8], 2, 64), ALU.mult), "xte_ready")
                        if n + 1 < len(SEGS):
                            decay(n + 1)
                    for c in range(NL):
                        rsqrt(f"s{c}", 2)
                    end_stage(pool, "ssd1")
                    end_stage(pool, "out1")
                rsqrt(2 * l + 1, nt)
                end_stage(pool, f"norm2{l}")
                pool.wait_ge(S("h_stored"), 16 * nt + before("h_stored", l))
                link(pool.memset(xg, 0.0))
                for t in range(nt):
                    pool.wait_ge(S("onehot"), t + 1 + before("onehot", l))
                    link(pool.tensor_tensor(hi_oh, hi_oh, bc(C["rowid"][:, t * TOPK:(t + 1) * TOPK], 2, NCOL), ALU.mult), "rows_onehot")
                end_stage(pool, f"route{l}")

                def gather(i, n):
                    e, _, _, slot, _ = nth(l, i, n)
                    if not is_expert(i, n):
                        return
                    wait(pool, "x_turned", e * 2 - 6)
                    waited()
                    pool.tensor_copy(gat_i[:, slot:slot + 1], toks_i[:, bass.ds(i * 4 + n, 1)]).then_inc(S("gat_idx"), 1)
                    pool.wait_ge(S("gat_idx"), e + 1)
                    waited()
                    pool.indirect_dma_start(out=xg[:, slot, :], out_offset=None, in_=h_rows,
                                            in_offset=bass.IndirectOffsetOnAxis(gat_i[:, slot:slot + 1], 0),
                                            bounds_check=nt * P - 1, oob_is_err=False).then_inc(S(f"xg_ld{slot}"), 16)

                def scatter(i, n):
                    e, _, _, slot, turns = nth(l, i, n)
                    if not is_expert(i, n):
                        return
                    wait(pool, f"y_stored{slot}", turns * 16)
                    waited()
                    pool.tensor_copy(sca_i[:, slot:slot + 1], rows_i[:, bass.ds(i * 4 + n, 1)]).then_inc(S("sca_idx"), 1)
                    pool.wait_ge(S("sca_idx"), e + 1)
                    pool.wait_ge(S("y_act"), e + 1)
                    pool.wait_ge(S("y_dve"), e + 1)
                    waited()
                    pool.indirect_dma_start(out=y_rows, out_offset=bass.IndirectOffsetOnAxis(sca_i[:, slot:slot + 1], 0),
                                            in_=ysb[:, slot, :], in_offset=None,
                                            bounds_check=nt * P * TOPK - 1, oob_is_err=False).then_inc(S(f"y_stored{slot}"), 16)

                def four(i):
                    for n in range(4):
                        gather(i, n + 3)
                        if is_expert(i, n - 1):
                            scatter(i, n - 1)

                for n in range(3):
                    gather(0, n)
                over_fours(pool, four)
                scatter(NE // 4 - 1, 3)
                for n in range(4):
                    pool.wait_ge(S(f"y_stored{n}"), 16 * (NE // 4) * (l + 1))
                end_stage(pool, f"experts{l}")
                more = pool.value_load(more_i[0:1, 0:1], min_val=0, max_val=OVB)
                with pool.If(more):
                    with pool.Fori(0, OVB) as i:
                        step = S(f"more_step{l}")
                        pool.tensor_copy(gat_i[:, 0:1], toks_i[:, bass.ds(i + NE, 1)]).then_inc(step, 1)
                        pool.tensor_copy(sca_i[:, 0:1], rows_i[:, bass.ds(i + NE, 1)]).then_inc(step, 1)
                        pool.wait_ge(step, i * MORE_STEPS + 2)
                        waited()
                        pool.indirect_dma_start(out=xg[:, 0, :], out_offset=None, in_=h_rows,
                                                in_offset=bass.IndirectOffsetOnAxis(gat_i[:, 0:1], 0),
                                                bounds_check=nt * P - 1, oob_is_err=False).then_inc(S(f"more_dma{l}"), 16)
                        pool.wait_ge(step, i * MORE_STEPS + 13)
                        waited()
                        pool.indirect_dma_start(out=y_rows, out_offset=bass.IndirectOffsetOnAxis(sca_i[:, 0:1], 0),
                                                in_=ysb[:, 0, :], in_offset=None,
                                                bounds_check=nt * P * TOPK - 1, oob_is_err=False).then_inc(S(f"more_dma{l}"), 16)
                        pool.wait_ge(S(f"more_dma{l}"), i * 32 + 32)
                end_stage(pool, f"more{l}")
                combine(pool, link, l, SPLIT, D)
                end_stage(pool, f"combine{l}")
            rsqrt(4, NL)
            pool.drain()

        @block.scalar
        def _(act):
            link = linker(act, "act_chain")

            def squares(q):
                for t in range(norm_tiles[q]):
                    link(act.activation(xn[:, t, :], X[:, t, :], ACT.Square, accum_out=ss[:, t:t + 1]), "ss")

            def norm(q, which):
                nt = norm_tiles[q]
                if which:
                    squares(q)
                if q == 1:
                    store_mod1(MOD1_NORM)
                act.wait_ge(S("rstd"), 1 + before("rstd", q))
                for t in range(0, nt, 2):
                    link(act.activation(xn[:, t, :], X[:, t, :], ACT.Copy, scale=rstd[:, t:t + 1]), "xn_act")
                for k in range(0, KD, 2):
                    act.wait_ge(S("xT"), k + 1 + before("xT", q))
                    for s in range(nt // 2):
                        link(act.activation(hT[:, k, s * H:s * H + H], B[k][:, s * H:s * H + H], ACT.Identity,
                                            scale=mscale[:, which, k, s:s + 1], bias=modT[:, 2 * which, k, s:s + 1]), "hT_act")

            def store_mod1(j):
                bank = mod1_bank(j)
                act.wait_ge(S("mod1_mm"), j + 1)
                act.wait_ge(S("mod_stored"), 16 * (12 + j))
                act.activation(mod_stage, bank[0:2, :], ACT.Copy).then_inc(S("mod_moved"), 1)
                act.wait_ge(S("mod_moved"), 2 + 12 + j + 1)
                act.dma_start(mod_dram[1, :, j * 512:j * 512 + 512], mod_stage).then_inc(S("mod_stored"), 16)

            act.sem_inc(S("mod_moved"), 2)
            act.wait_ge(S("ld_c"), 32)
            link(act.activation(csT[:].rearrange("p k s -> p s k"), craw[:], ACT.Silu), "c_silu")
            with act.Fori(0, 6) as i:
                for j in range(2):
                    act.wait_ge(S("stream_free"), i * 2 + (j + 3))
                    act.activation(mod_stage, B[j][0:2, :], ACT.Copy).then_inc(S("mod_moved"), 1)
                    act.wait_ge(S("mod_moved"), i * 2 + (j + 3))
                    act.dma_start(mod_dram[0, :, bass.ds(i * 1024 + j * 512, 512)], mod_stage).then_inc(S("mod_stored"), 16)
                    act.wait_ge(S("mod_stored"), i * 32 + (j * 16 + 16))
            act.wait_ge(S("ld_small"), 16 * N_SMALL)
            act.wait_ge(S("ld_x"), 32)
            act.wait_ge(S("v_turned"), 1)
            for l in range(DEPTH):
                nt = NT if l == 0 else NL
                squares(2 * l)
                end_stage(act, f"mod{l}")
                norm(2 * l, 0)
                end_stage(act, f"norm1{l}")
                if l == 0:
                    act.wait_ge(S("pads_zeroed"), 1)
                    for n in range(0, 14, 2):
                        act.wait_ge(S("proj0"), n + 1)
                        src = B[n % 8][:, :]
                        if n < 8:
                            dst = catA[:, n, :]
                        elif n < 12:
                            dst = xap[:, n - 8, :].rearrange("p (s w) -> p s w", s=2)[:, :, 1:1 + H]
                            src = src.rearrange("p (s w) -> p s w", s=2)
                        else:
                            dst = ktmp
                        link(act.activation(dst, src, ACT.Copy), "proj0_act")
                    end_stage(act, "proj0")
                    for m in range(4):
                        link(act.activation(catA[:, m, :], catA[:, m, :], ACT.Gelu_apprx_tanh), "gelu")
                    act.wait_ge(S("rope0"), 5)
                    for g in range(2):
                        for b in range(2):
                            link(act.activation(kd[64 * b:64 * b + 64, g, :], ktmp[64 * g:64 * g + 64, :], ACT.Copy))
                    act.wait_ge(S("lam_abs"), 1)
                    link(act.activation(tmpc[:, 8:16], tmpc[:, 0:8], ACT.Exp, scale=-1.0))
                    link(act.activation(tmpc[:, 16:24], tmpc[:, 8:16], ACT.Ln, bias=1.0), "lam_ln")
                    store_mod1(0)
                    act.wait_ge(S("lsc_ready"), 1)
                    for d in range(2):
                        for c in range(4):
                            n = d * 4 + c
                            if d:
                                act.wait_ge(S("scan_done"), c + 1)
                            act.wait_ge(S("lru_mm"), 2 * n + 1)
                            link(act.activation(a4[:, c, :], B[(2 * n) % 6][:, :], ACT.Tanh, scale=0.5, bias=hbr[:, n:n + 1]), "lru_r")
                            link(act.activation(m4[:, c, :], a4[:, c, :], ACT.Tanh, scale=lnsc[:, n:n + 1], bias=lnsc[:, n:n + 1]), "lru_th")
                            link(act.activation(a4[:, c, :], a4[:, c, :], ACT.Exp, scale=lsc[:, n:n + 1], bias=lsc[:, n:n + 1]), "lru_a")
                            act.wait_ge(S("lru_mm"), 2 * n + 2)
                            link(act.activation(z4[:, c, :], B[(2 * n + 1) % 6][:, :], ACT.Tanh, scale=0.5, bias=hbi[:, n:n + 1]), "lru_i")
                        for c in range(4):
                            n = d * 4 + c
                            act.wait_ge(S("lru_m"), n + 1)
                            link(act.activation(m4[:, c, :], m4[:, c, :], ACT.Sqrt, scale=0.25), "lru_sq")
                        for j in MOD1_LRU[1 + d]:
                            store_mod1(j)
                    end_stage(act, "lru0")
                    for n in range(8 * NT + 7):
                        if n < 8 * NT:
                            nk = T if n < 8 * NL else CTX
                            act.wait_ge(S("nmax0"), n + 1)
                            wait(act, "p_turned", n - 1)
                            link(act.activation(pA[:, n % 2, 0:nk], B[n % 2][:, 0:nk], ACT.Exp, scale=SCALE, bias=nmx[:, n:n + 1],
                                                accum_out=rsum[:, n:n + 1]), "p_ready")
                        if n == 1:
                            store_mod1(MOD1_ATT)
                        if n > 2 and n % 8 == 2:
                            act.wait_ge(S("sink_in"), n // 8)
                            link(act.activation(tmpc[:, 8:16], tmpc[:, 0:8], ACT.Exp), "sink_exp")
                        if n > 6 and n % 8 == 6:
                            qt = n // 8 - 1
                            act.wait_ge(S("att_turned"), qt + 1)
                            link(act.activation(catA[:, 4:8, qt * P:qt * P + P],
                                                B[6 + qt % 2][:, :].rearrange("p (c q) -> p c q", c=4), ACT.Copy), "att_cat")
                    end_stage(act, "attn0")
                    end_stage(act, "out0")
                else:
                    act.wait_ge(S("pads_zeroed"), 3)
                    for n in range(0, len(proj1), 2):
                        act.wait_ge(S("proj1"), n + 1)
                        dst, src = proj1_move(n)
                        link(act.activation(dst, src, ACT.Copy), "proj1_act")
                    end_stage(act, "proj1")
                    for c in range(8):
                        act.wait_ge(S("conv1"), c + 1)
                        link(act.activation(hT[:, c, :], hT[:, c, :], ACT.Silu))
                    link(act.activation(zC, zC, ACT.Silu))
                    act.wait_ge(S("dt_in"), 1)
                    link(act.activation(dta[:], dta[:], ACT.Exp, scale=-1.0))
                    link(act.activation(alog, alog, ACT.Exp))
                    link(act.activation(lamc[:, 0:2], lamc[:, 0:2], ACT.Exp))
                    link(act.activation(dta[:], dta[:], ACT.Ln, bias=1.0), "dt_ln")
                    end_stage(act, "conv1")
                    for u in range(4 * NL + 1):
                        if u < 4 * NL:
                            wait(act, "w_turned", u - 1)
                            for m in range(2):
                                n = 2 * u + m
                                act.wait_ge(S("nmax1"), n + 1)
                                link(act.activation(pC[:, 2 * (u % 2) + m, :], B[n % 2][:, :], ACT.Exp, scale=SCALE, bias=nmx[:, n:n + 1],
                                                    accum_out=rsum[:, n:n + 1]), "p1_ready")
                        if u:
                            act.wait_ge(S("w_turned"), u)
                            wait(act, "pv1_done", u - 2)
                            link(act.activation(wTC[:, (u - 1) % 2, :], B[2 + (u - 1) % 2][:, :], ACT.Copy), "wT_ready")
                    end_stage(act, "attn1")
                    act.wait_ge(S("acum_ready"), 1)
                    link(act.activation(eac[:], acum[:], ACT.Exp))
                    link(act.activation(tend[:], tend[:], ACT.Exp))
                    link(act.activation(etot[:], etot[:], ACT.Exp), "acum_exp")
                    for n in range(len(SEGS)):
                        act.wait_ge(S("seg_ready"), n + 1)
                        link(act.activation(seg[:, n % 2, :], seg[:, n % 2, :], ACT.Exp), "seg_exp")
                    end_stage(act, "ssd1")
                    end_stage(act, "out1")
                norm(2 * l + 1, 1)
                for t in range(nt):
                    act.wait_ge(S("row_turned"), 2 * t + 1 + before("row_turned", l))
                    link(act.activation(row_half(t, 0), B[2 * t][:, :].rearrange("q (k p) -> q k p", k=4), ACT.Copy), "hrow_act")
                end_stage(act, f"norm2{l}")
                act.wait_ge(S("logits"), 1 + before("logits", l))
                link(act.activation(scores[:, 0:nt, :], B[0][:, 0:nt * NE].rearrange("p (t e) -> p t e", e=NE), ACT.Sigmoid), "scores")
                for m in range(2):
                    act.wait_ge(S("shared_gu"), 2 * m + 1 + before("shared_gu", l))
                    link(act.activation(sS[:, m, 0:nt * P], B[4 + 2 * m][:, 0:nt * P], ACT.Silu), "shared_silu")
                if l == 0:
                    for j in MOD1_ROUTE:
                        store_mod1(j)
                end_stage(act, f"route{l}")

                def x_evac(i, n):
                    e, half, _, _, _ = nth(l, i, n)
                    act.wait_ge(S("x_turned"), e * 2 + 1)
                    act.activation(xgT[:, half, 0:512], B[0][:, :], ACT.Copy).then_inc(S("xgT_act"), 1)

                def y_evac(i, n):
                    e, _, _, slot, turns = nth(l, i, n)
                    act.wait_ge(S("y_done"), e * 2 + 1)
                    wait(act, f"y_stored{slot}", turns * 16)
                    act.activation(ysb[:, slot, 0:512], B[6][:, :], ACT.Copy).then_inc(S("y_act"), 1)

                def four(i):
                    for n in range(4):
                        e, half, _, _, _ = nth(l, i, n)
                        act.wait_ge(S("gu_done"), e + 1)
                        act.activation(sg[:, half, :], B[2 + half][:, 0:DE], ACT.Silu).then_inc(S("sg_ready"), 1)
                        if is_expert(i, n + 1):
                            x_evac(i, n + 1)
                        if is_expert(i, n - 1):
                            y_evac(i, n - 1)

                x_evac(0, 0)
                over_fours(act, four)
                y_evac(NE // 4 - 1, 3)
                end_stage(act, f"experts{l}")
                more = act.value_load(more_i[0:1, 0:1], min_val=0, max_val=OVB)
                with act.If(more):
                    with act.Fori(0, OVB) as i:
                        act.wait_ge(S(f"more_step{l}"), i * MORE_STEPS + 6)
                        act.activation(sg[:, 0, :], B[2][:, 0:DE], ACT.Silu).then_inc(S(f"more_step{l}"), 1)
                end_stage(act, f"more{l}")
                if l == 0:
                    for j in MOD1_COMBINE:
                        store_mod1(j)
                end_stage(act, f"combine{l}")
            squares(4)
            act.drain()

        @block.tensor
        def _(pe):
            def product(out, pairs, start=True):
                for n, (lhsT, rhs) in enumerate(pairs):
                    ins = pe.matmul(out, lhsT, rhs, start=(start and n == 0), stop=(n == len(pairs) - 1))
                return ins

            def turn(out, in_, n=P):
                return pe.transpose(out, in_, C["ident"][0:n, 0:n])

            def block_ready(s):
                pe.wait_ge(S(f"stream_ld{s % 2}"), 16 * loads_before(s))
                return stream[:, s % 2]

            def mod1(j):
                W = block_ready(mod1_blocks[j])
                pe.wait_ge(S("mod_moved"), 14 + j - 1)
                product(mod1_bank(j)[0:2, :], [(csT[:, k, :], W[:, k, :]) for k in range(KD)]).then_inc(S("mod1_mm"), 1)
                pe.drain().then_inc(S("stream_free"), 1)

            def norm(q):
                nt = norm_tiles[q]
                pe.wait_ge(S("xn_act"), nt // 2 + before("xn_act", q))
                pe.wait_ge(S("xn_dve"), nt // 2 + before("xn_dve", q))
                for k in range(KD):
                    for t in range(nt):
                        ins = turn(B[k][:, t * P:t * P + P], xn[:, t, k::KD])
                    ins.then_inc(S("xT"), 1)

            pe.sem_inc(S("stream_free"), 2)
            pe.wait_ge(S("c_silu"), 1)
            for l in range(DEPTH):
                nt = NT if l == 0 else NL
                cat = catA if l == 0 else catC
                if l == 0:
                    with pe.Fori(0, 6) as i:
                        for j in range(2):
                            pe.wait_ge(S(f"stream_ld{j}"), i * 16 + 16)
                            pe.wait_ge(S("mod_moved"), i * 2 + (j + 1))
                            product(B[j][0:2, :], [(csT[:, k, :], stream[:, j, k, :]) for k in range(KD)]).then_inc(S("stream_free"), 1)
                    pe.wait_ge(S("ld_small"), 16 * N_SMALL)
                    turn(B[7][:, 0:V_ROWS], vraw, V_ROWS).then_inc(S("v_turned"), 1)
                end_stage(pe, f"mod{l}")
                norm(2 * l)
                end_stage(pe, f"norm1{l}")
                if l == 0:
                    for n in range(14):
                        blk, m = n // 4, n % 4
                        if m == 0:
                            W = block_ready(first_in[0] + blk)
                        if n >= 8:
                            pe.wait_ge(S("proj0_act" if n % 2 == 0 else "proj0_dve"), (n - 8) // 2 + 1)
                        if n < 13:
                            ins = product(B[n % 8][:, :], [(W[:, k, m * P:m * P + P], hT[:, k, :]) for k in range(KD)])
                        else:
                            for t in range(NT):
                                ins = product(B[n % 8][:, t * P:t * P + P],
                                              [(hT[:, k, t * P:t * P + P], W[:, k, P:2 * P]) for k in range(KD)])
                        ins.then_inc(S("proj0"), 1)
                        if m == 3 or n == 13:
                            pe.drain().then_inc(S("stream_free"), 1)
                    end_stage(pe, "proj0")
                    for m in range(5):
                        src = catA[:, 4 + m, 0:H] if m < 4 else ktmp[:, 0:H]
                        pe.matmul(B[m][:, 0:H], C["swap"], src, start=True, stop=True).then_inc(S("swapped0"), 1)
                    mod1(0)
                    pe.wait_ge(S("ld_bdiag"), 16 * 8)
                    pe.wait_ge(S("rope0"), 5)
                    for d in range(2):
                        for c in range(4):
                            n = d * 4 + c
                            if d == 0:
                                pe.wait_ge(S("conv0"), c + 1)
                            wait(pe, "lru_r", n - 2)
                            pe.matmul(B[(2 * n) % 6][:, :], bdiag[:, d * 8 + c, :], uA[:, c, :], start=True, stop=True).then_inc(S("lru_mm"), 1)
                            wait(pe, "lru_i", n - 2)
                            pe.matmul(B[(2 * n + 1) % 6][:, :], bdiag[:, d * 8 + 4 + c, :], uA[:, c, :], start=True, stop=True).then_inc(S("lru_mm"), 1)
                        for j in MOD1_LRU[1 + d]:
                            mod1(j)
                    end_stage(pe, "lru0")

                    def att_turn(qt):
                        pe.wait_ge(S("att_ready"), qt + 1)
                        wait(pe, "att_cat", qt - 1)
                        for c in range(4):
                            ins = turn(B[6 + qt % 2][:, c * P:c * P + P], attA[:, c * P:c * P + P])
                        ins.then_inc(S("att_turned"), 1)

                    for n in range(8 * NT + 2):
                        if n < 8 * NT:
                            qt, h = n // 8, n % 8
                            b, g = 64 * (h % 2), h // 4
                            k0, nk = (0, T) if qt < NL else (SEQ, CTX)
                            wait(pe, "p_ready", n - 1)
                            masked = {0: P, 1: 0}.get(qt)
                            for c0, c1 in {0: ((0, P), (P, 2 * P), (2 * P, T)), 1: ((0, P), (P, T))}.get(qt, ((0, nk),)):
                                q_ap, k_ap = catA[b:b + 64, 4 + h // 2, qt * P:qt * P + P], kd[b:b + 64, g, k0 + c0:k0 + c1]
                                if c0 == masked:
                                    pe.matmul(B[n % 2][:, c0:c1], C["ident"], C["mask_hi" if qt == 0 else "mask_lo"],
                                              start=True, stop=False)
                                ins = pe.matmul(B[n % 2][:, c0:c1], q_ap, k_ap, start=(c0 != masked), stop=True)
                            ins.then_inc(S("scores0"), 1)
                        if n == 1:
                            mod1(MOD1_ATT)
                        if 0 < n <= 8 * NT:
                            m = n - 1
                            nk = NT if m < 8 * NL else NL
                            pe.wait_ge(S("p_ready"), m + 1)
                            wait(pe, "pT_ready", m - 1)
                            for t in range(nk):
                                ins = turn(B[2 + m % 2][:, t * P:t * P + P], pA[:, m % 2, t * P:t * P + P])
                            ins.then_inc(S("p_turned"), 1)
                        if n > 1:
                            m = n - 2
                            qt, h = m // 8, m % 8
                            nk, t0 = (NT, 0) if qt < NL else (NL, NL)
                            pe.wait_ge(S("pT_ready"), m + 1)
                            if h == 0:
                                wait(pe, "att_ready", qt - 1)
                            g = h // 4
                            ins = product(B[4 + qt % 2][:, h * 64:h * 64 + 64],
                                          [(pTA[:, m % 2, t * P:t * P + P], vA[:, t0 + t, g * 64:g * 64 + 64]) for t in range(nk)])
                            if h == 7:
                                ins.then_inc(S("pv_done"), 1)
                            else:
                                ins.then_inc(S("pv_step"), 1)
                            if h == 3 and qt:
                                att_turn(qt - 1)
                    att_turn(NT - 1)
                    end_stage(pe, "attn0")
                else:
                    for n, (kind, blk, m) in enumerate(proj1):
                        first = n == 0 or proj1[n - 1][1] != blk
                        last = n + 1 == len(proj1) or proj1[n + 1][1] != blk
                        if kind == "dt":
                            pe.wait_ge(S("ld_dtw"), 16)
                        elif first:
                            W = block_ready(first_in[1] + blk)
                        if n >= 8:
                            pe.wait_ge(S("proj1_act" if n % 2 == 0 else "proj1_dve"), (n - 8) // 2 + 1)
                        col = m % 4 * P
                        if kind == "q":
                            ins = product(B[n % 8][:, 0:SEQ], [(W[:, k, m * P:m * P + P], hT[:, k, 0:SEQ]) for k in range(KD)])
                        elif kind in "zv":
                            ins = product(B[n % 8][:, :], [(hT[:, k, m * P:m * P + P], W[:, k, :]) for k in range(KD)])
                        elif kind == "dt":
                            for t in range(NT):
                                ins = product(B[n % 8][:, t * 16:t * 16 + 16],
                                              [(hT[:, k, t * P:t * P + P], dtw[:, k, :]) for k in range(KD)])
                        else:
                            width = H if kind == "xbc" and m >= 6 else T
                            ins = product(B[n % 8][:, 0:width], [(W[:, k, col:col + P], hT[:, k, 0:width]) for k in range(KD)])
                        ins.then_inc(S("proj1"), 1)
                        if last and kind != "dt":
                            pe.drain().then_inc(S("stream_free"), 1)
                    end_stage(pe, "proj1")
                    for m in range(8):
                        src = qC[:, m, :] if m < 4 else kC[:, m - 4, 0:SEQ]
                        pe.matmul(B[m][:, 0:SEQ], C["swap"], src, start=True, stop=True).then_inc(S("swapped1"), 1)
                    end_stage(pe, "conv1")

                    def o_turn(qt):
                        pe.wait_ge(S("o_ready"), qt + 1)
                        for c in range(4):
                            ins = turn(B[6 + qt][:, c * P:c * P + P], oC[:, c * P:c * P + P])
                        ins.then_inc(S("o_turned"), 1)

                    for u in range(4 * NL + 2):
                        if u < 4 * NL:
                            qt, h = u // 4, u % 4
                            for m in range(2):
                                n = 2 * u + m
                                wait(pe, "p1_ready", n - 1)
                                pe.matmul(B[n % 2][:, :], qC[64 * m:64 * m + 64, h, qt * P:qt * P + P],
                                          kC[64 * m:64 * m + 64, h, :], start=True, stop=True).then_inc(S("scores1"), 1)
                        if 0 < u <= 4 * NL:
                            w = u - 1
                            pe.wait_ge(S("w_ready1"), w + 1)
                            wait(pe, "wT_ready", w - 1)
                            for t in range(NT):
                                ins = turn(B[2 + w % 2][:, t * P:t * P + P], pC[:, 2 * (w % 2), t * P:t * P + P])
                            ins.then_inc(S("w_turned"), 1)
                        if u > 1:
                            w = u - 2
                            qt, h = w // 4, w % 4
                            pe.wait_ge(S("wT_ready"), w + 1)
                            ins = product(B[4 + qt][:, h * P:h * P + P],
                                          [(wTC[:, w % 2, t * P:t * P + P], vC[:, t, h * P:h * P + P]) for t in range(NT)])
                            ins.then_inc(S("pv1_done"), 1)
                            if h == 2 and qt:
                                o_turn(qt - 1)
                    o_turn(NL - 1)
                    end_stage(pe, "attn1")
                    for t in range(NT):
                        pe.matmul(B[0][:, t * 16:t * 16 + 8], C["tri_le"], dta[:, t, 0:8], start=True, stop=True)
                        pe.matmul(B[0][:, t * 16 + 8:t * 16 + 16], C["tri_ge"], dta[:, t, 8:16], start=True, stop=True)
                        ins = pe.matmul(B[1][:, t * 16:t * 16 + 16], C["ones"], dta[:, t, :], start=True, stop=True)
                    ins.then_inc(S("acum_mm"), 1)
                    for c in range(NL):
                        for g in range(2):
                            ins = pe.matmul(B[2][:, (2 * c + g) * P:(2 * c + g) * P + P], hT[:, 4 + g, c * P:c * P + P],
                                            hT[:, 6 + g, c * P:c * P + P], start=True, stop=True)
                    ins.then_inc(S("cb_mm"), 1)
                    for t in range(NT):
                        for c in range(4):
                            ins = turn(B[3 + t][:, c * P:c * P + P], hT[:, c, t * P:t * P + P])
                        ins.then_inc(S("ssd_turned"), 1)
                    for t in range(NT):
                        bank = B[7] if t < 2 else B[0]
                        if t == 2:
                            pe.wait_ge(S("acum_ready"), 1)
                        for g in range(2):
                            o = (2 * (t % 2) + g) * P
                            ins = turn(bank[:, o:o + P], hT[:, 4 + g, t * P:t * P + P])
                        if t % 2:
                            ins.then_inc(S("ssd_turned"), 1)
                    pe.wait_ge(S("ssd_moved"), 7)

                    def decay(n):
                        pe.wait_ge(S("tri_dta"), n + 1)
                        wait(pe, "seg_ready", n - 1)
                        pe.matmul(B[3 + n % 2][:, :], C["ones"], tri_dta[:, n % 2, :], start=True, stop=True).then_inc(S("seg_mm"), 1)

                    decay(0)
                    for n, (d, t, g) in enumerate(SEGS):
                        k = n % 4
                        if k >= 2:
                            pe.wait_ge(S("H_ready"), 3 * d + k)
                            for gg in range(2):
                                ins = pe.matmul(B[5][:, gg * 256:gg * 256 + 256], hT[:, 6 + gg, chunks(d)[k] * P:chunks(d)[k] * P + P],
                                                Hst[:, gg * 256:gg * 256 + 256], start=True, stop=True)
                            ins.then_inc(S("inter_mm"), 1)
                        if k < 3:
                            pe.wait_ge(S("xte_ready"), 3 * d + k + 1)
                            wait(pe, "H_ready", 3 * d + k)
                            for gg in range(2):
                                ins = pe.matmul(B[2][:, gg * 256:gg * 256 + 256], btok[:, chunks(d)[k], gg * P:gg * P + P],
                                                xte[:, gg * 256:gg * 256 + 256], start=True, stop=True)
                            ins.then_inc(S("state_mm"), 1)
                        if n + 1 < len(SEGS):
                            decay(n + 1)
                        pe.wait_ge(S("w_ready"), n + 1)
                        for r in range(4):
                            h = 4 * g + r
                            ins = pe.matmul(B[6 + t][:, h * 64:h * 64 + 64], seg[:, n % 2, r * P:r * P + P],
                                            xdt[:, n // 2 % 2, h * 64:h * 64 + 64], start=(d == 0 and h == 0),
                                            stop=(d == 1 and h == 7), skip_group_check=True)
                        ins.then_inc(S("y_mm"), 1)
                    for c in range(NL):
                        pe.wait_ge(S("ssd_y"), c + 1)
                        for m in range(4):
                            ins = turn(B[3 + c][:, m * P:m * P + P], yacc[:, c, m * P:m * P + P])
                        ins.then_inc(S("ssd_y_turned"), 1)
                    end_stage(pe, "ssd1")
                for h in range(2):
                    W = block_ready(first_out[l] + h)
                    for t in range(nt):
                        ins = product(B[h * nt + t][:, :], [(cat[:, k, t * P:t * P + P], W[:, k, :]) for k in range(KD)])
                        ins.then_inc(S("out"), 1)
                    pe.drain().then_inc(S("stream_free"), 1)
                end_stage(pe, f"out{l}")
                q = 2 * l + 1
                if l == 0:
                    mod1(MOD1_NORM)
                    pe.wait_ge(S("mod_moved"), 14 + MOD1_NORM + 1)
                norm(q)
                pe.wait_ge(S("hT_act"), 4 * (nt // 2) + before("hT_act", q))
                pe.wait_ge(S("hT_dve"), 4 * (nt // 2) + before("hT_dve", q))
                for t in range(nt):
                    for half in range(2):
                        for k in range(4):
                            ins = turn(B[2 * t + half][:, k * P:k * P + P], hT[:, 4 * half + k, t * P:t * P + P])
                        ins.then_inc(S("row_turned"), 1)
                end_stage(pe, f"norm2{l}")
                pe.wait_ge(S("ld_router"), 32 + before("ld_router", l))
                for t in range(nt):
                    ins = product(B[0][:, t * NE:t * NE + NE], [(hT[:, k, t * P:t * P + P], router_w[:, k, :]) for k in range(KD)])
                ins.then_inc(S("logits"), 1)
                s = first_shared[l]
                pe.wait_ge(S("ld_shared"), 32 + before("ld_shared", l))
                for m in range(2):
                    for up in range(2):
                        c0 = up * DE + m * P
                        ins = product(B[4 + 2 * m + up][:, 0:nt * P],
                                      [(stream[:, s % 2, k, c0:c0 + P], hT[:, k, 0:nt * P]) for k in range(KD)])
                        ins.then_inc(S("shared_gu"), 1)
                    if m == 0:
                        pe.wait_ge(S("Msel"), l + 1)
                        for t in range(nt):
                            product(B[1][:, t * NE:t * NE + NE],
                                    [(C["tri_lt"], Msel[:, t, :])] + [(C["ones"], Msel[:, u, :]) for u in range(t)])
                        product(B[2][:, 0:NE], [(C["ones"], Msel[:, t, :]) for t in range(nt)]).then_inc(S("ranks"), 1)
                pe.drain().then_inc(S("stream_free"), 1)
                if l == 0:
                    for j in MOD1_ROUTE:
                        mod1(j)
                    pe.wait_ge(S("mod_moved"), 14 + MOD1_ROUTE[-1] + 1)
                pe.wait_ge(S("more_col"), 1 + before("more_col", l))
                turn(B[0][0:1, 0:P], s1[:, 0:1]).then_inc(S("more_row"), 1)
                pe.wait_ge(S("ld_sdown"), 16 + before("ld_sdown", l))
                pe.wait_ge(S("act_shared"), 2 + before("act_shared", l))
                for t in range(nt):
                    for h in range(2):
                        n = 2 * t + h
                        wait(pe, "shared_out", n - 3, before("shared_out", l))
                        ins = product(B[4 + n % 4][:, :], [(actS[:, j, t * P:t * P + P], sdown[:, j, h * 512:h * 512 + 512]) for j in range(2)])
                        ins.then_inc(S("shared_y"), 1)
                    pe.wait_ge(S("rows_onehot"), t + 1 + before("rows_onehot", l))
                    for k in range(TOPK):
                        ins = pe.matmul(B[3][:, 0:NCOL], lo_oh[:, k, :], hi_oh[:, k, :],
                                        start=(t == 0 and k == 0), stop=(t == nt - 1 and k == TOPK - 1), skip_group_check=True)
                    ins.then_inc(S("table"), 1)
                end_stage(pe, f"route{l}")

                def turn_x(i, n):
                    e, _, _, slot, turns = nth(l, i, n)
                    pe.wait_ge(S(f"xg_ld{slot}"), turns * 16 + 16)
                    for b, moved in ((0, "xgT_act"), (1, "xgT_dve")):
                        wait(pe, moved, e)
                        for k in range(4):
                            ins = turn(B[b][:, k * P:k * P + P], xg[:, slot, 4 * b + k::KD])
                        ins.then_inc(S("x_turned"), 1)

                def gate_up(i, n):
                    e, half, turns, _, _ = nth(l, i, n)
                    pe.wait_ge(S(f"gu_ld{half}"), turns * 32 + 32)
                    pe.wait_ge(S("xgT_act"), e + 1)
                    pe.wait_ge(S("xgT_dve"), e + 1)
                    for w, c0 in ((wg, 0), (wu, DE)):
                        ins = product(B[2 + half][:, c0:c0 + DE], [(xgT[:, half, k * P:k * P + P], w[:, half, k, :]) for k in range(KD)])
                    ins.then_inc(S("gu_done"), 1)

                def turn_act(i, n):
                    e, half, _, _, _ = nth(l, i, n)
                    pe.wait_ge(S("act_ready"), e + 1)
                    for j in range(2):
                        ins = turn(B[4 + half][:, j * P:j * P + P], act_[:, half, j::2])
                    ins.then_inc(S("act_turned"), 1)

                def down(i, n):
                    e, half, turns, _, _ = nth(l, i, n)
                    pe.wait_ge(S("actT_ready"), e + 1)
                    pe.wait_ge(S(f"down_ld{half}"), turns * 16 + 16)
                    for h, moved in ((0, "y_act"), (1, "y_dve")):
                        wait(pe, moved, e)
                        product(B[6 + h][:, :], [(actT[:, half, j * P:j * P + P], wd[:, half, j, h * 512:h * 512 + 512])
                                                 for j in range(2)]).then_inc(S("y_done"), 1)

                def four(i):
                    for n in range(4):
                        gate_up(i, n)
                        if is_expert(i, n + 1):
                            turn_x(i, n + 1)
                        if is_expert(i, n - 1):
                            down(i, n - 1)
                        turn_act(i, n)

                turn_x(0, 0)
                over_fours(pe, four)
                down(NE // 4 - 1, 3)
                end_stage(pe, f"experts{l}")
                more = pe.value_load(more_i[0:1, 0:1], min_val=0, max_val=OVB)
                with pe.If(more):
                    with pe.Fori(0, OVB) as i:
                        step = S(f"more_step{l}")
                        pe.wait_ge(S(f"more_dma{l}"), i * 32 + 16)
                        for b in range(2):
                            for k in range(4):
                                ins = turn(B[b][:, k * P:k * P + P], xg[:, 0, 4 * b + k::KD])
                        ins.then_inc(step, 1)
                        pe.wait_ge(step, i * MORE_STEPS + 5)
                        pe.wait_ge(S(f"more_w{l}"), i * 48 + 48)
                        for w, c0 in ((wg, 0), (wu, DE)):
                            ins = product(B[2][:, c0:c0 + DE], [(xgT[:, 0, k * P:k * P + P], w[:, 0, k, :]) for k in range(KD)])
                        ins.then_inc(step, 1)
                        pe.wait_ge(step, i * MORE_STEPS + 8)
                        for j in range(2):
                            ins = turn(B[4][:, j * P:j * P + P], act_[:, 0, j::2])
                        ins.then_inc(step, 1)
                        pe.wait_ge(step, i * MORE_STEPS + 10)
                        for h in range(2):
                            ins = product(B[6 + h][:, :], [(actT[:, 0, j * P:j * P + P], wd[:, 0, j, h * 512:h * 512 + 512]) for j in range(2)])
                        ins.then_inc(step, 1)
                end_stage(pe, f"more{l}")
                if l == 0:
                    for j in MOD1_COMBINE:
                        mod1(j)
                end_stage(pe, f"combine{l}")
            pe.drain()

        @block.vector
        def _(dve):
            link = linker(dve, "dve_chain")

            def tt(dst, x, y, op, name="dve_chain"):
                link(dve.tensor_tensor(dst, x, y, op), name)

            def ts(dst, x, s1_, s2_, op0, op1=None, name="dve_chain"):
                link(dve.tensor_scalar(dst, x, s1_, s2_, op0, op1) if op1 is not None
                     else dve.tensor_scalar(dst, x, s1_, s2_, op0), name)

            def stt(dst, x, s_, y, op0, op1, name="dve_chain"):
                link(dve.scalar_tensor_tensor(out=dst, in0=x, scalar=s_, in1=y, op0=op0, op1=op1), name)

            def red(dst, x, op, name="dve_chain"):
                link(dve.tensor_reduce(dst, x, AX, op), name)

            def copy(dst, x, name="dve_chain"):
                link(dve.tensor_copy(dst, x), name)

            def mean_square(q, n, width):
                ts(ss[:, 0:n], ss[:, 0:n], 1.0 / width, EPS, ALU.mult, ALU.add, "ms")
                dve.wait_ge(S("rstd"), 1 + before("rstd", q))

            def norm(q, which):
                nt = norm_tiles[q]
                dve.wait_ge(S("ss"), nt + before("ss", q))
                mean_square(q, nt, D)
                for t in range(1, nt, 2):
                    ts(xn[:, t, :], X[:, t, :], rstd[:, t:t + 1], None, ALU.mult, name="xn_dve")
                for k in range(1, KD, 2):
                    dve.wait_ge(S("xT"), k + 1 + before("xT", q))
                    for s in range(nt // 2):
                        ts(hT[:, k, s * H:s * H + H], B[k][:, s * H:s * H + H], mscale[:, which, k, s:s + 1],
                           modT[:, 2 * which, k, s:s + 1], ALU.mult, ALU.add, "hT_dve")

            def conv(u, src, w0, nch, c, name):
                x = src.rearrange("p (s w) -> p s w", s=2)
                u = u.rearrange("p (s w) -> p s w", s=2)
                ts(u, x[:, :, 0:H], VT[:, w0 + c:w0 + c + 1], VT[:, w0 + 4 * nch + c:w0 + 4 * nch + c + 1], ALU.mult, ALU.add)
                for j in range(1, 4):
                    stt(u, x[:, :, j:j + H], VT[:, w0 + j * nch + c:w0 + j * nch + c + 1], u, ALU.mult, ALU.add,
                        name if j == 3 else "dve_chain")

            def rope(x, bank, tmp, name):
                tt(tmp, bank[:, 0:H], C["sin"], ALU.mult)
                tt(x, x, C["cos"], ALU.mult)
                tt(x, x, tmp, ALU.add, name)

            dve.wait_ge(S("ld_small"), 16 * N_SMALL)
            dve.wait_ge(S("v_turned"), 1)
            copy(VT[:], B[7][:, 0:V_ROWS])
            ts(hbr, VT[:, V_BR:V_BR + 8], 0.5, None, ALU.mult)
            ts(hbi, VT[:, V_BI:V_BI + 8], 0.5, None, ALU.mult)
            ts(sink8, sinkb, 1.0 / SCALE, None, ALU.mult)
            ts(subg[:], subg[:], 1.0 - LAM_INIT, None, ALU.mult)
            for l in range(DEPTH):
                nt = NT if l == 0 else NL
                cat = catA if l == 0 else catC
                dve.wait_ge(S("ld_mod"), 16 * 6 * (l + 1))
                for s in range(2):
                    tt(modT[:, :, :, s], mod_cols[:, s], mod_cols_bias, ALU.add)
                for w in range(2):
                    stt(mscale[:, w], modT[:, 2 * w + 1], 1.0, bc(gvec[:, w, l, :], 2, 2), ALU.add, ALU.mult)
                end_stage(dve, f"mod{l}")
                norm(2 * l, 0)
                end_stage(dve, f"norm1{l}")
                if l == 0:
                    dve.wait_ge(S("pads_zeroed"), 1)
                    for n in range(1, 14, 2):
                        dve.wait_ge(S("proj0"), n + 1)
                        src = B[n % 8][:, :]
                        if n < 8:
                            dst = catA[:, n, :]
                        elif n < 12:
                            dst = xap[:, n - 8, :].rearrange("p (s w) -> p s w", s=2)[:, :, 1:1 + H]
                            src = src.rearrange("p (s w) -> p s w", s=2)
                        else:
                            dst, src = vA, src.rearrange("p (t d) -> p t d", t=NT)
                        copy(dst, src, "proj0_dve")
                    end_stage(dve, "proj0")
                    for m in range(5):
                        dve.wait_ge(S("swapped0"), m + 1)
                        x = catA[:, 4 + m, 0:H] if m < 4 else ktmp[:, 0:H]
                        rope(x, B[m], rec[:, 0, 0:H], "rope0")
                    for c in range(4):
                        conv(uA[:, c, :], xap[:, c, :], V_CONVW, 4, c, "conv0")
                    lam = VT[:, V_LAM:V_LAM + 8]
                    stt(tmpc[:, 0:8], lam, -1.0, lam, ALU.mult, ALU.max, "lam_abs")
                    dve.wait_ge(S("lam_ln"), 1)
                    ts(tmpc[:, 24:32], lam, -1.0, 0.0, ALU.mult, ALU.max)
                    tt(tmpc[:, 24:32], tmpc[:, 24:32], tmpc[:, 16:24], ALU.add)
                    ts(lsc, tmpc[:, 24:32], -LRU_C / 2, None, ALU.mult)
                    ts(lnsc, tmpc[:, 24:32], LRU_C / 2, None, ALU.mult, name="lsc_ready")
                    for d in range(2):
                        for c in range(4):
                            n = d * 4 + c
                            dve.wait_ge(S("lru_th"), n + 1)
                            dve.wait_ge(S("lru_a"), n + 1)
                            tt(ktmp, a4[:, c, :], a4[:, c, :], ALU.mult)
                            stt(m4[:, c, :], ktmp, 1.0, m4[:, c, :], ALU.add, ALU.mult, "lru_m")
                            dve.wait_ge(S("lru_i"), n + 1)
                            stt(z4[:, c, :], z4[:, c, :], 1.0, uA[:, c, :], ALU.add, ALU.mult)
                        for c in range(4):
                            n = d * 4 + c
                            dve.wait_ge(S("lru_sq"), n + 1)
                            tt(z4[:, c, :], z4[:, c, :], m4[:, c, :], ALU.mult)
                            if d == 0:
                                link(dve.tensor_tensor_scan(rec[:, c, H:T], a4[:, c, H:T], z4[:, c, H:T], 0.0, ALU.mult, ALU.add))
                                link(dve.tensor_tensor_scan(rec[:, c, 0:H], a4[:, c, 0:H], z4[:, c, 0:H], rec[:, c, T - 1:T],
                                                            ALU.mult, ALU.add), "scan_done")
                            else:
                                link(dve.tensor_tensor_scan(m4[:, c, ::-1], a4[:, c, ::-1], z4[:, c, ::-1], 0.0, ALU.mult, ALU.add))
                                tt(rec[:, c, :], rec[:, c, :], m4[:, c, :], ALU.add)
                                dve.wait_ge(S("gelu"), 4)
                                tt(catA[:, c, :], catA[:, c, :], rec[:, c, :], ALU.mult)
                    end_stage(dve, "lru0")
                    for n in range(8 * NT + 3):
                        if n < 8 * NT:
                            nk = T if n < 8 * NL else CTX
                            dve.wait_ge(S("scores0"), n + 1)
                            red(tmpc[:, 32:33], B[n % 2][:, 0:nk], ALU.max)
                            ts(nmx[:, n:n + 1], tmpc[:, 32:33], sink8[:, n % 8:n % 8 + 1], -SCALE, ALU.max, ALU.mult, "nmax0")
                        if 0 < n <= 8 * NT:
                            m = n - 1
                            nk = T if m < 8 * NL else CTX
                            dve.wait_ge(S("p_turned"), m + 1)
                            wait(dve, "pv_done", (m - 1) // 8)
                            wait(dve, "pv_step", m - 1 - (m - 1) // 8)
                            copy(pTA[:, m % 2, 0:nk], B[2 + m % 2][:, 0:nk], "pT_ready")
                        if n > 2 and n % 8 == 2:
                            qt = n // 8 - 1
                            tt(tmpc[:, 0:8], nmx[:, qt * 8:qt * 8 + 8], sinkb, ALU.add, "sink_in")
                            dve.wait_ge(S("sink_exp"), qt + 1)
                            tt(tmpc[:, 16:24], tmpc[:, 8:16], rsum[:, qt * 8:qt * 8 + 8], ALU.add)
                            link(dve.reciprocal(tmpc[:, 24:32], tmpc[:, 16:24]))
                            dve.wait_ge(S("pv_done"), qt + 1)
                            wait(dve, "att_turned", qt)
                            tt(attA.rearrange("p (h d) -> p h d", h=8), B[4 + qt % 2][:, :].rearrange("p (h d) -> p h d", h=8),
                               bc(tmpc[:, 24:32], 2, 64), ALU.mult, "att_ready")
                    dve.wait_ge(S("att_turned"), NT)
                    end_stage(dve, "attn0")
                else:
                    dve.wait_ge(S("pads_zeroed"), 3)
                    for n in range(1, len(proj1), 2):
                        dve.wait_ge(S("proj1"), n + 1)
                        dst, src = proj1_move(n)
                        copy(dst, src, "proj1_dve")
                    end_stage(dve, "proj1")
                    tt(dt_[:], dtraw, bc(dtb, 1, NT), ALU.add)
                    stt(dta[:], dt_[:], -1.0, dt_[:], ALU.mult, ALU.max)
                    for i in range(2):
                        tt(tmpc[:, 0:64], lamv[:, 128 * i:128 * i + 64], lamv[:, 128 * i + 64:128 * i + 128], ALU.mult)
                        red(lamc[:, i:i + 1], tmpc[:, 0:64], ALU.add, "dve_chain" if i == 0 else "dt_in")
                    for c in range(8):
                        conv(hT[:, c, :], xbc[:, c, :], V_DCONVW, 8, c, "conv1")
                    for m in range(8):
                        dve.wait_ge(S("swapped1"), m + 1)
                        rope(qC[:, m, :] if m < 4 else kC[:, m - 4, 0:H], B[m], ropeC, "dve_chain")
                    dve.wait_ge(S("dt_ln"), 1)
                    stt(dt_[:], dt_[:], 0.0, dta[:], ALU.max, ALU.add)
                    stt(dta[:], dt_[:], -1.0, bc(alog, 1, NT), ALU.mult, ALU.mult)
                    tt(lamc[:, 2:3], lamc[:, 1:2], lamc[:, 0:1], ALU.subtract)
                    ts(lamc[:, 2:3], lamc[:, 2:3], -LAM_INIT, None, ALU.add)
                    end_stage(dve, "conv1")

                    def weights(u):
                        dve.wait_ge(S("p1_ready"), 2 * u + 2)
                        link(dve.reciprocal(tmpc[:, 0:2], rsum[:, 2 * u:2 * u + 2]))
                        tt(tmpc[:, 2:3], tmpc[:, 1:2], lamc[:, 2:3], ALU.mult)
                        p0, p1 = pC[:, 2 * (u % 2), :], pC[:, 2 * (u % 2) + 1, :]
                        ts(p0, p0, tmpc[:, 0:1], None, ALU.mult)
                        stt(p0, p1, tmpc[:, 2:3], p0, ALU.mult, ALU.add, "w_ready1")

                    for u in range(4 * NL + 3):
                        if 0 < u <= 4 * NL:
                            weights(u - 1)
                        if u < 4 * NL:
                            for m in range(2):
                                n = 2 * u + m
                                dve.wait_ge(S("scores1"), n + 1)
                                red(tmpc[:, 4:5], B[n % 2][:, :], ALU.max)
                                ts(nmx[:, n:n + 1], tmpc[:, 4:5], -SCALE, None, ALU.mult, name="nmax1")
                        if u > 4 and u % 4 == 2:
                            qt = u // 4 - 1
                            dve.wait_ge(S("pv1_done"), 4 * qt + 4)
                            wait(dve, "o_turned", qt)
                            copy(oC, B[4 + qt][:, :])
                            tt(sqC, oC, oC, ALU.mult)
                            red(ss, sqC.rearrange("p (h e) -> p h e", h=4), ALU.add)
                            mean_square(f"d{qt}", 4, P)
                            o3 = oC.rearrange("p (h e) -> p h e", h=4)
                            tt(o3, o3, bc(rstd, 2, P), ALU.mult)
                            tt(o3, o3, bc(subg[:], 1, 4), ALU.mult, "o_ready")
                    dve.wait_ge(S("o_turned"), NL)
                    for qt in range(NL):
                        copy(catC[:, 0:4, qt * P:qt * P + P], B[6 + qt][:, :].rearrange("p (c q) -> p c q", c=4))
                    end_stage(dve, "attn1")
                    flat = "p t h -> p (t h)"
                    dve.wait_ge(S("acum_mm"), 1)
                    copy(acum[:].rearrange(flat), B[0][:, 0:NT * 16])
                    ts(nac_, acum[:].rearrange(flat), -1.0, None, ALU.mult)
                    copy(etot[:].rearrange(flat), B[1][:, 0:NT * 16])
                    tt(tend[:], etot[:], acum[:], ALU.subtract, "acum_ready")
                    dve.wait_ge(S("cb_mm"), 1)
                    copy(cbT.rearrange("p a b -> p (a b)"), B[2][:, :], "ssd_moved")
                    for t in range(NT):
                        dve.wait_ge(S("ssd_turned"), t + 1)
                        copy(xtok[:, t, :], B[3 + t][:, :], "ssd_moved")
                    for i in range(2):
                        dve.wait_ge(S("ssd_turned"), NT + i + 1)
                        copy(btok[:, 2 * i:2 * i + 2, :].rearrange("p a b -> p (a b)"), (B[7] if i == 0 else B[0])[:, :], "ssd_moved")
                    dve.wait_ge(S("acum_exp"), 1)
                    tt(tend[:], tend[:], dt_[:], ALU.mult, "tend_ready")
                    by_head = "p (h d) -> p h d"
                    for c in range(NL):
                        tt(yacc[:, c, :].rearrange(by_head, h=8), xtok[:, c, :].rearrange(by_head, h=8), bc(dskip, 2, 64), ALU.mult)

                    for n, (d, t, g) in enumerate(SEGS):
                        k = n % 4
                        c = chunks(d)[k]
                        hd = slice(8 * d, 8 * d + 8)
                        dve.wait_ge(S("seg_mm"), n + 1)
                        wait(dve, "y_mm", n - 1)
                        for r in range(4):
                            col = t * 16 + 8 * d + 4 * g + r
                            link(dve.scalar_tensor_tensor(out=seg[:, n % 2, r * P:r * P + P], in0=B[3 + n % 2][:, r * P:r * P + P],
                                                          scalar=nac_[:, col:col + 1], in1=C["mask_lo" if d == 0 else "mask_hi"],
                                                          op0=ALU.add, op1=ALU.add),
                                 "seg_ready" if r == 3 else "dve_chain", wait=(r == 3))
                        if k >= 2:
                            dve.wait_ge(S("inter_mm"), 2 * d + k - 1)
                            tt(ytmp.rearrange(by_head, h=8), B[5][:, :].rearrange(by_head, h=8), bc(eac[:, c, hd], 2, 64), ALU.mult)
                            tt(yacc[:, c, :], yacc[:, c, :], ytmp, ALU.add)
                        if k < 3:
                            dve.wait_ge(S("state_mm"), 3 * d + k + 1)
                            if k == 0:
                                copy(Hst, B[2][:, :], "H_ready")
                            else:
                                tt(Hst.rearrange(by_head, h=8), Hst.rearrange(by_head, h=8), bc(etot[:, c, hd], 2, 64), ALU.mult)
                                tt(Hst, Hst, B[2][:, :], ALU.add, "H_ready")
                        dve.wait_ge(S("seg_exp"), n + 1)
                        s3 = seg[:, n % 2, :].rearrange("p (r q) -> p r q", r=4)
                        tt(s3, s3, bc(cbT[:, 2 * t + g, :], 1, 4), ALU.mult, "w_ready")
                    dve.wait_ge(S("y_mm"), len(SEGS))
                    for c in range(NL):
                        y = yacc[:, c, :]
                        tt(y, y, B[6 + c][:, :], ALU.add)
                        tt(y, y, zC[:, c, :], ALU.mult)
                        tt(ytmp, y, y, ALU.mult)
                        red(ss[:, 0:2], ytmp.rearrange("p (g e) -> p g e", g=2), ALU.add)
                        mean_square(f"s{c}", 2, 256)
                        y2 = y.rearrange("p (g e) -> p g e", g=2)
                        tt(y2, y2, bc(rstd[:, 0:2], 2, 256), ALU.mult)
                        dve.wait_ge(S("ld_normg"), 16)
                        tt(y, y, normg[:], ALU.mult, "ssd_y")
                    for c in range(NL):
                        dve.wait_ge(S("ssd_y_turned"), c + 1)
                        copy(catC[:, 4:8, c * P:c * P + P], B[3 + c][:, :].rearrange("p (m q) -> p m q", m=4))
                    end_stage(dve, "ssd1")
                outtmp = hT[:, 0, :]
                for h in range(2):
                    for t in range(nt):
                        n = h * nt + t
                        dve.wait_ge(S("out"), n + 1 + before("out", l))
                        tt(outtmp, B[n][:, :], G[:, 0, t // 2, h * 512:h * 512 + 512], ALU.mult)
                        xs = X[:, t, h * 512:h * 512 + 512]
                        tt(xs, xs, outtmp, ALU.add)
                end_stage(dve, f"out{l}")
                norm(2 * l + 1, 1)
                for t in range(nt):
                    dve.wait_ge(S("row_turned"), 2 * t + 2 + before("row_turned", l))
                    copy(row_half(t, 1), B[2 * t + 1][:, :].rearrange("q (k p) -> q k p", k=4), "hrow_dve")
                end_stage(dve, f"norm2{l}")

                dve.wait_ge(S("ld_router"), 32 + before("ld_router", l))
                dve.wait_ge(S("scores"), 1 + before("scores", l))
                tk = nt * TOPK
                by_choice = "p (t k e) -> p t k e"
                sel_, oh_, tmp_ = selv[:, 0:nt, :], oh[:, 0:nt, :], ohtmp[:, 0:tk * NE]
                oh4 = oh_.rearrange("p t (k e) -> p t k e", k=TOPK)
                tmp4 = tmp_.rearrange(by_choice, t=nt, k=TOPK)
                per_choice = tmp_.rearrange("p (a e) -> p a e", e=NE)

                def flat(v):
                    return v[:, 0:nt, :].rearrange("p t k -> p (t k)")

                tt(sel_, scores[:, 0:nt, :], bc(router_b[:], 1, nt), ALU.add)
                for t in range(nt):
                    for g in range(NG):
                        link(dve.max(srt[:, t * NG + g, :], selv[:, t, 8 * g:8 * g + 8]), wait=(t == nt - 1 and g == NG - 1))
                tt(flat(gsc), srt[:, 0:nt * NG, 0], srt[:, 0:nt * NG, 1], ALU.add)
                for t in range(nt):
                    link(dve.max(top8[:, t, :], gsc[:, t, :]), wait=(t == nt - 1))
                for t in range(nt):
                    link(dve.max_index(i8[:, t, :], top8[:, t, :], gsc[:, t, :]), wait=(t == nt - 1))
                copy(flat(gidx), flat(i8))
                goh_ = goh[:, 0:nt]
                tt(goh_, bc(bc(C["iota"][:, 0:NG], 1, TOPG), 1, nt), bc(gidx[:, 0:nt, 0:TOPG], 3, NG), ALU.is_equal)
                red(gmask[:, 0:nt, :], goh_.rearrange("p t a g -> p t g a"), ALU.max)
                s3 = sel_.rearrange("p t (g e) -> p (t g) e", g=NG)
                tt(s3, s3, bc(flat(gmask), 2, 8), ALU.mult)
                ts(flat(gmask), flat(gmask), 1.0, -NEG, ALU.subtract, ALU.mult)
                tt(s3, s3, bc(flat(gmask), 2, 8), ALU.add)
                for t in range(nt):
                    link(dve.max(top8[:, t, :], selv[:, t, :]), wait=(t == nt - 1))
                for t in range(nt):
                    link(dve.max_index(i8[:, t, :], top8[:, t, :], selv[:, t, :]), wait=(t == nt - 1))
                copy(flat(idx8), flat(i8))
                oh3 = oh_.rearrange("p t (k e) -> p (t k) e", k=TOPK)
                tt(oh3, bc(C["iota"][:, 0:NE], 1, tk), bc(flat(idx8), 2, NE), ALU.is_equal)
                red(Msel[:, 0:nt, :], oh_.rearrange("p t (k e) -> p t e k", k=TOPK), ALU.add, "Msel")
                tt(tmp4, oh4, bc(scores[:, 0:nt, :], 2, TOPK), ALU.mult)
                red(flat(gates), per_choice, ALU.add)
                red(top8[:, 0:nt, 0], gates[:, 0:nt, :], ALU.add)
                link(dve.reciprocal(top8[:, 0:nt, 1], top8[:, 0:nt, 0]))
                ts(top8[:, 0:nt, 1], top8[:, 0:nt, 1], SCALED, None, ALU.mult)
                tt(gates[:, 0:nt, :], gates[:, 0:nt, :], bc(top8[:, 0:nt, 1], 2, TOPK), ALU.mult)
                dve.wait_ge(S("ranks"), 1 + before("ranks", l))
                copy(rank[:, 0:nt, :].rearrange("p t e -> p (t e)"), B[1][:, 0:nt * NE])
                copy(cnt, B[2][:, 0:NE])
                ts(t64a, cnt, 128.0, None, ALU.is_gt)
                stt(t64a, cnt, 256.0, t64a, ALU.is_gt, ALU.add)
                stt(t64a, cnt, 384.0, t64a, ALU.is_gt, ALU.add)
                link(dve.tensor_tensor_scan(ends, C["ones"][:, 0:NE], t64a, 0.0, ALU.mult, ALU.add))
                tt(v1, ends, t64a, ALU.subtract)
                tt(v1, v1, C["iota"][:, 0:NE], ALU.subtract)
                ts(v1, v1, float(NE - 1), None, ALU.add)
                copy(more_i[:], ends[:, NE - 1:NE])
                ts(t64b, ends, C["pcol"], None, ALU.is_le)
                red(s1[:, 1:2], t64b, ALU.add)
                ts(s1[:, 0:1], s1[:, 1:2], float(NE - 1), None, ALU.min, name="more_col")
                for dst, per_expert in ((r8, rank[:, 0:nt, :]), (q8, bc(v1, 1, nt))):
                    tt(tmp4, oh4, bc(per_expert, 2, TOPK), ALU.mult)
                    red(flat(dst), per_choice, ALU.add)
                ts(flat(b8), flat(r8), 128.0, None, ALU.is_ge)
                copy(flat(c8), flat(b8))
                stt(flat(b8), flat(r8), 256.0, flat(b8), ALU.is_ge, ALU.add)
                stt(flat(b8), flat(r8), 384.0, flat(b8), ALU.is_ge, ALU.add)
                tt(flat(q8), flat(q8), flat(c8), ALU.mult)
                tt(flat(q8), flat(q8), flat(b8), ALU.add)
                tt(flat(q8), flat(q8), flat(idx8), ALU.add)
                stt(flat(r8), flat(b8), -128.0, flat(r8), ALU.mult, ALU.add)
                dve.wait_ge(S("more_row"), 1 + before("more_row", l))
                copy(moree_i[:], B[0][0:1, 0:P])
                for m in range(2):
                    dve.wait_ge(S("shared_silu"), m + 1 + before("shared_silu", l))
                    dve.wait_ge(S("shared_gu"), 2 * m + 2 + before("shared_gu", l))
                    tt(actS[:, m, 0:nt * P], sS[:, m, 0:nt * P], B[5 + 2 * m][:, 0:nt * P], ALU.mult, "act_shared")
                for t in range(nt):
                    wait(dve, "table", t, before("table", l))
                    tt(lo_oh, bc(C["iota"], 1, TOPK), bc(r8[:, t, :], 2, P), ALU.is_equal)
                    tt(hi_oh, bc(C["iota"][:, 0:NCOL], 1, TOPK), bc(q8[:, t, :], 2, NCOL), ALU.is_equal, "onehot")
                    for h in range(2):
                        n = 2 * t + h
                        dve.wait_ge(S("shared_y"), n + 1 + before("shared_y", l))
                        tt(shtmp, B[4 + n % 4][:, :], G[:, 1, t // 2, h * 512:h * 512 + 512], ALU.mult, "shared_out")
                        xs = X[:, t, h * 512:h * 512 + 512]
                        tt(xs, xs, shtmp, ALU.add)
                dve.wait_ge(S("table"), nt + before("table", l))
                copy(tabf, B[3][:, 0:NCOL])
                ts(tab2, tabf, 0.5, BIG, ALU.is_lt, ALU.mult)
                stt(tabf, tabf, -1.0, tab2, ALU.add, ALU.add)
                copy(rows_i[:], tabf)
                ts(toks_i[:], rows_i[:], 3, None, ALU.logical_shift_right)
                end_stage(dve, f"route{l}")

                def x_evac(i, n):
                    e, half, _, _, _ = nth(l, i, n)
                    dve.wait_ge(S("x_turned"), e * 2 + 2)
                    dve.tensor_copy(xgT[:, half, 512:1024], B[1][:, :]).then_inc(S("xgT_dve"), 1)

                def y_evac(i, n):
                    e, _, _, slot, turns = nth(l, i, n)
                    dve.wait_ge(S("y_done"), e * 2 + 2)
                    wait(dve, f"y_stored{slot}", turns * 16)
                    dve.tensor_copy(ysb[:, slot, 512:1024], B[7][:, :]).then_inc(S("y_dve"), 1)

                def four(i):
                    for n in range(4):
                        e, half, _, _, _ = nth(l, i, n)
                        dve.wait_ge(S("sg_ready"), e + 1)
                        dve.tensor_tensor(act_[:, half, :], sg[:, half, :], B[2 + half][:, DE:2 * DE], ALU.mult).then_inc(S("act_ready"), 1)
                        if is_expert(i, n + 1):
                            x_evac(i, n + 1)
                        if is_expert(i, n - 1):
                            y_evac(i, n - 1)
                        dve.wait_ge(S("act_turned"), e + 1)
                        dve.tensor_copy(actT[:, half, :], B[4 + half][:, 0:2 * P]).then_inc(S("actT_ready"), 1)

                x_evac(0, 0)
                over_fours(dve, four)
                y_evac(NE // 4 - 1, 3)
                end_stage(dve, f"experts{l}")
                more = dve.value_load(more_i[0:1, 0:1], min_val=0, max_val=OVB)
                with dve.If(more):
                    with dve.Fori(0, OVB) as i:
                        step = S(f"more_step{l}")
                        dve.wait_ge(step, i * MORE_STEPS + 3)
                        for b in range(2):
                            dve.tensor_copy(xgT[:, 0, b * 512:b * 512 + 512], B[b][:, :]).then_inc(step, 1)
                        dve.wait_ge(step, i * MORE_STEPS + 7)
                        dve.tensor_tensor(act_[:, 0, :], sg[:, 0, :], B[2][:, DE:2 * DE], ALU.mult).then_inc(step, 1)
                        dve.wait_ge(step, i * MORE_STEPS + 9)
                        dve.tensor_copy(actT[:, 0, :], B[4][:, 0:2 * P]).then_inc(step, 1)
                        dve.wait_ge(step, i * MORE_STEPS + 11)
                        for b in range(2):
                            dve.tensor_copy(ysb[:, 0, b * 512:b * 512 + 512], B[6 + b][:, :]).then_inc(step, 1)
                end_stage(dve, f"more{l}")
                combine(dve, link, l, 0, SPLIT)
                end_stage(dve, f"combine{l}")
            dve.wait_ge(S("ss"), NL + before("ss", 4))
            mean_square(4, NL, D)
            dve.wait_ge(S("ld_gfin"), 16)
            for t in range(NL):
                stt(xn[:, t, :], X[:, t, :], rstd[:, t:t + 1], G[:, 0, 0, :], ALU.mult, ALU.mult, "out_ready")
            dve.drain()


_INS = ["x", "c", "ctx", "c_ctx", "w_mod", "b_mod", "g_mix", "g_ffn", "g_final", "ab_w_in", "ab_w_out", "ab_conv_w",
        "ab_conv_b", "ab_w_r", "ab_b_r", "ab_w_i", "ab_b_i", "ab_lam", "ab_sink", "cd_w_in", "cd_w_out", "cd_lam",
        "cd_subln_g", "cd_conv_w", "cd_conv_b", "cd_dt_bias", "cd_a_log", "cd_d_skip", "cd_norm_g", "w_router",
        "b_router", "w_e_gate", "w_e_up", "w_e_down", "ws_gate", "ws_up", "ws_down"]


def kernel(**inputs):
    import concourse.bacc as bacc
    from concourse.bass_utils import run_bass_kernel_spmd

    nc = bacc.Bacc("TRN2", target_bir_lowering=False, num_devices=1)
    arrays, aps = {}, {}
    for name in _INS:
        arrays[f"in_{name}"] = np.ascontiguousarray(inputs[name])
    arrays["in_con"] = const_table()
    for name, v in arrays.items():
        aps[name[3:]] = nc.dram_tensor(name, v.shape, mybir.dt.from_np(v.dtype), kind="ExternalInput").ap()
    out = nc.dram_tensor("out_0", (1, SEQ, D), F32, kind="ExternalOutput").ap()
    build(nc, aps, out)
    r = run_bass_kernel_spmd(nc, [arrays], core_ids=[0])
    return r.results[0]["out_0"]
```
